# Optimizing a Trainium2 kernel written in Bass

```python
import jax, jax.numpy as jnp
from jax import lax
import numpy as np

D_MODEL = 1024
BATCH = 1
SEQ = 256
DEPTH = 1
DEC_BATCH = 8
DEC_SEQ = 16
PAST_LEN = 128

CHUNK = 64
D_MIX = D_MODEL
D_RET = D_MIX // 2
D_CONV = D_MIX - D_RET
N_RET_HEADS = 4
HEAD_DIM = D_RET // N_RET_HEADS
CONV_W = 3
N_EXPERTS = 32
TOP_K = 4
D_FF = D_MODEL
SWIGLU_LIMIT = 7.0
SWIGLU_ALPHA = 1.702
ROPE_BASE = 10000.0
LN_EPS = 1e-5
GN_EPS = 1e-5
MOE_BLOCK = 128
DEEPNORM_ALPHA = (2.0 * DEPTH) ** 0.25
DEEPNORM_BETA = (8.0 * DEPTH) ** -0.25
D_IN_PROJ = 4 * D_RET + 3 * D_CONV

kernel_name = "hybrid_retention_shortconv_moe_step"

def layer_norm(x, g, b):
    xf = x.astype(jnp.float32)
    mu = jnp.mean(xf, axis=-1, keepdims=True)
    var = jnp.mean(jnp.square(xf - mu), axis=-1, keepdims=True)
    y = (xf - mu) * lax.rsqrt(var + LN_EPS) * g.astype(jnp.float32) + b.astype(jnp.float32)
    return y.astype(x.dtype)

def rotary(x, pos):
    half = HEAD_DIM // 2
    inv_freq = ROPE_BASE ** (-jnp.arange(0, HEAD_DIM, 2, dtype=jnp.float32) / HEAD_DIM)
    ang = pos.astype(jnp.float32)[:, None] * inv_freq[None, :]
    cos = jnp.cos(ang)[None, :, None, :]
    sin = jnp.sin(ang)[None, :, None, :]
    x1, x2 = x[..., :half], x[..., half:]
    return jnp.concatenate([x1 * cos - x2 * sin, x1 * sin + x2 * cos], axis=-1)

def log_gammas():
    return jnp.log1p(-jnp.power(2.0, -5.0 - jnp.arange(N_RET_HEADS, dtype=jnp.float32)))

def retention_block(q, k, v, s):
    L = q.shape[1]
    lg = log_gammas()
    i = jnp.arange(L, dtype=jnp.float32)
    diff = i[:, None] - i[None, :]
    decay = jnp.where(diff[None] >= 0, jnp.exp(lg[:, None, None] * jnp.maximum(diff, 0.0)[None]), 0.0)
    scores = jnp.einsum('bihd,bjhd->bhij', q, k) * decay[None]
    intra = jnp.einsum('bhij,bjhe->bihe', scores, v)
    q_decay = jnp.exp(lg[None, :] * (i + 1.0)[:, None])
    cross = jnp.einsum('bihd,bhde->bihe', q, s) * q_decay[None, :, :, None]
    k_decay = jnp.exp(lg[None, :] * (L - 1.0 - i)[:, None])
    s_new = jnp.exp(lg * L)[None, :, None, None] * s + jnp.einsum('bjhd,bjhe->bhde', k * k_decay[None, :, :, None], v)
    return intra + cross, s_new

def retention_prompt(q, k, v, s0):
    B, S = q.shape[0], q.shape[1]
    nc = S // CHUNK
    to_chunks = lambda t: jnp.moveaxis(t.reshape(B, nc, CHUNK, N_RET_HEADS, HEAD_DIM), 1, 0)

    def step(s, qkv):
        o, s = retention_block(qkv[0], qkv[1], qkv[2], s)
        return s, o

    s_final, o = lax.scan(step, s0, (to_chunks(q), to_chunks(k), to_chunks(v)))
    o = jnp.moveaxis(o, 0, 1).reshape(B, S, N_RET_HEADS, HEAD_DIM)
    return o, s_final

def token_mixer(x, s_ret, s_conv, pos, chunked, w_in, beta_ret, beta_conv, conv_w, conv_b, w_out):
    B, L, _ = x.shape
    proj = jnp.einsum('bld,de->ble', x, w_in)
    q, k, v, g, bg, cg, hc = jnp.split(
        proj, [D_RET, 2 * D_RET, 3 * D_RET, 4 * D_RET, 4 * D_RET + D_CONV, 4 * D_RET + 2 * D_CONV], axis=-1)
    q = rotary(q.astype(jnp.float32).reshape(B, L, N_RET_HEADS, HEAD_DIM), pos)
    k = rotary(k.astype(jnp.float32).reshape(B, L, N_RET_HEADS, HEAD_DIM), pos) * (HEAD_DIM ** -0.5)
    v = v.astype(jnp.float32).reshape(B, L, N_RET_HEADS, HEAD_DIM)
    s0 = s_ret.astype(jnp.float32)
    if chunked:
        o, s_ret_new = retention_prompt(q, k, v, s0)
    else:
        o, s_ret_new = retention_block(q, k, v, s0)
    mu = jnp.mean(o, axis=-1, keepdims=True)
    var = jnp.mean(jnp.square(o - mu), axis=-1, keepdims=True)
    o = ((o - mu) * lax.rsqrt(var + GN_EPS)).reshape(B, L, D_RET)
    ret_out = (o * jax.nn.silu(g.astype(jnp.float32)) * beta_ret.astype(jnp.float32)).astype(x.dtype)
    u = cg * hc
    upad = jnp.concatenate([s_conv.astype(u.dtype), u], axis=1)
    z = conv_b
    for t in range(CONV_W):
        z = z + conv_w[t] * upad[:, t:t + L]
    conv_out = bg * z * beta_conv
    s_conv_new = upad[:, -(CONV_W - 1):]
    y = jnp.einsum('ble,ed->bld', jnp.concatenate([ret_out, conv_out], axis=-1), w_out)
    return y, s_ret_new.astype(s_ret.dtype), s_conv_new.astype(s_conv.dtype)

def moe(x2, w_router, b_router, w_gu, b_gu, w_down, b_down):
    T, D = x2.shape
    logits = jnp.einsum('td,de->te', x2.astype(jnp.float32), w_router.astype(jnp.float32)) + b_router.astype(jnp.float32)
    top_vals, top_idx = lax.top_k(logits, TOP_K)
    gates = jax.nn.softmax(top_vals, axis=-1)
    A = T * TOP_K
    flat_e = top_idx.reshape(A)
    flat_tok = jnp.repeat(jnp.arange(T, dtype=jnp.int32), TOP_K)
    flat_g = gates.reshape(A)
    order = jnp.argsort(flat_e)
    sorted_e = flat_e[order]
    counts = jnp.bincount(flat_e, length=N_EXPERTS)
    padded = ((counts + MOE_BLOCK - 1) // MOE_BLOCK) * MOE_BLOCK
    start = jnp.cumsum(counts) - counts
    pstart = jnp.cumsum(padded) - padded
    dest = pstart[sorted_e] + (jnp.arange(A, dtype=jnp.int32) - start[sorted_e])
    n_blocks = -(-A // MOE_BLOCK) + N_EXPERTS
    n_slots = n_blocks * MOE_BLOCK
    slot_tok = jnp.full((n_slots,), T, dtype=jnp.int32).at[dest].set(flat_tok[order])
    slot_gate = jnp.zeros((n_slots,), jnp.float32).at[dest].set(flat_g[order])
    block_start = jnp.arange(n_blocks, dtype=jnp.int32) * MOE_BLOCK
    block_e = jnp.minimum(jnp.searchsorted(jnp.cumsum(padded), block_start, side='right'), N_EXPERTS - 1)
    x_pad = jnp.concatenate([x2, jnp.zeros((1, D), x2.dtype)], axis=0)

    def expert_block(args):
        tok, e = args
        xb = x_pad[tok]
        gu = xb @ w_gu[e] + b_gu[e]
        gate, up = gu[:, :D_FF], gu[:, D_FF:]
        gate = jnp.minimum(gate, SWIGLU_LIMIT)
        up = jnp.clip(up, -SWIGLU_LIMIT, SWIGLU_LIMIT)
        h = (up + 1.0) * gate * jax.nn.sigmoid(SWIGLU_ALPHA * gate)
        return h @ w_down[e] + b_down[e]

    out = lax.map(expert_block, (slot_tok.reshape(n_blocks, MOE_BLOCK), block_e))
    out = out.reshape(n_slots, D) * slot_gate[:, None].astype(out.dtype)
    return jnp.zeros((T + 1, D), out.dtype).at[slot_tok].add(out)[:T]

def encoder_layer(x, s_ret, s_conv, pos, chunked, w_in, beta_ret, beta_conv, conv_w, conv_b, w_out,
                  ln1_g, ln1_b, w_router, b_router, w_gu, b_gu, w_down, b_down, ln2_g, ln2_b):
    B, L, D = x.shape
    m, s_ret_new, s_conv_new = token_mixer(x, s_ret, s_conv, pos, chunked, w_in, beta_ret, beta_conv,
                                           conv_w, conv_b, w_out)
    h = layer_norm(DEEPNORM_ALPHA * x + m, ln1_g, ln1_b)
    f = moe(h.reshape(B * L, D), w_router, b_router, w_gu, b_gu, w_down, b_down).reshape(B, L, D)
    y = layer_norm(DEEPNORM_ALPHA * h + f, ln2_g, ln2_b)
    return y, s_ret_new, s_conv_new

def setup_inputs(seed: int = 0) -> dict:
    key = jax.random.key(seed)
    ks = jax.random.split(key, 24)
    f32 = jnp.float32
    nrm = lambda k, shape, scale: jax.random.normal(k, shape, f32) * scale
    return {
        "x_prompt": nrm(ks[0], (BATCH, SEQ, D_MODEL), 1.0),
        "x_sample": nrm(ks[1], (DEC_BATCH, DEC_SEQ, D_MODEL), 1.0),
        "state_retention": nrm(ks[2], (DEPTH, DEC_BATCH, N_RET_HEADS, HEAD_DIM, HEAD_DIM), 0.3),
        "state_conv": nrm(ks[3], (DEPTH, DEC_BATCH, CONV_W - 1, D_CONV), 1.0),
        "w_in": nrm(ks[4], (DEPTH, D_MODEL, D_IN_PROJ), D_MODEL ** -0.5),
        "beta_ret": 1.0 + nrm(ks[5], (DEPTH, D_RET), 0.02),
        "beta_conv": 1.0 + nrm(ks[6], (DEPTH, D_CONV), 0.02),
        "conv_w": nrm(ks[7], (DEPTH, CONV_W, D_CONV), CONV_W ** -0.5),
        "conv_b": nrm(ks[8], (DEPTH, D_CONV), 0.02),
        "w_out": nrm(ks[9], (DEPTH, D_MIX, D_MODEL), D_MIX ** -0.5 * DEEPNORM_BETA),
        "ln1_g": 1.0 + nrm(ks[10], (DEPTH, D_MODEL), 0.02),
        "ln1_b": nrm(ks[11], (DEPTH, D_MODEL), 0.02),
        "w_router": nrm(ks[12], (DEPTH, D_MODEL, N_EXPERTS), D_MODEL ** -0.5),
        "b_router": nrm(ks[13], (DEPTH, N_EXPERTS), 0.01),
        "w_gu": nrm(ks[14], (DEPTH, N_EXPERTS, D_MODEL, 2 * D_FF), D_MODEL ** -0.5),
        "b_gu": nrm(ks[15], (DEPTH, N_EXPERTS, 2 * D_FF), 0.01),
        "w_down": nrm(ks[16], (DEPTH, N_EXPERTS, D_FF, D_MODEL), D_FF ** -0.5 * DEEPNORM_BETA),
        "b_down": nrm(ks[17], (DEPTH, N_EXPERTS, D_MODEL), 0.01),
        "ln2_g": 1.0 + nrm(ks[18], (DEPTH, D_MODEL), 0.02),
        "ln2_b": nrm(ks[19], (DEPTH, D_MODEL), 0.02),
    }

def reference(x_prompt, x_sample, state_retention, state_conv, w_in, beta_ret, beta_conv, conv_w, conv_b,
              w_out, ln1_g, ln1_b, w_router, b_router, w_gu, b_gu, w_down, b_down, ln2_g, ln2_b):
    B, S, _ = x_prompt.shape
    Bd, Ld, _ = x_sample.shape
    pos_prompt = jnp.arange(S, dtype=jnp.int32)
    pos_sample = PAST_LEN + jnp.arange(Ld, dtype=jnp.int32)
    hp, hs = x_prompt, x_sample
    ret_p, conv_p, ret_s, conv_s = [], [], [], []
    for l in range(DEPTH):
        w = (w_in[l], beta_ret[l], beta_conv[l], conv_w[l], conv_b[l], w_out[l], ln1_g[l], ln1_b[l],
             w_router[l], b_router[l], w_gu[l], b_gu[l], w_down[l], b_down[l], ln2_g[l], ln2_b[l])
        s_ret0 = jnp.zeros((B, N_RET_HEADS, HEAD_DIM, HEAD_DIM), x_prompt.dtype)
        s_conv0 = jnp.zeros((B, CONV_W - 1, D_CONV), x_prompt.dtype)
        hp, sr, sc = encoder_layer(hp, s_ret0, s_conv0, pos_prompt, True, *w)
        ret_p.append(sr)
        conv_p.append(sc)
        hs, sr, sc = encoder_layer(hs, state_retention[l], state_conv[l], pos_sample, False, *w)
        ret_s.append(sr)
        conv_s.append(sc)
    new_ret_prompt = jnp.stack(ret_p, axis=0)
    new_conv_prompt = jnp.stack(conv_p, axis=0)
    new_ret_sample = jnp.stack(ret_s, axis=0)
    new_conv_sample = jnp.stack(conv_s, axis=0)
    return (hp, hs, new_ret_prompt, new_conv_prompt, new_ret_sample, new_conv_sample)


_drawn_inputs = setup_inputs


def setup_inputs(seed=0):
    import zlib

    import numpy as np

    out = dict(_drawn_inputs(seed))
    spreads = {}
    factors = {'beta_ret': 4.618,
     'beta_conv': 3.648,
     'conv_b': 3.727,
     'b_router': 3.477,
     'b_gu': 8.0,
     'b_down': 8.0,
     'ln2_g': 2.895,
     'ln2_b': 2.841}
    for name, (base, spread) in spreads.items():
        noise = np.random.default_rng([zlib.crc32(name.encode()), seed]).standard_normal(out[name].shape)
        drawn = base * np.exp(spread * noise) if base else spread * noise
        out[name] = __import__('jax').numpy.asarray(drawn.astype(out[name].dtype))
    for name, factor in factors.items():
        out[name] = (out[name] * factor).astype(out[name].dtype)
    return out
```

```python
import math
from contextlib import ExitStack

import numpy as np

import concourse.bass as bass
from concourse import mybir

F32 = mybir.dt.float32
BF16 = mybir.dt.bfloat16
I32 = mybir.dt.int32
U32 = mybir.dt.uint32
ALU = mybir.AluOpType
ACT = mybir.ActivationFunctionType
AXX = mybir.AxisListType.X

D = 1024
KC = D // 128
SEQ, STREAMS, STEP = 256, 8, 16
PAST = 128
T = SEQ + STREAMS * STEP
NT = T // 128
PT = SEQ // 128
DR = 512
H, HD = 4, 128
DC = 512
CT = DC // 128
TAPS = 3
E = 32
TOPK = 4
FF = 1024
LIMIT = 7.0
SIG = 1.702
EPS = 1e-5
ALPHA = 2.0 ** 0.25
SLOTS = 64
MORE = T // SLOTS - 1
OV = (T * TOPK) // (SLOTS + 1) + 1
OV += OV % 2
NB = E + OV + 2
RING = 12
PW = 2048
IN_COLS = [0, DR, 2 * DR, 3 * DR, 4 * DR + DC, 4 * DR + 2 * DC, 4 * DR]
IN_PIECES = 2 * len(IN_COLS)
OUT_PIECES = 4
MIX_PIECES = IN_PIECES + OUT_PIECES
GU_PIECES, DN_PIECES = 8, 4
PAIR_PIECES = 2 * (GU_PIECES + DN_PIECES)
CW = SEQ + 2 + STREAMS * (STEP + 2)
ZW = CW - 2

C_ID, C_IOTA, C_TRI, C_BM, C_TRIR, C_EC, C_SEL, C_OV, C_THR, C_HALF = np.cumsum(
    [0, 128, 64, 128, 8, 96, 1, 32, OV, MORE]).tolist()
C_W = C_HALF + OV // 2
M_COS, M_SIN, M_QD, M_KD = np.cumsum([0, NT * 64, NT * 64, H * STEP]).tolist()
M_W = M_KD + NT * H


def constants():
    c = np.zeros((128, C_W), np.float32)
    p = np.arange(128)
    c[:, C_ID:C_ID + 128] = np.eye(128)
    c[:, C_IOTA:C_IOTA + 64] = np.arange(64)
    c[:, C_TRI:C_TRI + 128] = p[:, None] < p[None, :]
    c[:, C_BM:C_BM + 8] = (p[:, None] // STEP) == np.arange(8)
    c[:, C_TRIR:C_TRIR + 96] = p[:, None] < (np.arange(96) % E)[None, :]
    c[:, C_EC] = p
    c[:, C_SEL:C_SEL + E] = (p[:, None] % E) == np.arange(E)
    c[:, C_OV:C_OV + OV] = np.arange(OV)
    c[:, C_THR:C_THR + MORE] = SLOTS * np.arange(1, MORE + 1)
    c[:, C_HALF:] = 2 * np.arange(OV // 2)
    gamma = 1.0 - 2.0 ** (-5.0 - np.arange(H))
    lg = np.log(gamma)
    m = np.zeros((128, M_W), np.float32)
    pos = np.stack([p, 128 + p, PAST + p % STEP], 1).astype(np.float32)
    inv = (np.float32(10000.0) ** (-np.arange(0, HD, 2, dtype=np.float32) / np.float32(HD))).astype(np.float32)
    ang = (pos[:, :, None] * inv).astype(np.float32)
    m[:, M_COS:M_SIN] = np.cos(ang).reshape(128, -1)
    m[:, M_SIN:M_QD] = np.sin(ang).reshape(128, -1)
    m[:, M_QD:M_KD] = np.exp(lg[:, None] * (np.arange(STEP) + 1.0)).reshape(1, -1)
    scale = HD ** -0.5
    left = np.stack([255 - p, 127 - p, STEP - 1 - p % STEP], 1)
    m[:, M_KD:] = (np.exp(lg * left[:, :, None]) * scale).reshape(128, -1)
    d = np.zeros((128, H, 4, 128))
    diff = p[None, :] - p[:, None]
    same = (p[None, :] // STEP) == (p[:, None] // STEP)
    for h in range(H):
        near = np.where(diff >= 0, np.exp(lg[h] * np.maximum(diff, 0)), 0.0)
        d[:, h, 0] = near
        d[:, h, 1] = np.exp(lg[h] * (diff + 128))
        d[:, h, 2] = near
        d[:, h, 3] = near * same
    return c, m, (d * scale).reshape(128, H * 512).astype(np.float32), np.exp(lg * STEP)


def build(nc, x_tok, x_t, s_ret, conv_in, w_in, w_out, chan, beta_ret, ln1, ln2, w_router, b_router,
          w_gu, b_gu, w_down, b_down, consts, mconsts, dmask, y_out, retp_out, rets_out, conv_out):
    carry = constants()[3]
    es = ExitStack()
    with es:
        def sb(name, shape, dt=F32, ctx=es):
            return ctx.enter_context(nc.sbuf_tensor(name, shape, dt))

        def sem(name):
            return es.enter_context(nc.semaphore(name))

        ring = sb("ring", [128, RING, PW])
        xy = sb("xy", [128, NT, D])
        hid = sb("hid", [128, NT, D])
        lnp = sb("lnp", [128, 2, D])
        cst = sb("cst", [128, C_W])
        biasp = sb("biasp", [3 * E, 3 * D], BF16)
        sel_all = sb("sel_all", [3 * E, NB])
        rank_all = sb("rank_all", [128, NT, NB])
        gate_all = sb("gate_all", [128, NT, NB])
        etab = sb("etab", [1, OV], I32)
        ntab = sb("ntab", [1, 2], I32)
        stat = sb("stat", [128, NT, 2, 6])
        mv = sb("mv", [128, NT, 2])
        veps = sb("veps", [128, NT])
        rstd = sb("rstd", [128, NT])
        minus_half = sb("minus_half", [128, 16])
        ident = cst[:, C_ID:C_ID + 128]

        bank = [es.enter_context(nc.psum_tensor(f"bank{i}", [128, 512], F32)) for i in range(8)]

        mix = ExitStack()
        xt = sb("xt", [128, KC, T], ctx=mix)
        qo = sb("qo", [128, NT, DR], ctx=mix)
        kk = sb("kk", [128, NT, DR], ctx=mix)
        vv = sb("vv", [128, NT, DR], ctx=mix)
        gg = sb("gg", [128, NT, DR], ctx=mix)
        tmp = sb("tmp", [128, 2 * DR], ctx=mix)
        qkt = sb("qkt", [128, 2 * H, T], ctx=mix)
        z = sb("z", [128, CT, ZW], ctx=mix)
        u = sb("u", [128, CT, CW], ctx=mix)
        st0 = sb("st0", [128, H, STREAMS * HD], ctx=mix)
        mcst = sb("mcst", [128, M_W], ctx=mix)
        chn = sb("chn", [128, CT, 5], ctx=mix)
        btr = sb("btr", [128, H], ctx=mix)
        cin = sb("cin", [128, CT, STREAMS, 2], ctx=mix)
        ust = sb("ust", [128, CT, 2 + 2 * STREAMS], ctx=mix)
        gst = sb("gst", [128, NT, H, 6], ctx=mix)
        gmv = sb("gmv", [128, NT, H, 2], ctx=mix)
        gve = sb("gve", [128, NT, H], ctx=mix)
        grs = sb("grs", [128, NT, H], ctx=mix)
        wr = sb("wr", [128, KC, E], ctx=mix)
        br = sb("br", [128, E], ctx=mix)
        nm1 = sb("nm1", [128, NT], ctx=mix)
        ix8 = sb("ix8", [128, NT, 8], U32, ctx=mix)
        gs = sb("gs", [128, NT, 2], ctx=mix)
        room = vv[:, :, :].rearrange("p a b -> p (a b)")
        ones = room[:, 0:128]
        ovt = room[0:3 * E, 128:128 + 6 + MORE + 4 * OV]
        half = room[0:1, 512:512 + 2 + OV // 2]
        room = gg[:, :, :].rearrange("p a b -> p (a b)")
        lg, ex, msk, rk = (room[:, n * NT * E:(n + 1) * NT * E].rearrange("p (t e) -> p t e", t=NT) for n in range(4))
        msk3 = room[:, 4 * NT * E:7 * NT * E].rearrange("p (t r e) -> p t r e", t=NT, r=3)
        m8, ixf = (room[:, 7 * NT * E + n * NT * 8:7 * NT * E + (n + 1) * NT * 8].rearrange("p (t k) -> p t k", t=NT)
                   for n in range(2))
        tr = room[0:E, 7 * NT * E + 2 * NT * 8:7 * NT * E + 2 * NT * 8 + 2 * T].rearrange("p (r t) -> p r t", r=2)
        scores = hid[:, :, :].rearrange("p a b -> p (a b)")[:, 0:H * 512].rearrange("p (h n) -> p h n", h=H)
        qmask = hid[:, :, :].rearrange("p a b -> p (a b)")[:, H * 512:H * 512 + 1024]
        dm = lnp[:, :, :].rearrange("p a b -> p (a b)")
        bias32 = qkt[0:3 * E, :, :].rearrange("p a b -> p (a b)")
        qT, kT = qkt[:, 0:H, :], qkt[:, H:2 * H, :]
        mix.close()

        xg = sb("xg", [128, KC, 128])
        onehot = sb("onehot", [128, NT, 128])
        onehot_g = sb("onehot_g", [128, NT, 128])
        gt = sb("gt", [128, T])
        sel = sb("sel", [3 * E, 2, SLOTS], BF16)
        gate_c = sb("gate_c", [128, 512])
        up_c = sb("up_c", [128, 512])
        sig = sb("sig", [128, 512])
        act_h = sb("act_h", [128, 2, 512])
        act_t = sb("act_t", [128, 2, 4, 128])
        oo = sb("oo", [128, D])

        slot_full = [sem(f"slot_full{i}") for i in range(RING)]
        piece_used = sem("piece_used")
        xt_in, x_in, cst_in, mcst_in, dm_in, st_in = map(sem, ("xt_in", "x_in", "cst_in", "mcst_in", "dm_in", "st_in"))
        chan_in, bias_in, ln1_in, ln2_in, router_in = map(sem, ("chan_in", "bias_in", "ln1_in", "ln2_in", "router_in"))
        states_stored, y_stored = sem("states_stored"), sem("y_stored")
        dve_step = sem("dve_step")
        pool_ready = sem("pool_ready")
        bias_split = sem("bias_split")
        tok_mm, rotated, v_out, g_sig, g_out = map(sem, ("tok_mm", "rotated", "v_out", "g_sig", "g_out"))
        qk_t, qk_t_out = sem("qk_t"), sem("qk_t_out")
        score_mm, score_out = sem("score_mm"), sem("score_out")
        qm_ready, qm_used = sem("qm_ready"), sem("qm_used")
        chan_mm, c_out, u_out, conv_ready = map(sem, ("chan_mm", "c_out", "u_out", "conv_ready"))
        gn_var, gn_rstd, o_free, o_ready_m = map(sem, ("gn_var", "gn_rstd", "o_free", "o_ready_m"))
        kd_ready, stp_mm, stp_out = sem("kd_ready"), sem("stp_mm"), sem("stp_out")
        vm_ready, sts_mm, sts_out = sem("vm_ready"), sem("sts_mm"), sem("sts_out")
        ust_out = sem("ust_out")
        o_t, o_t_out = sem("o_t"), sem("o_t_out")
        mix_mm, res_out, ln_var, ln_rstd, h_ready = map(sem, ("mix_mm", "res_out", "ln_var", "ln_rstd", "h_ready"))
        ln1_done = sem("ln1_done")
        h_t, h_t_out = sem("h_t"), sem("h_t_out")
        logit_mm, lg_out, nm_ready, exp_ready, mask_ready = map(
            sem, ("logit_mm", "lg_out", "nm_ready", "exp_ready", "mask_ready"))
        rank_mm, rank_out, r_t, r_t_out = map(sem, ("rank_mm", "rank_out", "r_t", "r_t_out"))
        cnt_mm, more_ready, cum_mm, ov_ready, ov_mm, tab_ready = map(
            sem, ("cnt_mm", "more_ready", "cum_mm", "ov_ready", "ov_mm", "tab_ready"))
        onehot_ready, sel_ready = sem("onehot_ready"), sem("sel_ready")
        gathered, xg_ready, gt_mm, gt_ready = map(sem, ("gathered", "xg_ready", "gt_mm", "gt_ready"))
        gate_ready, sig_ready, up_ready, prod_ready, act_ready = map(
            sem, ("gate_ready", "sig_ready", "up_ready", "prod_ready", "act_ready"))
        act_tr, act_t_ready, out_ready = map(sem, ("act_tr", "act_t_ready", "out_ready"))
        comb_mm, y_added = sem("comb_mm"), sem("y_added")
        y_stats, y_normed = sem("y_stats"), sem("y_normed")

        def uses(slot):
            return len(range(slot, MIX_PIECES, RING))

        def tok_done(eng, group, t):
            if t < NT - 1:
                eng.wait_ge(tok_mm, (NT - 1) * group + t + 1)
            else:
                eng.wait_ge(piece_used, 2 * (group + 1))

        def chan_done(eng, group, c):
            if c < CT - 1:
                eng.wait_ge(chan_mm, (CT - 1) * (group - 4) + c + 1)
            else:
                eng.wait_ge(piece_used, 2 * (group + 1))

        block = es.enter_context(nc.Block())

        @block.sync
        def _(sp):
            def in_piece(i):
                c, k = IN_COLS[i // 2], (i % 2) * 4 * 128
                return ring[:, i % RING, :].rearrange("p (k n) -> p k n", n=512), \
                    w_in[k:k + 512, c:c + 512].rearrange("(k p) n -> p k n", p=128)

            def out_piece(i):
                k = (i - IN_PIECES) * 256
                return ring[:, i % RING, :].rearrange("p (k n) -> p k n", n=D), \
                    w_out[k:k + 256, :].rearrange("(k p) n -> p k n", p=128)

            for i in range(MIX_PIECES):
                if i >= RING:
                    sp.wait_ge(piece_used, i - RING + 1)
                dst, src = in_piece(i) if i < IN_PIECES else out_piece(i)
                sp.dma_start(dst, src).then_inc(slot_full[i % RING], 16)
                if i == 0:
                    sp.dma_start(xt[:, :, :], x_t.rearrange("(k p) n -> p k n", p=128)).then_inc(xt_in, 16)

            def pair_pieces(first, ea, eb):
                for j in range(PAIR_PIECES):
                    s = (MIX_PIECES + j) % RING
                    sp.wait_ge(piece_used, first + (j - RING + 1))
                    if j < 2 * GU_PIECES:
                        e, k = (ea, eb)[j // GU_PIECES], (j % GU_PIECES) * 128
                        sp.dma_start(ring[:, s, :].unsqueeze(1), w_gu[bass.ds(e, 1), k:k + 128, :]
                                     .rearrange("e p n -> p e n")).then_inc(slot_full[s], 16)
                    else:
                        i = j - 2 * GU_PIECES
                        e, k = (ea, eb)[i // DN_PIECES], (i % DN_PIECES) * 256
                        sp.dma_start(ring[:, s, :].rearrange("p (k n) -> p k n", n=D),
                                     w_down[bass.ds(e, 1), k:k + 256, :].rearrange("e (k p) n -> p (e k) n", p=128)
                                     ).then_inc(slot_full[s], 16)

            with sp.Fori(0, E // 2) as p:
                pair_pieces(MIX_PIECES + PAIR_PIECES * p, 2 * p, 2 * p + 1)
            sp.wait_ge(tab_ready, 1)
            pairs = sp.value_load(ntab[0:1, 0:1], min_val=E // 2, max_val=(E + OV) // 2)
            with sp.If(pairs > E // 2):
                with sp.Fori(E // 2, pairs) as p:
                    ea = sp.value_load(etab[0:1, bass.ds(2 * p - E, 1)], min_val=0, max_val=E - 1)
                    eb = sp.value_load(etab[0:1, bass.ds(2 * p - E + 1, 1)], min_val=0, max_val=E - 1)
                    pair_pieces(MIX_PIECES + PAIR_PIECES * p, ea, eb)
            for t in range(NT):
                sp.wait_ge(y_normed, t + 1)
                sp.dma_start(y_out[t * 128:(t + 1) * 128, :], xy[:, t, :]).then_inc(y_stored, 16)
            sp.wait_ge(y_stored, 16 * NT)
            sp.wait_ge(states_stored, 16 * (H + 2))

        @block.tensor
        def _(pe):
            fills = [0] * RING
            def piece(i):
                fills[i % RING] += 1
                pe.wait_ge(slot_full[i % RING], 16 * fills[i % RING])

            def tok_proj(group, banks):
                for hf in range(2):
                    i = 2 * group + hf
                    piece(i)
                    w = ring[:, i % RING, :].rearrange("p (k n) -> p k n", n=512)
                    for t in range(NT):
                        for k in range(4):
                            c = 4 * hf + k
                            mm = pe.matmul(bank[banks[t]][:, :], xt[:, c, t * 128:(t + 1) * 128], w[:, k, :],
                                           start=(c == 0), stop=(c == KC - 1))
                        if hf == 1 and t < NT - 1:
                            mm.then_inc(tok_mm, 1)
                    mm.then_inc(piece_used, 1)

            def chan_proj(group):
                for hf in range(2):
                    i = 2 * group + hf
                    piece(i)
                    w = ring[:, i % RING, :].rearrange("p (k n) -> p k n", n=512)
                    for c in range(CT):
                        for k in range(4):
                            kc = 4 * hf + k
                            mm = pe.matmul(bank[3 + c][:, 0:T], w[:, k, c * 128:(c + 1) * 128], xt[:, kc, :],
                                           start=(kc == 0), stop=(kc == KC - 1))
                        if hf == 1 and c < CT - 1:
                            mm.then_inc(chan_mm, 1)
                    mm.then_inc(piece_used, 1)

            pe.wait_ge(xt_in, 16)
            tok_proj(0, (0, 1, 2))
            tok_proj(1, (3, 4, 5))
            pe.wait_ge(rotated, 3)
            tok_proj(2, (0, 1, 2))
            pe.wait_ge(rotated, 6)
            tok_proj(3, (3, 4, 5))
            pe.wait_ge(cst_in, 16)
            pe.wait_ge(v_out, 3)
            for n, (src, b) in enumerate(((qo, 0), (qo, 1), (qo, 2), (kk, 7), (kk, 6), (kk, 0))):
                if n == 5:
                    pe.wait_ge(qk_t_out, 1)
                for h in range(H):
                    mm = pe.transpose(bank[b][:, h * 128:(h + 1) * 128],
                                      src[:, n % 3, h * 128:(h + 1) * 128], ident)
                mm.then_inc(qk_t, 1)
            pe.wait_ge(g_out, 3)
            pe.wait_ge(qk_t_out, 5)
            chan_proj(4)
            pe.wait_ge(qk_t_out, 6)
            for h, b in enumerate((0, 1, 2, 7)):
                pe.matmul(bank[b][:, 0:256], kT[:, h, 0:128], qT[:, h, 0:256], start=True, stop=True)
                pe.matmul(bank[b][:, 256:384], kT[:, h, 128:256], qT[:, h, 128:256], start=True, stop=True)
                pe.matmul(bank[b][:, 384:512], kT[:, h, 256:384], qT[:, h, 256:384], start=True, stop=True)\
                    .then_inc(score_mm, 1)
            pe.wait_ge(c_out, CT)
            chan_proj(5)
            pe.wait_ge(score_out, H)
            pe.wait_ge(st_in, 16 * H)
            for h in range(H):
                o = slice(h * 128, (h + 1) * 128)
                s = scores[:, h, :]
                mm = pe.matmul(bank[0][:, o], s[:, 0:128], vv[:, 0, o], start=True, stop=True)
                pe.matmul(bank[1][:, o], s[:, 128:256], vv[:, 0, o], start=True, stop=False)
                pe.matmul(bank[1][:, o], s[:, 256:384], vv[:, 1, o], start=False, stop=True)
                pe.matmul(bank[2][:, o], s[:, 384:512], vv[:, 2, o], start=True, stop=False)
                pe.wait_ge(qm_ready, h + 1)
                for b in range(STREAMS):
                    mm = pe.matmul(bank[2][:, o], qmask[:, b * 128:(b + 1) * 128],
                                   st0[:, h, b * HD:(b + 1) * HD], start=False, stop=(b == STREAMS - 1))
                mm.then_inc(qm_used, 1)
            pe.wait_ge(kd_ready, 1)
            for h in range(H):
                o = slice(h * 128, (h + 1) * 128)
                pe.matmul(bank[7][:, o], kk[:, 0, o], vv[:, 0, o], start=True, stop=False)
                mm = pe.matmul(bank[7][:, o], kk[:, 1, o], vv[:, 1, o], start=False, stop=True)
            mm.then_inc(stp_mm, 1)
            pe.wait_ge(u_out, CT)
            chan_proj(6)
            pe.wait_ge(o_free, NT)
            for h in range(H):
                pe.wait_ge(vm_ready, h + 1)
                for n in range(2):
                    i = 2 * h + n
                    if i >= 2:
                        pe.wait_ge(sts_out, i - 1)
                    mm = pe.matmul(bank[i % 2][:, :], kk[:, 2, h * 128:(h + 1) * 128],
                                   tmp[:, n * 512:(n + 1) * 512], start=True, stop=True)
                    mm.then_inc(sts_mm, 1)
            pe.wait_ge(o_ready_m, NT)
            pe.wait_ge(conv_ready, CT)
            for h in range(H):
                for t in range(NT):
                    mm = pe.transpose(bank[3 + h][:, t * 128:(t + 1) * 128], qo[:, t, h * 128:(h + 1) * 128], ident)
                mm.then_inc(o_t, 1)
            for i in range(OUT_PIECES):
                piece(IN_PIECES + i)
            pe.wait_ge(o_t_out, H)
            pe.wait_ge(sts_out, 2 * H)
            pe.wait_ge(stp_out, 1)
            mix_banks = ((0, 1), (2, 7), (3, 4))
            tr_banks = ((5, 6), (0, 1), (2, 7))

            def wout(t):
                for c in range(KC):
                    w = ring[:, (IN_PIECES + c // 2) % RING, :].rearrange("p (k n) -> p k n", n=D)
                    for n in range(2):
                        mm = pe.matmul(bank[mix_banks[t][n]][:, :], qkt[:, c, t * 128:(t + 1) * 128],
                                       w[:, c % 2, n * 512:(n + 1) * 512], start=(c == 0), stop=(c == KC - 1))
                    if t == NT - 1 and c % 2 == 1:
                        mm.then_inc(piece_used, 1)
                if t < NT - 1:
                    mm.then_inc(mix_mm, 1)

            def transpose_h(t):
                pe.wait_ge(h_ready, t + 1)
                for c in range(KC):
                    mm = pe.transpose(bank[tr_banks[t][c // 4]][:, (c % 4) * 128:(c % 4 + 1) * 128],
                                      hid[:, t, c * 128:(c + 1) * 128], ident)
                mm.then_inc(h_t, 1)

            def logits(t, b):
                pe.wait_ge(h_t_out, 2 * (t + 1))
                for c in range(KC):
                    mm = pe.matmul(bank[b][:, 0:E], xt[:, c, t * 128:(t + 1) * 128], wr[:, c, :],
                                   start=(c == 0), stop=(c == KC - 1))
                mm.then_inc(logit_mm, 1)

            wout(0)
            wout(1)
            pe.wait_ge(router_in, 32)
            transpose_h(0)
            wout(2)
            logits(0, 5)
            transpose_h(1)
            logits(1, 6)
            transpose_h(2)
            logits(2, 3)

            tri = cst[:, C_TRI:C_TRI + 128]
            pe.wait_ge(mask_ready, NT)
            for t in range(NT):
                for s in range(t):
                    pe.matmul(bank[0][:, t * E:(t + 1) * E], ones[:, :], msk[:, s, :], start=(s == 0), stop=False)
                mm = pe.matmul(bank[0][:, t * E:(t + 1) * E], tri, msk[:, t, :], start=(t == 0), stop=True)
            for t in range(NT):
                mm = pe.matmul(bank[1][0:3 * E, 0:1], msk3[:, t, :, :].rearrange("p a b -> p (a b)"), ones[:, 0:1],
                               start=(t == 0), stop=(t == NT - 1))
            mm.then_inc(rank_mm, 1)
            pe.wait_ge(more_ready, 1)
            pe.matmul(bank[2][0:3 * E, 0:1], cst[0:E, C_TRIR:C_TRIR + 96], ovt[0:E, 0:1], start=True, stop=True)
            pe.matmul(bank[2][0:1, 1:2], ovt[0:E, 0:1], ones[0:E, 0:1], start=True, stop=True).then_inc(cum_mm, 1)
            pe.wait_ge(rank_out, 1)
            for t in range(NT):
                pe.transpose(bank[3][0:E, t * 128:(t + 1) * 128], rk[:, t, :], ident)
            for t in range(NT):
                mm = pe.transpose(bank[4][0:E, t * 128:(t + 1) * 128], ex[:, t, :], ident)
            mm.then_inc(r_t, 1)
            pe.wait_ge(r_t_out, 2)
            pe.wait_ge(ov_ready, 1)
            oh = ovt[0:E, 6 + MORE:6 + MORE + OV]
            off = ovt[0:E, 6 + MORE + OV:6 + MORE + 2 * OV]
            for t in range(NT):
                pe.matmul(bank[5][:, t * OV:(t + 1) * OV], tr[:, 0, t * 128:(t + 1) * 128], oh, start=True, stop=False)
                pe.matmul(bank[5][:, t * OV:(t + 1) * OV], ones[0:E, :], off, start=False, stop=True)
                pe.matmul(bank[6][:, t * OV:(t + 1) * OV], tr[:, 1, t * 128:(t + 1) * 128], oh, start=True, stop=True)
            pe.matmul(bank[7][0:1, 0:OV], cst[0:E, C_EC:C_EC + 1], oh, start=True, stop=True).then_inc(ov_mm, 1)

            def gather(first):
                for c in range(KC):
                    for t in range(NT):
                        mm = pe.matmul(bank[6 + c // 4][:, (c % 4) * 128:(c % 4 + 1) * 128],
                                       hid[:, t, c * 128:(c + 1) * 128], onehot[:, t, :],
                                       start=(t == 0), stop=(t == NT - 1))
                mm.then_inc(gathered, 1)

            def gates():
                for t in range(NT):
                    mm = pe.transpose(bank[5][:, t * 128:(t + 1) * 128], onehot_g[:, t, :], ident)
                mm.then_inc(gt_mm, 1)

            def slot_wait(j, p):
                s, turn = (MIX_PIECES + j) % RING, j // RING
                pe.wait_ge(slot_full[s], 16 * (uses(s) + turn + 1) + 32 * p)
                return s

            pe.wait_ge(tab_ready, 1)
            pairs = pe.value_load(ntab[0:1, 0:1], min_val=E // 2, max_val=(E + OV) // 2)
            pe.wait_ge(onehot_ready, 2)
            gather(0)
            gates()
            with pe.Fori(0, pairs) as p:
                def transpose_act(a):
                    pe.wait_ge(act_ready, 2 * p + a + 1)
                    for j in range(4):
                        mm = pe.transpose(bank[5][:, j * 128:(j + 1) * 128],
                                          act_h[:, a, j * 128:(j + 1) * 128], ident)
                    mm.then_inc(act_tr, 1)

                def gate_up(a, middle=None):
                    for n in range(2):
                        for hf in range(2):
                            pe.matmul(bank[2 * a + n][64 * hf:64 * hf + 64, :], sel[:, a, :],
                                      biasp[:, n * FF + hf * 512:n * FF + (hf + 1) * 512], start=True, stop=False)
                    for c in range(KC):
                        if c == 4 and middle:
                            middle()
                        s = slot_wait(GU_PIECES * a + c, p)
                        for n in range(2):
                            for hf in range(2):
                                col = n * FF + hf * 512
                                mm = pe.matmul(bank[2 * a + n][64 * hf:64 * hf + 64, :],
                                               xg[:, c, 64 * a:64 * a + 64], ring[:, s, col:col + 512],
                                               start=False, stop=(c == KC - 1))
                        mm.then_inc(piece_used, 1)

                def down(a, middle=None):
                    for hf in range(2):
                        pe.matmul(bank[4][64 * hf:64 * hf + 64, :], sel[:, a, :],
                                  biasp[:, 2 * FF + hf * 512:2 * FF + (hf + 1) * 512], start=True, stop=False)
                    for c in range(KC):
                        if c == 4 and middle:
                            middle()
                        if c % 2 == 0:
                            s = slot_wait(2 * GU_PIECES + DN_PIECES * a + c // 2, p)
                        w = ring[:, s, :].rearrange("p (k n) -> p k n", n=D)
                        for hf in range(2):
                            mm = pe.matmul(bank[4][64 * hf:64 * hf + 64, :],
                                           act_t[:, a, c % 4, 64 * (c // 4):64 * (c // 4) + 64],
                                           w[:, c % 2, hf * 512:(hf + 1) * 512], start=False, stop=(c == KC - 1))
                        if c % 2 == 1:
                            mm.then_inc(piece_used, 1)

                pe.wait_ge(xg_ready, 2 * p + 2)
                pe.wait_ge(sel_ready, p + 1)
                gate_up(0)
                gate_up(1, middle=lambda: transpose_act(0))
                pe.wait_ge(act_t_ready, 2 * p + 1)
                down(0, middle=lambda: transpose_act(1))
                pe.wait_ge(act_t_ready, 2 * p + 2)
                pe.wait_ge(out_ready, 4 * p + 2)
                down(1)
                pe.wait_ge(out_ready, 4 * p + 4)
                pe.wait_ge(gt_ready, p + 1)
                for i in range(2 * NT):
                    if i >= 3:
                        pe.wait_ge(y_added, 6 * p + i - 2)
                    t, hf = i // 2, i % 2
                    pe.matmul(bank[2 + i % 3][:, :], gt[:, t * 128:(t + 1) * 128], oo[:, hf * 512:(hf + 1) * 512],
                              start=True, stop=True).then_inc(comb_mm, 1)
                pe.wait_ge(onehot_ready, 2 * p + 4)
                gather(1)
                gates()
                pe.wait_ge(y_added, 6 * p + 6)

        @block.scalar
        def _(act):
            act.dma_start(cst[:, :], consts).then_inc(cst_in, 16)
            act.dma_start(mcst[:, :], mconsts).then_inc(mcst_in, 16)
            for n in range(3):
                act.dma_start(bias32[E * n:E * (n + 1), 0:2 * FF], b_gu).then_inc(bias_in, 16)
                act.dma_start(bias32[E * n:E * (n + 1), 2 * FF:], b_down).then_inc(bias_in, 16)
            act.dma_start(chn[:, :, :], chan).then_inc(chan_in, 16)
            act.dma_start(btr[:, :], beta_ret).then_inc(chan_in, 16)
            act.dma_start(cin[:, :, :, :], conv_in).then_inc(chan_in, 16)
            act.dma_start(dm, dmask).then_inc(dm_in, 16)
            for h in range(H):
                act.dma_start(st0[:, h, :].rearrange("p (b e) -> p b e", b=STREAMS),
                              s_ret[:, h].rearrange("b d e -> d b e")).then_inc(st_in, 16)
            act.dma_start(xy[:, :, :], x_tok.rearrange("(t p) n -> p t n", p=128)).then_inc(x_in, 16)
            act.dma_start(wr[:, :, :], w_router.rearrange("(k p) n -> p k n", p=128)).then_inc(router_in, 16)
            act.dma_start(br[:, :], b_router.rearrange("(a n) -> a n", a=1).to_broadcast([128, E]))\
                .then_inc(router_in, 16)

            for t in range(NT):
                tok_done(act, 2, t)
                act.copy(vv[:, t, :], bank[t][:, :]).then_inc(v_out, 1)
            for t in range(NT):
                tok_done(act, 3, t)
                act.activation(gg[:, t, :], bank[3 + t][:, :], ACT.Sigmoid).then_inc(g_sig, 1)
            act.wait_ge(bias_split, 1)
            for n, (dst, b) in enumerate(((qT, 0), (qT, 1), (qT, 2), (kT, 7), (kT, 6), (kT, 0))):
                act.wait_ge(qk_t, n + 1)
                act.copy(dst[:, :, (n % 3) * 128:(n % 3 + 1) * 128],
                         bank[b][:, :].rearrange("p (h n) -> p h n", h=H)).then_inc(qk_t_out, 1)
            for c in range(CT):
                chan_done(act, 4, c)
                act.copy(z[:, c, 0:T], bank[3 + c][:, 0:T]).then_inc(c_out, 1)
            act.wait_ge(score_out, H)
            for n in range(2):
                act.dma_start(lnp[:, n, :], ln1[n:n + 1, :].to_broadcast([128, D])).then_inc(ln1_in, 16)
            act.wait_ge(stp_mm, 1)
            act.wait_ge(qk_t_out, 6)
            act.copy(kk[:, 0, :], bank[7][:, :]).then_inc(stp_out, 1)
            act.wait_ge(stp_out, 1)
            act.dma_start(retp_out.rearrange("h d e -> d h e"), kk[:, 0, :].rearrange("p (h e) -> p h e", h=H))\
                .then_inc(states_stored, 16)
            act.wait_ge(ust_out, 2)
            act.dma_start(conv_out, ust[:, :, :]).then_inc(states_stored, 16)
            act.wait_ge(chan_in, 48)
            for h in range(H):
                act.wait_ge(o_t, h + 1)
                act.activation(qkt[:, h, :], bank[3 + h][:, 0:T], ACT.Copy, scale=btr[:, h:h + 1])\
                    .then_inc(o_t_out, 1)
                act.wait_ge(sts_out, 2 * h + 2)
                act.dma_start(rets_out[:, h].rearrange("b d e -> d b e"),
                              st0[:, h, :].rearrange("p (b e) -> p b e", b=STREAMS)).then_inc(states_stored, 16)
            for t, banks in enumerate(((5, 6), (0, 1), (2, 7))):
                act.wait_ge(h_t, t + 1)
                for n in range(2):
                    act.copy(xt[:, 4 * n:4 * n + 4, t * 128:(t + 1) * 128],
                             bank[banks[n]][:, :].rearrange("p (k n) -> p k n", k=4)).then_inc(h_t_out, 1)
                act.wait_ge(nm_ready, t + 1)
                act.activation(ex[:, t, :], lg[:, t, :], ACT.Exp, bias=nm1[:, t:t + 1]).then_inc(exp_ready, 1)
            act.wait_ge(ln1_done, 1)
            for n in range(2):
                act.dma_start(lnp[:, n, :], ln2[n:n + 1, :].to_broadcast([128, D])).then_inc(ln2_in, 16)
            act.wait_ge(r_t, 1)
            act.copy(tr[:, 0, :], bank[3][0:E, 0:T]).then_inc(r_t_out, 1)
            act.copy(tr[:, 1, :], bank[4][0:E, 0:T]).then_inc(r_t_out, 1)

            def copy_gathered(n):
                act.wait_ge(gathered, n)
                for i in range(2):
                    act.copy(xg[:, 4 * i:4 * i + 4, :].rearrange("p k n -> p (k n)"), bank[6 + i][:, :])\
                        .then_inc(xg_ready, 1)
                act.wait_ge(gt_mm, n)
                act.copy(gt[:, :], bank[5][:, 0:T]).then_inc(gt_ready, 1)

            act.wait_ge(states_stored, 16 * (H + 2))
            act.wait_ge(tab_ready, 1)
            pairs = act.value_load(ntab[0:1, 0:1], min_val=E // 2, max_val=(E + OV) // 2)
            copy_gathered(1)
            with act.Fori(0, pairs) as p:
                for a in range(2):
                    act.wait_ge(gate_ready, 2 * p + a + 1)
                    act.activation(sig[:, :], gate_c[:, :], ACT.Sigmoid, scale=SIG).then_inc(sig_ready, 1)
                    act.wait_ge(act_tr, 2 * p + a + 1)
                    act.copy(act_t[:, a, :, :].rearrange("p k n -> p (k n)"), bank[5][:, :]).then_inc(act_t_ready, 1)
                for a in range(2):
                    act.wait_ge(piece_used, PAIR_PIECES * p + MIX_PIECES + 2 * GU_PIECES + DN_PIECES * (a + 1))
                    for hf in range(2):
                        act.copy(oo[64 * a:64 * a + 64, hf * 512:(hf + 1) * 512],
                                 bank[4][64 * hf:64 * hf + 64, :]).then_inc(out_ready, 1)
                copy_gathered(p + 2)

        @block.gpsimd
        def _(pool):
            pool.memset(minus_half[:, :], -0.5).then_inc(pool_ready, 1)
            pool.memset(u[:, :, 0:2], 0.0).then_inc(pool_ready, 1)
            pool.memset(qmask, 0.0).then_inc(pool_ready, 1)
            pool.memset(sel_all[:, :], 0.0).then_inc(pool_ready, 1)
            pool.memset(rank_all[:, :, :], -1.0).then_inc(pool_ready, 1)
            pool.memset(gate_all[:, :, :], 0.0).then_inc(pool_ready, 1)
            pool.wait_ge(pool_ready, 6)
            for t in range(NT):
                pool.wait_ge(gn_var, t + 1)
                pool.tensor_tensor(grs[:, t, :], gve[:, t, :], minus_half[:, 0:H], ALU.pow).then_inc(gn_rstd, 1)
            for t in range(2 * NT):
                pool.wait_ge(ln_var, t + 1)
                n = t % NT
                pool.tensor_tensor(rstd[:, n:n + 1], veps[:, n:n + 1], minus_half[:, 0:1], ALU.pow)\
                    .then_inc(ln_rstd, 1)

        @block.vector
        def _(dve):
            chain = [0]

            def link(ins):
                chain[0] += 1
                ins.then_inc(dve_step, 1)
                dve.wait_ge(dve_step, chain[0])

            dve.wait_ge(bias_in, 96)
            link(dve.tensor_copy(biasp[:, :], bias32))
            for n in (1, 2):
                for m in range(n, 3):
                    r = slice(E * m, E * (m + 1))
                    ins = dve.tensor_tensor(bias32[r, :], bias32[r, :], biasp[r, :], ALU.subtract)
                    link(ins)
                    ins = dve.tensor_copy(biasp[r, :], bias32[r, :])
                    if n < m:
                        link(ins)
            ins.then_inc(bias_split, 1)

            dve.wait_ge(mcst_in, 16)
            for n, (dst, b) in enumerate(((qo, 0), (qo, 1), (qo, 2), (kk, 3), (kk, 4), (kk, 5))):
                t = n % NT
                cos = mcst[:, M_COS + 64 * t:M_COS + 64 * t + 64].unsqueeze(1)
                sin = mcst[:, M_SIN + 64 * t:M_SIN + 64 * t + 64].unsqueeze(1)
                src = bank[b][:, :].rearrange("p (h s d) -> p h s d", s=2, d=64)
                out = dst[:, t, :].rearrange("p (h s d) -> p h s d", s=2, d=64)
                pc = tmp[:, 0:DR].rearrange("p (h s d) -> p h s d", s=2, d=64)
                ps = tmp[:, DR:].rearrange("p (h s d) -> p h s d", s=2, d=64)
                tok_done(dve, n // NT, t)
                dve.tensor_tensor(tmp[:, 0:DR].rearrange("p (a d) -> p a d", d=64),
                                  bank[b][:, :].rearrange("p (a d) -> p a d", d=64),
                                  cos.to_broadcast([128, 8, 64]), ALU.mult)
                for s in range(2):
                    ins = dve.tensor_tensor(ps[:, :, s, :], src[:, :, 1 - s, :], sin.to_broadcast([128, H, 64]), ALU.mult)
                link(ins)
                dve.tensor_tensor(out[:, :, 0, :], pc[:, :, 0, :], ps[:, :, 0, :], ALU.subtract)
                ins = dve.tensor_tensor(out[:, :, 1, :], pc[:, :, 1, :], ps[:, :, 1, :], ALU.add)
                ins.then_inc(rotated, 1)
                dve.wait_ge(rotated, n + 1)
            for t in range(NT):
                dve.wait_ge(g_sig, t + 1)
                dve.tensor_tensor(gg[:, t, :], gg[:, t, :], bank[3 + t][:, :], ALU.mult).then_inc(g_out, 1)
            dve.wait_ge(dm_in, 16)
            dve.wait_ge(pool_ready, 6)
            for h, b in enumerate((0, 1, 2, 7)):
                dve.wait_ge(score_mm, h + 1)
                dve.tensor_tensor(scores[:, h, :], bank[b][:, :], dm[:, h * 512:(h + 1) * 512], ALU.mult)\
                    .then_inc(score_out, 1)

            def q_slabs(h):
                if h:
                    dve.wait_ge(qm_used, h)
                flat = qmask.rearrange("p (b c) -> p b c", b=STREAMS)
                for_b = bass.AP(tensor=flat.tensor, offset=flat.offset,
                                ap=[list(flat.ap[0]), [128 + STEP, STREAMS], [1, STEP]])
                dve.tensor_tensor(for_b, qT[:, h, SEQ:].rearrange("p (b i) -> p b i", b=STREAMS),
                                  mcst[:, M_QD + h * STEP:M_QD + (h + 1) * STEP].unsqueeze(1)
                                  .to_broadcast([128, STREAMS, STEP]), ALU.mult).then_inc(qm_ready, 1)

            q_slabs(0)
            dve.wait_ge(chan_in, 48)
            sview = u[:, :, SEQ + 2:].rearrange("p c (b i) -> p c b i", b=STREAMS)
            dve.tensor_copy(sview[:, :, :, 0:2], cin[:, :, :, :])
            for c in range(CT):
                chan_done(dve, 5, c)
                b = bank[3 + c]
                dve.tensor_tensor(u[:, c, 2:SEQ + 2], b[:, 0:SEQ], z[:, c, 0:SEQ], ALU.mult)
                dve.tensor_tensor(sview[:, c, :, 2:], b[:, SEQ:T].rearrange("p (b i) -> p b i", b=STREAMS),
                                  z[:, c, SEQ:T].rearrange("p (b i) -> p b i", b=STREAMS), ALU.mult)\
                    .then_inc(u_out, 1)
            for h in range(1, H):
                q_slabs(h)
            dve.wait_ge(u_out, CT)
            dve.tensor_copy(ust[:, :, 0:2], u[:, :, SEQ:SEQ + 2]).then_inc(ust_out, 1)
            dve.tensor_copy(ust[:, :, 2:].rearrange("p c (b r) -> p c b r", r=2), sview[:, :, :, STEP:])\
                .then_inc(ust_out, 1)
            dve.wait_ge(qk_t_out, 6)
            for t in range(NT):
                ins = dve.tensor_tensor(kk[:, t, :].rearrange("p (h d) -> p h d", h=H),
                                        kk[:, t, :].rearrange("p (h d) -> p h d", h=H),
                                        mcst[:, M_KD + t * H:M_KD + (t + 1) * H].unsqueeze(2)
                                        .to_broadcast([128, H, HD]), ALU.mult)
            ins.then_inc(kd_ready, 1)
            dve.wait_ge(qm_used, H)
            for t in range(NT):
                for h in range(H):
                    ins = dve.bn_stats(gst[:, t, h, :], bank[t][:, h * 128:(h + 1) * 128])
                link(ins)
                for h in range(H):
                    ins = dve.bn_aggr(gmv[:, t, h, :], gst[:, t, h, :])
                link(ins)
                dve.tensor_scalar_add(gve[:, t, :], gmv[:, t, :, 1], EPS).then_inc(gn_var, 1)
            def v_streams(h):
                if h:
                    dve.wait_ge(sts_mm, 2 * h)
                dve.tensor_tensor(tmp[:, :].rearrange("p (b e) -> p b e", b=STREAMS),
                                  vv[:, 2, h * 128:(h + 1) * 128].unsqueeze(1).to_broadcast([128, STREAMS, HD]),
                                  cst[:, C_BM:C_BM + 8].unsqueeze(2).to_broadcast([128, STREAMS, HD]), ALU.mult)\
                    .then_inc(vm_ready, 1)

            dve.wait_ge(cst_in, 16)
            v_streams(0)
            for t in range(NT):
                dve.wait_ge(gn_rstd, t + 1)
                for h in range(H):
                    ins = dve.tensor_scalar(qo[:, t, h * 128:(h + 1) * 128], bank[t][:, h * 128:(h + 1) * 128],
                                            gmv[:, t, h, 0:1], grs[:, t, h:h + 1], ALU.subtract, ALU.mult)
                ins.then_inc(o_free, 1)
                dve.wait_ge(o_free, t + 1)
                dve.tensor_tensor(qo[:, t, :], qo[:, t, :], gg[:, t, :], ALU.mult).then_inc(o_ready_m, 1)
            for c in range(CT):
                ins = dve.tensor_scalar(z[:, c, :], u[:, c, 0:ZW], chn[:, c, 0:1], chn[:, c, 3:4], ALU.mult, ALU.add)
            for tap in (1, 2):
                link(ins)
                for c in range(CT):
                    ins = dve.scalar_tensor_tensor(z[:, c, :], u[:, c, tap:tap + ZW], chn[:, c, tap:tap + 1],
                                             z[:, c, :], ALU.mult, ALU.add)
            link(ins)
            for c in range(CT):
                chan_done(dve, 6, c)
                b = bank[3 + c]
                dve.scalar_tensor_tensor(qkt[:, H + c, 0:SEQ], b[:, 0:SEQ], chn[:, c, 4:5], z[:, c, 0:SEQ],
                                         ALU.mult, ALU.mult)
                zs = z[:, c, SEQ + 2:SEQ + 2 + (STREAMS - 1) * (STEP + 2) + STEP]
                zs = bass.AP(tensor=zs.tensor, offset=zs.offset,
                             ap=[list(zs.ap[0]), [STEP + 2, STREAMS], [1, STEP]])
                dve.scalar_tensor_tensor(qkt[:, H + c, SEQ:T].rearrange("p (b i) -> p b i", b=STREAMS),
                                         b[:, SEQ:T].rearrange("p (b i) -> p b i", b=STREAMS), chn[:, c, 4:5],
                                         zs, ALU.mult, ALU.mult).then_inc(conv_ready, 1)
            dve.wait_ge(st_in, 16 * H)
            for h in range(H):
                for n in range(2):
                    i = 2 * h + n
                    dve.wait_ge(sts_mm, i + 1)
                    o = slice(n * 512, (n + 1) * 512)
                    dve.scalar_tensor_tensor(st0[:, h, o], st0[:, h, o], float(carry[h]), bank[i % 2][:, :],
                                             ALU.mult, ALU.add).then_inc(sts_out, 1)
                if h < H - 1:
                    v_streams(h + 1)
            link(dve.memset(ones[:, :], 1.0))

            def norm(t, count, rows):
                for n in range(2):
                    ins = dve.bn_stats(stat[:, t, n, :], rows[:, n * 512:(n + 1) * 512])
                link(ins)
                link(dve.bn_aggr(mv[:, t, :], stat[:, t, :, :].rearrange("p a b -> p (a b)")))
                dve.tensor_scalar_add(veps[:, t:t + 1], mv[:, t, 1:2], EPS).then_inc(ln_var, 1)
                dve.wait_ge(ln_rstd, count)

            dve.wait_ge(x_in, 16)
            dve.wait_ge(ln1_in, 32)
            dve.wait_ge(router_in, 32)

            def first_norm(t, banks):
                if t < NT - 1:
                    dve.wait_ge(mix_mm, t + 1)
                else:
                    dve.wait_ge(piece_used, MIX_PIECES)
                for n in range(2):
                    o = slice(n * 512, (n + 1) * 512)
                    ins = dve.scalar_tensor_tensor(xy[:, t, o], xy[:, t, o], ALPHA, bank[banks[n]][:, :],
                                                   ALU.mult, ALU.add)
                link(ins)
                norm(t, t + 1, xy[:, t, :])
                link(dve.tensor_scalar(hid[:, t, :], xy[:, t, :], mv[:, t, 0:1], rstd[:, t:t + 1],
                                       ALU.subtract, ALU.mult))
                link(dve.tensor_tensor(hid[:, t, :], hid[:, t, :], lnp[:, 0, :], ALU.mult))
                dve.tensor_tensor(hid[:, t, :], hid[:, t, :], lnp[:, 1, :], ALU.add).then_inc(h_ready, 1)
                dve.wait_ge(h_ready, t + 1)
                ins = dve.tensor_scalar(xy[:, t, :], hid[:, t, :], ALPHA, None, ALU.mult)
                if t == NT - 1:
                    ins.then_inc(ln1_done, 1)

            def route(t, b):
                dve.wait_ge(logit_mm, t + 1)
                dve.tensor_tensor(lg[:, t, :], bank[b][:, 0:E], br[:, :], ALU.add).then_inc(lg_out, 1)
                dve.wait_ge(lg_out, t + 1)
                link(dve.max(m8[:, t, :], lg[:, t, :]))
                dve.tensor_scalar(nm1[:, t:t + 1], m8[:, t, 0:1], -1.0, None, ALU.mult).then_inc(nm_ready, 1)
                link(dve.max_index(ix8[:, t, :], m8[:, t, :], lg[:, t, :]))
                link(dve.tensor_copy(ixf[:, t, :], ix8[:, t, :]))
                iota = cst[:, C_IOTA:C_IOTA + E]
                link(dve.tensor_scalar(msk[:, t, :], iota, ixf[:, t, 0:1], None, ALU.is_equal))
                for k in range(1, TOPK):
                    link(dve.scalar_tensor_tensor(msk[:, t, :], iota, ixf[:, t, k:k + 1], msk[:, t, :],
                                                  ALU.is_equal, ALU.add))
                dve.tensor_copy(msk3[:, t, :, :], msk[:, t, :].unsqueeze(1).to_broadcast([128, 3, E]))\
                    .then_inc(mask_ready, 1)
                dve.wait_ge(exp_ready, t + 1)
                link(dve.tensor_tensor(ex[:, t, :], ex[:, t, :], msk[:, t, :], ALU.mult))
                link(dve.reduce_sum(gs[:, t, 0:1], ex[:, t, :], AXX))
                link(dve.reciprocal(gs[:, t, 1:2], gs[:, t, 0:1]))
                link(dve.tensor_scalar(ex[:, t, :], ex[:, t, :], gs[:, t, 1:2], None, ALU.mult))

            first_norm(0, (0, 1))
            first_norm(1, (2, 7))
            route(0, 5)
            first_norm(2, (3, 4))
            route(1, 6)
            route(2, 3)
            dve.wait_ge(rank_mm, 1)
            dve.scalar_tensor_tensor(rk[:, :, :].rearrange("p a b -> p (a b)"), bank[0][:, 0:NT * E], 1.0,
                                     msk[:, :, :].rearrange("p a b -> p (a b)"), ALU.add, ALU.mult)\
                .then_inc(rank_out, 1)
            dve.wait_ge(rank_out, 1)
            cnt, more, cum, end = ovt[:, 1:2], ovt[:, 0:1], ovt[:, 2:3], ovt[:, 3:4]
            thr_w = ovt[:, 6:6 + MORE]
            oh = ovt[:, 6 + MORE:6 + MORE + OV]
            off = ovt[:, 6 + MORE + OV:6 + MORE + 2 * OV]
            ws = ovt[:, 6 + MORE + 2 * OV:6 + MORE + 3 * OV]
            wq = ovt[:, 6 + MORE + 3 * OV:6 + MORE + 4 * OV]
            rows = slice(0, 3 * E)
            link(dve.tensor_copy(cnt, bank[1][0:3 * E, 0:1]))
            link(dve.tensor_scalar(thr_w, cst[rows, C_THR:C_THR + MORE], cnt, None, ALU.is_lt))
            dve.reduce_sum(more, thr_w, AXX).then_inc(more_ready, 1)
            dve.tensor_copy(sel_all[:, 0:E], cst[rows, C_SEL:C_SEL + E])
            dve.tensor_scalar(rank_all[:, :, 0:E], rk[:, :, :], -1.0, None, ALU.add)
            dve.tensor_copy(gate_all[:, :, 0:E], ex[:, :, :])
            dve.wait_ge(cum_mm, 1)
            link(dve.tensor_copy(cum, bank[2][0:3 * E, 0:1]))
            link(dve.tensor_tensor(end, cum, more, ALU.add))
            orow = cst[rows, C_OV:C_OV + OV]
            dve.tensor_scalar(ws, orow, cum, None, ALU.is_ge)
            link(dve.tensor_scalar(wq, orow, end, None, ALU.is_lt))
            link(dve.tensor_tensor(oh, ws, wq, ALU.mult))
            link(dve.tensor_scalar(ws, orow, cum, -float(SLOTS), ALU.subtract, ALU.mult))
            link(dve.scalar_tensor_tensor(off, ws, -float(SLOTS), oh, ALU.add, ALU.mult))
            dve.tensor_copy(sel_all[:, E:E + OV], oh).then_inc(ov_ready, 1)
            link(dve.tensor_copy(half[:, 0:1], bank[2][0:1, 1:2]))
            link(dve.tensor_scalar(half[:, 2:], cst[0:1, C_HALF:C_W], half[:, 0:1], None, ALU.is_lt))
            link(dve.reduce_sum(half[:, 1:2], half[:, 2:], AXX))
            dve.tensor_scalar(ntab[:, 0:1], half[:, 1:2], float(E // 2), None, ALU.add)
            dve.wait_ge(ov_mm, 1)
            dve.tensor_copy(etab[:, :], bank[7][0:1, 0:OV])
            dve.tensor_scalar(rank_all[:, :, E:E + OV], bank[5][:, 0:NT * OV].rearrange("p (t o) -> p t o", t=NT),
                              -1.0, None, ALU.add)
            dve.tensor_copy(gate_all[:, :, E:E + OV], bank[6][:, 0:NT * OV].rearrange("p (t o) -> p t o", t=NT))\
                .then_inc(tab_ready, 1)
            dve.wait_ge(tab_ready, 1)

            def slots_of(n, done):
                iota = cst[:, C_IOTA:C_IOTA + SLOTS].unsqueeze(1).unsqueeze(1).to_broadcast([128, NT, 2, SLOTS])
                rank = rank_all[:, :, bass.ds(2 * n, 2)].unsqueeze(3).to_broadcast([128, NT, 2, SLOTS])
                gate = gate_all[:, :, bass.ds(2 * n, 2)].unsqueeze(3).to_broadcast([128, NT, 2, SLOTS])
                oh4 = onehot[:, :, :].rearrange("p t (a s) -> p t a s", a=2)
                og4 = onehot_g[:, :, :].rearrange("p t (a s) -> p t a s", a=2)
                dve.tensor_tensor(oh4, iota, rank, ALU.is_equal).then_inc(onehot_ready, 1)
                dve.wait_ge(onehot_ready, 2 * done + 1)
                dve.tensor_tensor(og4, oh4, gate, ALU.mult).then_inc(onehot_ready, 1)

            def rows_of(n):
                dve.tensor_copy(sel[:, :, :], sel_all[:, bass.ds(2 * n, 2)].unsqueeze(2)
                                .to_broadcast([3 * E, 2, SLOTS])).then_inc(sel_ready, 1)

            dve.wait_ge(h_t_out, 2 * NT)
            dve.wait_ge(r_t_out, 2)
            dve.wait_ge(states_stored, 16 * (H + 2))
            pairs = dve.value_load(ntab[0:1, 0:1], min_val=E // 2, max_val=(E + OV) // 2)
            slots_of(0, 0)
            rows_of(0)
            with dve.Fori(0, pairs) as p:
                dve.wait_ge(gt_mm, p + 1)
                slots_of(p + 1, p + 1)
                for a in range(2):
                    n = 2 * p + a + 1
                    dve.wait_ge(piece_used, PAIR_PIECES * p + MIX_PIECES + GU_PIECES * (a + 1))
                    dve.tensor_scalar(gate_c[:, :], bank[2 * a][:, :], LIMIT, None, ALU.min).then_inc(gate_ready, 1)
                    dve.tensor_scalar(up_c[:, :], bank[2 * a + 1][:, :], LIMIT, -LIMIT, ALU.min, ALU.max)\
                        .then_inc(up_ready, 1)
                    dve.wait_ge(gate_ready, n)
                    dve.wait_ge(up_ready, n)
                    dve.scalar_tensor_tensor(up_c[:, :], up_c[:, :], 1.0, gate_c[:, :], ALU.add, ALU.mult)\
                        .then_inc(prod_ready, 1)
                    dve.wait_ge(prod_ready, n)
                    dve.wait_ge(sig_ready, n)
                    dve.tensor_tensor(act_h[:, a, :], up_c[:, :], sig[:, :], ALU.mult).then_inc(act_ready, 1)
                for i in range(2 * NT):
                    t, hf = i // 2, i % 2
                    o = slice(hf * 512, (hf + 1) * 512)
                    dve.wait_ge(comb_mm, 6 * p + i + 1)
                    dve.tensor_tensor(xy[:, t, o], xy[:, t, o], bank[2 + i % 3][:, :], ALU.add).then_inc(y_added, 1)
                rows_of(p + 1)
            dve.wait_ge(ln2_in, 32)
            for t in range(NT):
                dve.wait_ge(y_added, 6 * (E // 2))
                norm(t, NT + t + 1, xy[:, t, :])
                link(dve.tensor_scalar(xy[:, t, :], xy[:, t, :], mv[:, t, 0:1], rstd[:, t:t + 1],
                                       ALU.subtract, ALU.mult))
                link(dve.tensor_tensor(xy[:, t, :], xy[:, t, :], lnp[:, 0, :], ALU.mult))
                dve.tensor_tensor(xy[:, t, :], xy[:, t, :], lnp[:, 1, :], ALU.add).then_inc(y_normed, 1)


def kernel(x_prompt, x_sample, state_retention, state_conv, w_in, beta_ret, beta_conv, conv_w, conv_b, w_out,
           ln1_g, ln1_b, w_router, b_router, w_gu, b_gu, w_down, b_down, ln2_g, ln2_b):
    import concourse.bacc as bacc
    from concourse.bass_utils import run_bass_kernel_spmd

    a = np.ascontiguousarray
    x = np.concatenate([np.asarray(x_prompt).reshape(SEQ, D), np.asarray(x_sample).reshape(STREAMS * STEP, D)])
    by_channel = [np.asarray(v).reshape(CT, 128).T for v in
                  (*np.asarray(conv_w)[0], np.asarray(conv_b)[0], np.asarray(beta_conv)[0])]
    c, m, dmask, _ = constants()
    arrays = {
        "x_tok": a(x), "x_t": a(x.T), "s_ret": a(np.asarray(state_retention)[0]),
        "conv_in": a(np.asarray(state_conv)[0].reshape(STREAMS, 2, CT, 128).transpose(3, 2, 0, 1)),
        "w_in": a(np.asarray(w_in)[0]), "w_out": a(np.asarray(w_out)[0]),
        "chan": a(np.stack(by_channel, axis=-1)), "beta_ret": a(np.asarray(beta_ret).reshape(H, 128).T),
        "ln1": a(np.concatenate([np.asarray(ln1_g), np.asarray(ln1_b)])),
        "ln2": a(np.concatenate([np.asarray(ln2_g), np.asarray(ln2_b)])),
        "w_router": a(np.asarray(w_router)[0]), "b_router": a(np.asarray(b_router)[0]),
        "w_gu": a(np.asarray(w_gu)[0]), "b_gu": a(np.asarray(b_gu)[0]),
        "w_down": a(np.asarray(w_down)[0]), "b_down": a(np.asarray(b_down)[0]),
        "consts": c, "mconsts": m, "dmask": dmask,
    }
    outs = {"y": (T, D), "retp": (H, HD, HD), "rets": (STREAMS, H, HD, HD), "convs": (128, CT, 2 + 2 * STREAMS)}
    nc = bacc.Bacc("TRN2", target_bir_lowering=False, num_devices=1, dynamic_dma_scratch_size=1024)
    args = [nc.dram_tensor(n, v.shape, F32, kind="ExternalInput").ap() for n, v in arrays.items()]
    args += [nc.dram_tensor(n, s, F32, kind="ExternalOutput").ap() for n, s in outs.items()]
    build(nc, *args)
    r = run_bass_kernel_spmd(nc, [arrays], core_ids=[0]).results[0]
    y, conv = r["y"], r["convs"].transpose(2, 1, 0).reshape(2 + 2 * STREAMS, DC)
    return (y[:SEQ].reshape(1, SEQ, D), y[SEQ:].reshape(STREAMS, STEP, D),
            r["retp"].reshape(1, 1, H, HD, HD), a(conv[:2]).reshape(1, 1, 2, DC),
            r["rets"].reshape(1, STREAMS, H, HD, HD), a(conv[2:]).reshape(1, STREAMS, 2, DC))
```

```python
import math
from contextlib import ExitStack

import numpy as np

import concourse.bass as bass
from concourse import mybir

F32 = mybir.dt.float32
BF16 = mybir.dt.bfloat16
I32 = mybir.dt.int32
U32 = mybir.dt.uint32
ALU = mybir.AluOpType
ACT = mybir.ActivationFunctionType
AXX = mybir.AxisListType.X

D = 1024
KC = D // 128
SEQ, STREAMS, STEP = 256, 8, 16
PAST = 128
T = SEQ + STREAMS * STEP
NT = T // 128
PT = SEQ // 128
DR = 512
H, HD = 4, 128
DC = 512
CT = DC // 128
TAPS = 3
E = 32
TOPK = 4
FF = 1024
LIMIT = 7.0
SIG = 1.702
EPS = 1e-5
ALPHA = 2.0 ** 0.25
SLOTS = 64
MORE = T // SLOTS - 1
OV = (T * TOPK) // (SLOTS + 1) + 1
OV += OV % 2
NB = E + OV
RING = 12
PW = 2048
IN_COLS = [0, DR, 2 * DR, 3 * DR, 4 * DR + DC, 4 * DR + 2 * DC, 4 * DR]
IN_PIECES = 2 * len(IN_COLS)
OUT_PIECES = 4
MIX_PIECES = IN_PIECES + OUT_PIECES
GU_PIECES, DN_PIECES = 8, 4
PAIR_PIECES = 2 * (GU_PIECES + DN_PIECES)
EXTRA = 5
EXTRA_AT = RING - EXTRA
FIRST_RING = MIX_PIECES + PAIR_PIECES - EXTRA
CW = SEQ + 2 + STREAMS * (STEP + 2)
ZW = CW - 2

C_ID, C_IOTA, C_TRI, C_BM, C_TRIR, C_EC, C_SEL, C_OV, C_THR, C_HALF = np.cumsum(
    [0, 128, 1 + SLOTS, 128, 8, 96, 1, 32, OV, MORE]).tolist()
C_W = C_HALF + OV // 2
M_COS, M_SIN, M_QD, M_KD = np.cumsum([0, NT * 64, NT * 64, H * STEP]).tolist()
M_W = M_KD + NT * H


def constants():
    c = np.zeros((128, C_W), np.float32)
    p = np.arange(128)
    c[:, C_ID:C_ID + 128] = np.eye(128)
    c[:, C_IOTA:C_IOTA + 1 + SLOTS] = np.arange(1 + SLOTS)
    c[:, C_TRI:C_TRI + 128] = p[:, None] < p[None, :]
    c[:, C_BM:C_BM + 8] = (p[:, None] // STEP) == np.arange(8)
    c[:, C_TRIR:C_TRIR + 96] = p[:, None] < (np.arange(96) % E)[None, :]
    c[:, C_EC] = p
    c[:, C_SEL:C_SEL + E] = (p[:, None] % E) == np.arange(E)
    c[:, C_OV:C_OV + OV] = np.arange(OV)
    c[:, C_THR:C_THR + MORE] = SLOTS * np.arange(1, MORE + 1)
    c[:, C_HALF:] = 2 * np.arange(OV // 2)
    gamma = 1.0 - 2.0 ** (-5.0 - np.arange(H))
    lg = np.log(gamma)
    m = np.zeros((128, M_W), np.float32)
    pos = np.stack([p, 128 + p, PAST + p % STEP], 1).astype(np.float32)
    inv = (np.float32(10000.0) ** (-np.arange(0, HD, 2, dtype=np.float32) / np.float32(HD))).astype(np.float32)
    ang = (pos[:, :, None] * inv).astype(np.float32)
    m[:, M_COS:M_SIN] = np.cos(ang).reshape(128, -1)
    m[:, M_SIN:M_QD] = np.sin(ang).reshape(128, -1)
    m[:, M_QD:M_KD] = np.exp(lg[:, None] * (np.arange(STEP) + 1.0)).reshape(1, -1)
    scale = HD ** -0.5
    left = np.stack([255 - p, 127 - p, STEP - 1 - p % STEP], 1)
    m[:, M_KD:] = (np.exp(lg * left[:, :, None]) * scale).reshape(128, -1)
    d = np.zeros((128, H, 4, 128))
    diff = p[None, :] - p[:, None]
    same = (p[None, :] // STEP) == (p[:, None] // STEP)
    for h in range(H):
        near = np.where(diff >= 0, np.exp(lg[h] * np.maximum(diff, 0)), 0.0)
        d[:, h, 0] = near
        d[:, h, 1] = np.exp(lg[h] * (diff + 128))
        d[:, h, 2] = near
        d[:, h, 3] = near * same
    return c, m, (d * scale).reshape(128, H * 512).astype(np.float32), np.exp(lg * STEP)


def build(nc, x_tok, x_t, s_ret, conv_in, w_in, w_out, chan, beta_ret, ln1, ln2, w_router, b_router,
          w_gu, b_gu, w_down, b_down, consts, mconsts, dmask, y_out, retp_out, rets_out, conv_out):
    carry = constants()[3]
    es = ExitStack()
    with es:
        def sb(name, shape, dt=F32, ctx=es):
            return ctx.enter_context(nc.sbuf_tensor(name, shape, dt))

        def sem(name):
            return es.enter_context(nc.semaphore(name))

        ring = sb("ring", [128, RING, PW])
        xy = sb("xy", [128, NT, D])
        hid = sb("hid", [128, NT, D])
        lnp = sb("lnp", [128, 2, D])
        cst = sb("cst", [128, C_W])
        biasp = sb("biasp", [3 * E, 3 * D], BF16)
        sel_all = sb("sel_all", [3 * E, NB])
        rank_all = sb("rank_all", [128, NT, NB])
        gate_all = sb("gate_all", [128, NT, NB])
        etab = sb("etab", [1, OV], I32)
        ntab = sb("ntab", [1, 2], I32)
        stat = sb("stat", [128, NT, 2, 6])
        mv = sb("mv", [128, NT, 2])
        veps = sb("veps", [128, NT])
        rstd = sb("rstd", [128, NT])
        shift = sb("shift", [128, NT])
        minus_half = sb("minus_half", [128, 16])
        ident = cst[:, C_ID:C_ID + 128]

        bank = [es.enter_context(nc.psum_tensor(f"bank{i}", [128, 512], F32)) for i in range(8)]

        mix = ExitStack()
        xt = sb("xt", [128, KC, T], ctx=mix)
        qkt = sb("qkt", [128, 2 * H, T], ctx=mix)
        qo = sb("qo", [128, NT, DR], ctx=mix)
        gg = sb("gg", [128, NT, DR], ctx=mix)
        vv = sb("vv", [128, NT, DR], ctx=mix)
        kk = sb("kk", [128, NT, DR], ctx=mix)
        tmp = sb("tmp", [128, 2, DR], ctx=mix)
        zu = sb("zu", [128, CT * (ZW + CW)], ctx=mix)
        st0 = sb("st0", [128, H, STREAMS * HD], ctx=mix)
        mcst = sb("mcst", [128, M_W], ctx=mix)
        z = zu[:, 0:CT * ZW].rearrange("p (c n) -> p c n", c=CT)
        u = zu[:, CT * ZW:].rearrange("p (c n) -> p c n", c=CT)
        bias32 = zu[0:3 * E, 0:3 * D]
        chn = sb("chn", [128, CT, 5], ctx=mix)
        btr = sb("btr", [128, H], ctx=mix)
        cin = sb("cin", [128, CT, STREAMS, 2], ctx=mix)
        ust = sb("ust", [128, CT, 2 + 2 * STREAMS], ctx=mix)
        gst = sb("gst", [128, NT, H, 6], ctx=mix)
        gmv = sb("gmv", [128, NT, H, 2], ctx=mix)
        gve = sb("gve", [128, NT, H], ctx=mix)
        grs = sb("grs", [128, NT, H], ctx=mix)
        wr = sb("wr", [128, KC, E], ctx=mix)
        br = sb("br", [128, E], ctx=mix)
        nm1 = sb("nm1", [128, NT], ctx=mix)
        ix8 = sb("ix8", [128, NT, 8], U32, ctx=mix)
        gs = sb("gs", [128, NT, 2], ctx=mix)
        m8 = sb("m8", [128, NT, 8], ctx=mix)
        room = vv[:, :, :].rearrange("p a b -> p (a b)")
        cut = [0]

        def carve(words):
            cut[0] += words
            assert cut[0] <= NT * DR
            return room[:, cut[0] - words:cut[0]]

        ones = carve(128)
        lg, ex, msk = (carve(NT * E).rearrange("p (t e) -> p t e", t=NT) for _ in range(3))
        msk3 = carve(3 * E)
        picks = carve(TOPK * E).rearrange("p (k e) -> p k e", k=TOPK)
        tr = carve(2 * T)[0:E, :].rearrange("p (r t) -> p r t", r=2)
        ovt = carve(6 + MORE + 4 * OV)[0:3 * E, :]
        half = carve(2 + OV // 2)[0:1, :]
        hflat = hid[:, :, :].rearrange("p a b -> p (a b)")
        scores = hflat[:, 0:H * 512].rearrange("p (h n) -> p h n", h=H)
        qmask = hflat[:, H * 512:H * 512 + 1024]
        dm = lnp[:, :, :].rearrange("p a b -> p (a b)")
        qT, kT = qkt[:, 0:H, :], qkt[:, H:2 * H, :]
        mix.close()

        act_h = sb("act_h", [128, 2, 512])
        act_t = sb("act_t", [128, 2, 4, 128])
        oo = sb("oo", [128, D])
        xg = sb("xg", [128, KC, 128])
        onehot = sb("onehot", [128, NT, 128])
        onehot_g = sb("onehot_g", [128, NT, 128])
        gt = sb("gt", [128, T])
        sel = sb("sel", [3 * E, 2, SLOTS], BF16)
        gate_c = sb("gate_c", [128, 512])
        up_c = sb("up_c", [128, 512])
        sig = sb("sig", [128, 512])
        with ExitStack() as gap:
            kept = [sb("kept_free", [128, (KC + 2 * H) * T + 2 * NT * DR - (4 * D + 3 * T + SLOTS + 3 * 512)], ctx=gap),
                    sb("kept_router", [128, NT * DR], ctx=gap)]
            extra = sb("extra", [128, EXTRA, PW], ctx=gap)

        slot_full = [sem(f"slot_full{i}") for i in range(RING)]
        extra_full = [sem(f"extra_full{i}") for i in range(EXTRA)]
        piece_used = sem("piece_used")
        first_in = [sem(f"first_in{k}") for k in range(4)]
        xt_in, x_in, cst_in, mcst_in, dm_in, st_in = map(sem, ("xt_in", "x_in", "cst_in", "mcst_in", "dm_in", "st_in"))
        chan_in, bias_in, ln1_in, ln2_in, router_in = map(sem, ("chan_in", "bias_in", "ln1_in", "ln2_in", "router_in"))
        states_stored, y_stored = sem("states_stored"), sem("y_stored")
        dve_step = sem("dve_step")
        pool_ready = sem("pool_ready")
        bias_split = sem("bias_split")
        tok_mm, rotated, v_out, g_sig, g_out = map(sem, ("tok_mm", "rotated", "v_out", "g_sig", "g_out"))
        qk_t, qk_t_out = sem("qk_t"), sem("qk_t_out")
        score_mm, score_out = sem("score_mm"), sem("score_out")
        qm_ready, qm_used = sem("qm_ready"), sem("qm_used")
        chan_mm, c_out, u_out, conv_ready = map(sem, ("chan_mm", "c_out", "u_out", "conv_ready"))
        gn_var, gn_rstd, o_free, o_ready_m = map(sem, ("gn_var", "gn_rstd", "o_free", "o_ready_m"))
        kd_ready, stp_mm, stp_out = sem("kd_ready"), sem("stp_mm"), sem("stp_out")
        vm_ready, sts_mm, sts_out = sem("vm_ready"), sem("sts_mm"), sem("sts_out")
        ust_out = sem("ust_out")
        o_t, o_t_out = sem("o_t"), sem("o_t_out")
        mix_mm, res_out, ln_var, ln_rstd, h_ready = map(sem, ("mix_mm", "res_out", "ln_var", "ln_rstd", "h_ready"))
        y_init = sem("y_init")
        h_t, h_t_out, h_t_out_v = sem("h_t"), sem("h_t_out"), sem("h_t_out_v")
        logit_mm, lg_out, nm_ready, exp_ready, mask_ready = map(
            sem, ("logit_mm", "lg_out", "nm_ready", "exp_ready", "mask_ready"))
        rank_mm, rank_out, r_t, r_t_out = map(sem, ("rank_mm", "rank_out", "r_t", "r_t_out"))
        first_slots, xg_ready_v, gates_out = sem("first_slots"), sem("xg_ready_v"), sem("gates_out")
        counts_in, cnt_mm, more_ready, cum_mm, ov_ready, ov_mm, tab_ready = map(
            sem, ("counts_in", "cnt_mm", "more_ready", "cum_mm", "ov_ready", "ov_mm", "tab_ready"))
        onehot_ready, sel_ready = sem("onehot_ready"), sem("sel_ready")
        gathered, xg_ready, gt_mm, gt_ready = map(sem, ("gathered", "xg_ready", "gt_mm", "gt_ready"))
        gate_ready, sig_ready, up_ready, prod_ready, act_ready = map(
            sem, ("gate_ready", "sig_ready", "up_ready", "prod_ready", "act_ready"))
        act_tr, act_t_ready, out_ready = map(sem, ("act_tr", "act_t_ready", "out_ready"))
        comb_mm, y_added = sem("comb_mm"), sem("y_added")
        y_shift, y_scaled, y_gained, y_normed = map(sem, ("y_shift", "y_scaled", "y_gained", "y_normed"))

        last_banks = (2, 3, 4, 0, 1, 5)

        def fill_of(piece):
            j = piece - MIX_PIECES
            if EXTRA_AT <= j < RING:
                return None
            return piece if j < EXTRA_AT else piece - EXTRA

        piece_of = {fill_of(i): i for i in range(MIX_PIECES + PAIR_PIECES) if fill_of(i) is not None}

        def loop_slot(j):
            s = (FIRST_RING + j) % RING
            return s, len(range(s, FIRST_RING, RING)) + j // RING

        def tok_done(eng, group, t):
            if t < NT - 1:
                eng.wait_ge(tok_mm, (NT - 1) * group + t + 1)
            else:
                eng.wait_ge(piece_used, 2 * (group + 1))

        def chan_done(eng, group, c):
            if c < CT - 1:
                eng.wait_ge(chan_mm, (CT - 1) * (group - 4) + c + 1)
            else:
                eng.wait_ge(piece_used, 2 * (group + 1))

        block = es.enter_context(nc.Block())

        @block.sync
        def _(sp):
            def in_piece(i):
                c, k = IN_COLS[i // 2], (i % 2) * 4 * 128
                return ring[:, i % RING, :].rearrange("p (k n) -> p k n", n=512), \
                    w_in[k:k + 512, c:c + 512].rearrange("(k p) n -> p k n", p=128)

            def out_piece(i):
                k = (i - IN_PIECES) * 256
                return ring[:, i % RING, :].rearrange("p (k n) -> p k n", n=D), \
                    w_out[k:k + 256, :].rearrange("(k p) n -> p k n", p=128)

            for k in range(4):
                dst, src = in_piece(0)
                sp.dma_start(dst[:, k], src[:, k]).then_inc(first_in[k], 16)
                sp.dma_start(xt[:, k, :], x_t[k * 128:(k + 1) * 128, :]).then_inc(first_in[k], 16)
            sp.dma_start(xt[:, 4:, :], x_t[512:, :].rearrange("(k p) n -> p k n", p=128)).then_inc(xt_in, 16)
            for i in range(1, MIX_PIECES):
                if i >= RING:
                    sp.wait_ge(piece_used, i - RING + 1)
                dst, src = in_piece(i) if i < IN_PIECES else out_piece(i)
                sp.dma_start(dst, src).then_inc(slot_full[i % RING], 16)

            def expert_piece(j, ea, eb, dst):
                if j < 2 * GU_PIECES:
                    e, k = (ea, eb)[j // GU_PIECES], (j % GU_PIECES) * 128
                    return sp.dma_start(dst.unsqueeze(1), w_gu[bass.ds(e, 1), k:k + 128, :]
                                        .rearrange("e p n -> p e n"))
                i = j - 2 * GU_PIECES
                e, k = (ea, eb)[i // DN_PIECES], (i % DN_PIECES) * 256
                return sp.dma_start(dst.rearrange("p (k n) -> p k n", n=D), w_down[bass.ds(e, 1), k:k + 256, :]
                                    .rearrange("e (k p) n -> p (e k) n", p=128))

            def pair_pieces(first, ea, eb):
                for j in range(PAIR_PIECES):
                    s = loop_slot(j)[0]
                    sp.wait_ge(piece_used, first + (j - RING + 1))
                    expert_piece(j, ea, eb, ring[:, s, :]).then_inc(slot_full[s], 16)

            for j in range(PAIR_PIECES):
                fill = fill_of(MIX_PIECES + j)
                if fill is None:
                    if j == EXTRA_AT:
                        sp.wait_ge(conv_ready, CT)
                        sp.wait_ge(sts_out, 2 * H)
                        sp.wait_ge(states_stored, 16 * (H + 2))
                    expert_piece(j, 0, 1, extra[:, j - EXTRA_AT, :]).then_inc(extra_full[j - EXTRA_AT], 16)
                else:
                    sp.wait_ge(piece_used, piece_of[fill - RING] + 1)
                    s = fill % RING
                    expert_piece(j, 0, 1, ring[:, s, :]).then_inc(slot_full[s], 16)
            with sp.Fori(1, E // 2) as p:
                pair_pieces(MIX_PIECES + PAIR_PIECES * p, 2 * p, 2 * p + 1)
            sp.wait_ge(tab_ready, 1)
            last_pair = sp.value_load(ntab[0:1, 0:1], min_val=E // 2 - 1, max_val=NB // 2 - 1)
            with sp.If(last_pair >= E // 2):
                with sp.Fori(E // 2, last_pair + 1) as p:
                    ea = sp.value_load(etab[0:1, bass.ds(2 * p - E, 1)], min_val=0, max_val=E - 1)
                    eb = sp.value_load(etab[0:1, bass.ds(2 * p - E + 1, 1)], min_val=0, max_val=E - 1)
                    pair_pieces(MIX_PIECES + PAIR_PIECES * p, ea, eb)
            for t in range(NT):
                sp.wait_ge(y_normed, 2 * t + 2)
                sp.dma_start(y_out[t * 128:(t + 1) * 128, :], xy[:, t, :]).then_inc(y_stored, 16)
            sp.wait_ge(y_stored, 16 * NT)
            sp.wait_ge(states_stored, 16 * (H + 2))

        @block.tensor
        def _(pe):
            def piece(i):
                if i:
                    pe.wait_ge(slot_full[i % RING], 16 * (i // RING + (i % RING != 0)))

            def tok_proj(group, banks):
                for hf in range(2):
                    i = 2 * group + hf
                    piece(i)
                    if i == 1:
                        pe.wait_ge(xt_in, 16)
                    w = ring[:, i % RING, :].rearrange("p (k n) -> p k n", n=512)
                    for t in range(NT):
                        for k in range(4):
                            c = 4 * hf + k
                            if i == 0 and t == 0:
                                pe.wait_ge(first_in[k], 32)
                            mm = pe.matmul(bank[banks[t]][:, :], xt[:, c, t * 128:(t + 1) * 128], w[:, k, :],
                                           start=(c == 0), stop=(c == KC - 1))
                        if hf == 1 and t < NT - 1:
                            mm.then_inc(tok_mm, 1)
                    mm.then_inc(piece_used, 1)

            def chan_proj(group):
                for hf in range(2):
                    i = 2 * group + hf
                    piece(i)
                    w = ring[:, i % RING, :].rearrange("p (k n) -> p k n", n=512)
                    for c in range(CT):
                        for k in range(4):
                            kc = 4 * hf + k
                            mm = pe.matmul(bank[3 + c][:, 0:T], w[:, k, c * 128:(c + 1) * 128], xt[:, kc, :],
                                           start=(kc == 0), stop=(kc == KC - 1))
                        if hf == 1 and c < CT - 1:
                            mm.then_inc(chan_mm, 1)
                    mm.then_inc(piece_used, 1)

            tok_proj(0, (0, 1, 2))
            tok_proj(1, (3, 4, 5))
            pe.wait_ge(rotated, 3)
            tok_proj(2, (0, 1, 2))
            pe.wait_ge(rotated, 6)
            tok_proj(3, (3, 4, 5))
            pe.wait_ge(cst_in, 16)
            pe.wait_ge(v_out, 3)
            for n, (src, b) in enumerate(((qo, 0), (qo, 1), (qo, 2), (kk, 7), (kk, 6), (kk, 0))):
                if n == 5:
                    pe.wait_ge(qk_t_out, 1)
                for h in range(H):
                    mm = pe.transpose(bank[b][:, h * 128:(h + 1) * 128],
                                      src[:, n % 3, h * 128:(h + 1) * 128], ident)
                mm.then_inc(qk_t, 1)
            pe.wait_ge(g_out, 3)
            pe.wait_ge(qk_t_out, 5)
            chan_proj(4)
            pe.wait_ge(qk_t_out, 6)
            for h, b in enumerate((0, 1, 2, 7)):
                pe.matmul(bank[b][:, 0:256], kT[:, h, 0:128], qT[:, h, 0:256], start=True, stop=True)
                pe.matmul(bank[b][:, 256:384], kT[:, h, 128:256], qT[:, h, 128:256], start=True, stop=True)
                pe.matmul(bank[b][:, 384:512], kT[:, h, 256:384], qT[:, h, 256:384], start=True, stop=True)\
                    .then_inc(score_mm, 1)
            pe.wait_ge(c_out, CT)
            chan_proj(5)
            pe.wait_ge(score_out, H)
            pe.wait_ge(st_in, 16 * H)
            for h in range(H):
                o = slice(h * 128, (h + 1) * 128)
                s = scores[:, h, :]
                mm = pe.matmul(bank[0][:, o], s[:, 0:128], vv[:, 0, o], start=True, stop=True)
                pe.matmul(bank[1][:, o], s[:, 128:256], vv[:, 0, o], start=True, stop=False)
                pe.matmul(bank[1][:, o], s[:, 256:384], vv[:, 1, o], start=False, stop=True)
                pe.matmul(bank[2][:, o], s[:, 384:512], vv[:, 2, o], start=True, stop=False)
                pe.wait_ge(qm_ready, h + 1)
                for b in range(STREAMS):
                    mm = pe.matmul(bank[2][:, o], qmask[:, b * 128:(b + 1) * 128],
                                   st0[:, h, b * HD:(b + 1) * HD], start=False, stop=(b == STREAMS - 1))
                mm.then_inc(qm_used, 1)
            pe.wait_ge(kd_ready, 1)
            for h in range(H):
                o = slice(h * 128, (h + 1) * 128)
                pe.matmul(bank[7][:, o], kk[:, 0, o], vv[:, 0, o], start=True, stop=False)
                mm = pe.matmul(bank[7][:, o], kk[:, 1, o], vv[:, 1, o], start=False, stop=True)
            mm.then_inc(stp_mm, 1)
            pe.wait_ge(u_out, CT)
            chan_proj(6)
            pe.wait_ge(o_ready_m, NT)
            pe.wait_ge(stp_out, 1)
            for h, b in enumerate((0, 1, 2, 7)):
                for t in range(NT):
                    mm = pe.transpose(bank[b][:, t * 128:(t + 1) * 128], qo[:, t, h * 128:(h + 1) * 128], ident)
                mm.then_inc(o_t, 1)

            def streams(h):
                for n in range(2):
                    i = 2 * h + n
                    pe.wait_ge(vm_ready, i + 1)
                    if i >= 2:
                        pe.wait_ge(sts_out, i - 1)
                    mm = pe.matmul(bank[5 + i % 2][:, :], kk[:, 2, h * 128:(h + 1) * 128],
                                   tmp[:, i % 2, :], start=True, stop=True)
                    mm.then_inc(sts_mm, 1)

            for i in range(OUT_PIECES):
                piece(IN_PIECES + i)
            pe.wait_ge(o_t_out, H)
            mix_banks = ((0, 1), (2, 7), (3, 4))
            tr_banks = ((5, 6), (0, 1), (0, 1))

            def wout(t, n, middle=None):
                for c in range(KC):
                    if (t, n, c) == (0, 0, H):
                        pe.wait_ge(conv_ready, CT)
                    if c == 4 and middle:
                        middle()
                    w = ring[:, (IN_PIECES + c // 2) % RING, :].rearrange("p (k n) -> p k n", n=D)
                    mm = pe.matmul(bank[mix_banks[t][n]][:, :], qkt[:, c, t * 128:(t + 1) * 128],
                                   w[:, c % 2, n * 512:(n + 1) * 512], start=(c == 0), stop=(c == KC - 1))
                    if (t, n) == (NT - 1, 1) and c % 2 == 1:
                        mm.then_inc(piece_used, 1)
                if (t, n) != (NT - 1, 1):
                    mm.then_inc(mix_mm, 1)

            def transpose_h(t):
                pe.wait_ge(h_ready, t + 1)
                if t == 2:
                    pe.wait_ge(h_t_out, 4)
                for c in range(KC):
                    mm = pe.transpose(bank[tr_banks[t][c // 4]][:, (c % 4) * 128:(c % 4 + 1) * 128],
                                      hid[:, t, c * 128:(c + 1) * 128], ident)
                mm.then_inc(h_t, 1)

            def logits(t):
                if t < NT - 1:
                    pe.wait_ge(h_t_out, 2 * (t + 1))
                else:
                    pe.wait_ge(h_t_out, 2 * t + 1)
                    pe.wait_ge(h_t_out_v, 1)
                for c in range(KC):
                    mm = pe.matmul(bank[5][:, t * E:(t + 1) * E], xt[:, c, t * 128:(t + 1) * 128], wr[:, c, :],
                                   start=(c == 0), stop=(c == KC - 1))
                mm.then_inc(logit_mm, 1)

            def ranks(t):
                for q in range(t):
                    pe.matmul(bank[2][:, t * E:(t + 1) * E], ones, msk[:, q, :], start=(q == 0), stop=False)
                mm = pe.matmul(bank[2][:, t * E:(t + 1) * E], cst[:, C_TRI:C_TRI + 128], msk[:, t, :],
                               start=(t == 0), stop=True)
                mm.then_inc(rank_mm, 1)

            def gather_first(t):
                for c in range(KC):
                    mm = pe.matmul(bank[6 + c // 4][:, (c % 4) * 128:(c % 4 + 1) * 128],
                                   hid[:, t, c * 128:(c + 1) * 128], onehot[:, t, :],
                                   start=(t == 0 and c % 4 == 0), stop=(t == NT - 1), skip_group_check=True)
                return mm

            wout(0, 0)
            wout(0, 1)
            streams(0)
            streams(1)
            wout(1, 0)
            wout(1, 1)
            streams(2)
            streams(3)
            pe.wait_ge(router_in, 32)
            pe.wait_ge(sts_out, 2 * H)
            transpose_h(0)
            wout(2, 0)
            logits(0)
            transpose_h(1)
            wout(2, 1, middle=lambda: logits(1))
            pe.wait_ge(mask_ready, 2)
            ranks(0)
            ranks(1)
            pe.wait_ge(first_slots, 1)
            gather_first(0)
            gather_first(1)
            transpose_h(2)
            logits(2)
            pe.wait_ge(mask_ready, 3)
            ranks(2)
            pe.wait_ge(first_slots, 2)
            gather_first(2).then_inc(gathered, 1)

            def count():
                pe.wait_ge(counts_in, 1)
                pe.matmul(bank[4][0:3 * E, 0:1], msk3, ones[:, 0:1], start=True, stop=True).then_inc(cnt_mm, 1)

            def count_before():
                pe.wait_ge(more_ready, 1)
                pe.matmul(bank[4][0:3 * E, 1:2], cst[0:E, C_TRIR:C_TRIR + 96], ovt[0:E, 0:1], start=True, stop=True)
                pe.matmul(bank[4][0:1, 2:3], ovt[0:E, 0:1], ones[0:E, 0:1], start=True, stop=True)\
                    .then_inc(cum_mm, 1)

            def by_expert():
                pe.wait_ge(gates_out, NT)
                pe.wait_ge(xg_ready, 1)
                pe.wait_ge(xg_ready_v, 1)
                for t in range(NT):
                    pe.transpose(bank[6][0:E, t * 128:(t + 1) * 128], rank_all[:, t, 0:E], ident)
                for t in range(NT):
                    mm = pe.transpose(bank[7][0:E, t * 128:(t + 1) * 128], gate_all[:, t, 0:E], ident)
                mm.then_inc(r_t, 1)

            def overflow_tables():
                pe.wait_ge(r_t_out, 2)
                pe.wait_ge(ov_ready, 1)
                oh = ovt[0:E, 6 + MORE:6 + MORE + OV]
                off = ovt[0:E, 6 + MORE + OV:6 + MORE + 2 * OV]
                for t in range(NT):
                    o = slice(t * OV, (t + 1) * OV)
                    pe.matmul(bank[6][:, o], tr[:, 0, t * 128:(t + 1) * 128], oh, start=True, stop=False)
                    pe.matmul(bank[6][:, o], ones[0:E, :], off, start=False, stop=True)
                    pe.matmul(bank[7][:, o], tr[:, 1, t * 128:(t + 1) * 128], oh, start=True, stop=True)
                pe.matmul(bank[7][0:1, NT * OV:(NT + 1) * OV], cst[0:E, C_EC:C_EC + 1], oh, start=True, stop=True)\
                    .then_inc(ov_mm, 1)

            def gather():
                for c in range(KC):
                    for t in range(NT):
                        mm = pe.matmul(bank[6 + c // 4][:, (c % 4) * 128:(c % 4 + 1) * 128],
                                       hid[:, t, c * 128:(c + 1) * 128], onehot[:, t, :],
                                       start=(t == 0), stop=(t == NT - 1))
                mm.then_inc(gathered, 1)

            def gates():
                for t in range(NT):
                    mm = pe.transpose(bank[5][:, t * 128:(t + 1) * 128], onehot_g[:, t, :], ident)
                mm.then_inc(gt_mm, 1)

            def landed(j, p, first):
                if not first:
                    s, before = loop_slot(j)
                    pe.wait_ge(slot_full[s], 32 * p + 16 * (before + 1 - (s == 0)) - 32)
                    return ring[:, s, :]
                fill = fill_of(MIX_PIECES + j)
                if fill is None:
                    pe.wait_ge(extra_full[j - EXTRA_AT], 16)
                    return extra[:, j - EXTRA_AT, :]
                s = fill % RING
                pe.wait_ge(slot_full[s], 16 * (fill // RING + 1 - (s == 0)))
                return ring[:, s, :]

            def transpose_act(a, p):
                pe.wait_ge(act_ready, 2 * p + a + 1)
                for j in range(4):
                    mm = pe.transpose(bank[5][:, j * 128:(j + 1) * 128],
                                      act_h[:, a, j * 128:(j + 1) * 128], ident)
                mm.then_inc(act_tr, 1)

            def gate_up(a, p, first, between):
                for n in range(2):
                    for hf in range(2):
                        pe.matmul(bank[2 * a + n][64 * hf:64 * hf + 64, :], sel[:, a, :],
                                  biasp[:, n * FF + hf * 512:n * FF + (hf + 1) * 512], start=True, stop=False)
                for c in range(KC):
                    if c in between:
                        between[c]()
                    w = landed(GU_PIECES * a + c, p, first)
                    for n in range(2):
                        for hf in range(2):
                            col = n * FF + hf * 512
                            mm = pe.matmul(bank[2 * a + n][64 * hf:64 * hf + 64, :],
                                           xg[:, c, 64 * a:64 * a + 64], w[:, col:col + 512],
                                           start=False, stop=(c == KC - 1))
                    mm.then_inc(piece_used, 1)

            def down(a, p, first, between):
                for hf in range(2):
                    pe.matmul(bank[4][64 * hf:64 * hf + 64, :], sel[:, a, :],
                              biasp[:, 2 * FF + hf * 512:2 * FF + (hf + 1) * 512], start=True, stop=False)
                for c in range(KC):
                    if c in between:
                        between[c]()
                    if c % 2 == 0:
                        w = landed(2 * GU_PIECES + DN_PIECES * a + c // 2, p, first)\
                            .rearrange("p (k n) -> p k n", n=D)
                    for hf in range(2):
                        mm = pe.matmul(bank[4][64 * hf:64 * hf + 64, :],
                                       act_t[:, a, c % 4, 64 * (c // 4):64 * (c // 4) + 64],
                                       w[:, c % 2, hf * 512:(hf + 1) * 512], start=False, stop=(c == KC - 1))
                    if c % 2 == 1:
                        mm.then_inc(piece_used, 1)

            def pair(p, first=False, last=False):
                pe.wait_ge(xg_ready, 2 * p + 1)
                if first:
                    pe.wait_ge(xg_ready_v, 1)
                pe.wait_ge(sel_ready, p + 1)
                gate_up(0, p, first, {})
                if first:
                    pe.wait_ge(onehot_ready, 1)
                    gates()
                    count()
                gate_up(1, p, first, {4: lambda: transpose_act(0, p)} | ({2: count_before, 6: by_expert} if first else {}))
                pe.wait_ge(act_t_ready, 2 * p + 1)
                if first:
                    pe.wait_ge(ov_ready, 1)
                down(0, p, first, {4: lambda: transpose_act(1, p)})
                if first:
                    overflow_tables()
                pe.wait_ge(act_t_ready, 2 * p + 2)
                pe.wait_ge(out_ready, 4 * p + 2)
                down(1, p, first, {})
                pe.wait_ge(out_ready, 4 * p + 4)
                pe.wait_ge(gt_ready, p + 1)
                for i in range(2 * NT):
                    if not last and i >= 3:
                        pe.wait_ge(y_added, 6 * p + i - 2)
                    t, hf = i // 2, i % 2
                    pe.matmul(bank[last_banks[i] if last else 2 + i % 3][:, :], gt[:, t * 128:(t + 1) * 128],
                              oo[:, hf * 512:(hf + 1) * 512], start=True, stop=True).then_inc(comb_mm, 1)
                if not last:
                    if first:
                        pe.wait_ge(tab_ready, 1)
                    pe.wait_ge(onehot_ready, 2 * p + 2)
                    gather()
                    pe.wait_ge(onehot_ready, 2 * p + 3)
                    gates()
                    pe.wait_ge(y_added, 6 * p + 6)

            pair(0, first=True)
            last_pair = pe.value_load(ntab[0:1, 0:1], min_val=E // 2 - 1, max_val=NB // 2 - 1)
            with pe.Fori(1, last_pair) as p:
                pair(p)
            pair(last_pair, last=True)

        @block.scalar
        def _(act):
            act.dma_start(cst[:, :], consts).then_inc(cst_in, 16)
            act.dma_start(mcst[:, :], mconsts).then_inc(mcst_in, 16)
            for n in range(3):
                act.dma_start(bias32[E * n:E * (n + 1), 0:2 * FF], b_gu).then_inc(bias_in, 16)
                act.dma_start(bias32[E * n:E * (n + 1), 2 * FF:], b_down).then_inc(bias_in, 16)
            act.dma_start(chn[:, :, :], chan).then_inc(chan_in, 16)
            act.dma_start(btr[:, :], beta_ret).then_inc(chan_in, 16)
            act.dma_start(cin[:, :, :, :], conv_in).then_inc(chan_in, 16)
            act.dma_start(dm, dmask).then_inc(dm_in, 16)
            for h in range(H):
                act.dma_start(st0[:, h, :].rearrange("p (b e) -> p b e", b=STREAMS),
                              s_ret[:, h].rearrange("b d e -> d b e")).then_inc(st_in, 16)
            act.dma_start(xy[:, :, :], x_tok.rearrange("(t p) n -> p t n", p=128)).then_inc(x_in, 16)
            act.dma_start(wr[:, :, :], w_router.rearrange("(k p) n -> p k n", p=128)).then_inc(router_in, 16)
            act.dma_start(br[:, :], b_router.rearrange("(a n) -> a n", a=1).to_broadcast([128, E]))\
                .then_inc(router_in, 16)

            for t in range(NT):
                tok_done(act, 2, t)
                act.copy(vv[:, t, :], bank[t][:, :]).then_inc(v_out, 1)
            for t in range(NT):
                tok_done(act, 3, t)
                act.activation(gg[:, t, :], bank[3 + t][:, :], ACT.Sigmoid).then_inc(g_sig, 1)
            for n, (dst, b) in enumerate(((qT, 0), (qT, 1), (qT, 2), (kT, 7), (kT, 6), (kT, 0))):
                act.wait_ge(qk_t, n + 1)
                act.copy(dst[:, :, (n % 3) * 128:(n % 3 + 1) * 128],
                         bank[b][:, :].rearrange("p (h n) -> p h n", h=H)).then_inc(qk_t_out, 1)
            act.wait_ge(bias_split, 1)
            for c in range(CT):
                chan_done(act, 4, c)
                act.copy(z[:, c, 0:T], bank[3 + c][:, 0:T]).then_inc(c_out, 1)
            act.wait_ge(score_out, H)
            for n in range(2):
                act.dma_start(lnp[:, n, :], ln1[n:n + 1, :].to_broadcast([128, D])).then_inc(ln1_in, 16)
            act.wait_ge(stp_mm, 1)
            act.wait_ge(qk_t_out, 6)
            act.copy(kk[:, 0, :], bank[7][:, :]).then_inc(stp_out, 1)
            act.wait_ge(stp_out, 1)
            act.dma_start(retp_out.rearrange("h d e -> d h e"), kk[:, 0, :].rearrange("p (h e) -> p h e", h=H))\
                .then_inc(states_stored, 16)
            act.wait_ge(ust_out, 2)
            act.dma_start(conv_out, ust[:, :, :]).then_inc(states_stored, 16)
            act.wait_ge(chan_in, 48)
            for h, b in enumerate((0, 1, 2, 7)):
                act.wait_ge(o_t, h + 1)
                act.activation(qkt[:, h, :], bank[b][:, 0:T], ACT.Copy, scale=btr[:, h:h + 1])\
                    .then_inc(o_t_out, 1)

            def store_states(h):
                act.wait_ge(sts_out, 2 * h + 2)
                act.dma_start(rets_out[:, h].rearrange("b d e -> d b e"),
                              st0[:, h, :].rearrange("p (b e) -> p b e", b=STREAMS)).then_inc(states_stored, 16)

            store_states(0)
            store_states(1)

            def start_y(t):
                act.wait_ge(h_ready, t + 1)
                act.mul(xy[:, t, :], hid[:, t, :], ALPHA).then_inc(y_init, 1)

            for t, banks in enumerate(((5, 6), (0, 1), (0, 1))):
                if t == 0:
                    store_states(2)
                    store_states(3)
                act.wait_ge(h_t, t + 1)
                for n in range(2 if t < NT - 1 else 1):
                    act.copy(xt[:, 4 * n:4 * n + 4, t * 128:(t + 1) * 128],
                             bank[banks[n]][:, :].rearrange("p (k n) -> p k n", k=4)).then_inc(h_t_out, 1)
                start_y(t)
                act.wait_ge(nm_ready, t + 1)
                act.activation(ex[:, t, :], lg[:, t, :], ACT.Exp, bias=nm1[:, t:t + 1]).then_inc(exp_ready, 1)
            for n in range(2):
                act.dma_start(lnp[:, n, :], ln2[n:n + 1, :].to_broadcast([128, D])).then_inc(ln2_in, 16)

            act.wait_ge(gathered, 1)
            act.copy(xg[:, 0:4, :].rearrange("p k n -> p (k n)"), bank[6][:, :]).then_inc(xg_ready, 1)

            def copy_gates(n):
                act.wait_ge(gt_mm, n)
                act.copy(gt[:, :], bank[5][:, 0:T]).then_inc(gt_ready, 1)

            def pair(p, first=False, last=False):
                if first:
                    copy_gates(1)
                for a in range(2):
                    act.wait_ge(gate_ready, 2 * p + a + 1)
                    act.activation(sig[:, :], gate_c[:, :], ACT.Sigmoid, scale=SIG).then_inc(sig_ready, 1)
                    act.wait_ge(act_tr, 2 * p + a + 1)
                    act.copy(act_t[:, a, :, :].rearrange("p k n -> p (k n)"), bank[5][:, :]).then_inc(act_t_ready, 1)
                    if first and a == 0:
                        act.wait_ge(r_t, 1)
                        act.copy(tr[:, 0, :], bank[6][0:E, 0:T]).then_inc(r_t_out, 1)
                        act.copy(tr[:, 1, :], bank[7][0:E, 0:T]).then_inc(r_t_out, 1)
                for a in range(2):
                    act.wait_ge(piece_used, PAIR_PIECES * p + MIX_PIECES + 2 * GU_PIECES + DN_PIECES * (a + 1))
                    for hf in range(2):
                        act.copy(oo[64 * a:64 * a + 64, hf * 512:(hf + 1) * 512],
                                 bank[4][64 * hf:64 * hf + 64, :]).then_inc(out_ready, 1)
                if not last:
                    act.wait_ge(gathered, p + 2)
                    for i in range(2):
                        act.copy(xg[:, 4 * i:4 * i + 4, :].rearrange("p k n -> p (k n)"), bank[6 + i][:, :])\
                            .then_inc(xg_ready, 1)
                    copy_gates(p + 2)

            pair(0, first=True)
            act.wait_ge(tab_ready, 1)
            last_pair = act.value_load(ntab[0:1, 0:1], min_val=E // 2 - 1, max_val=NB // 2 - 1)
            with act.Fori(1, last_pair) as p:
                pair(p)
            pair(last_pair, last=True)
            for t in range(NT):
                act.wait_ge(y_shift, t + 1)
                for n in range(2):
                    b = bank[last_banks[2 * t + n]]
                    act.activation(b[:, :], b[:, :], ACT.Identity, scale=rstd[:, t:t + 1], bias=shift[:, t:t + 1])\
                        .then_inc(y_scaled, 1)

        @block.gpsimd
        def _(pool):
            pool.memset(minus_half[:, :], -0.5).then_inc(pool_ready, 1)
            pool.memset(qmask, 0.0).then_inc(pool_ready, 1)
            pool.wait_ge(pool_ready, 2)

            def v_streams(i):
                if i >= 2:
                    pool.wait_ge(sts_mm, i - 1)
                h, b0 = i // 2, (i % 2) * 4
                pool.tensor_tensor(tmp[:, i % 2, :].rearrange("p (b e) -> p b e", b=4),
                                   vv[:, 2, h * 128:(h + 1) * 128].unsqueeze(1).to_broadcast([128, 4, HD]),
                                   cst[:, C_BM + b0:C_BM + b0 + 4].unsqueeze(2).to_broadcast([128, 4, HD]), ALU.mult)\
                    .then_inc(vm_ready, 1)

            for t in range(NT):
                pool.wait_ge(gn_var, t + 1)
                pool.tensor_tensor(grs[:, t, :], gve[:, t, :], minus_half[:, 0:H], ALU.pow).then_inc(gn_rstd, 1)
            def row_rstd(t):
                pool.wait_ge(ln_var, t + 1)
                n = t % NT
                pool.tensor_tensor(rstd[:, n:n + 1], veps[:, n:n + 1], minus_half[:, 0:1], ALU.pow)\
                    .then_inc(ln_rstd, 1)

            pool.wait_ge(cst_in, 16)
            pool.wait_ge(v_out, NT)
            pool.wait_ge(rotated, 2 * NT)
            for i in range(4):
                v_streams(i)
            v_streams(4)
            v_streams(5)
            row_rstd(0)
            for i in range(6, 2 * H):
                v_streams(i)
            for t in range(1, NT):
                row_rstd(t)
            for t in range(NT):
                row_rstd(NT + t)
            pool.wait_ge(ln2_in, 32)
            for t in range(NT):
                for n in range(2):
                    pool.wait_ge(y_gained, 2 * t + n + 1)
                    o = slice(n * 512, (n + 1) * 512)
                    pool.tensor_tensor(xy[:, t, o], xy[:, t, o], lnp[:, 1, o], ALU.add).then_inc(y_normed, 1)

        @block.vector
        def _(dve):
            chain = [0]

            def link(ins):
                chain[0] += 1
                ins.then_inc(dve_step, 1)
                dve.wait_ge(dve_step, chain[0])

            dve.wait_ge(mcst_in, 16)
            for n, (dst, b) in enumerate(((qo, 0), (qo, 1), (qo, 2), (kk, 3), (kk, 4), (kk, 5))):
                t = n % NT
                cos = mcst[:, M_COS + 64 * t:M_COS + 64 * t + 64].unsqueeze(1)
                sin = mcst[:, M_SIN + 64 * t:M_SIN + 64 * t + 64].unsqueeze(1)
                src = bank[b][:, :].rearrange("p (h s d) -> p h s d", s=2, d=64)
                out = dst[:, t, :].rearrange("p (h s d) -> p h s d", s=2, d=64)
                pc = tmp[:, 0, :].rearrange("p (h s d) -> p h s d", s=2, d=64)
                ps = tmp[:, 1, :].rearrange("p (h s d) -> p h s d", s=2, d=64)
                tok_done(dve, n // NT, t)
                dve.tensor_tensor(tmp[:, 0, :].rearrange("p (a d) -> p a d", d=64),
                                  bank[b][:, :].rearrange("p (a d) -> p a d", d=64),
                                  cos.to_broadcast([128, 8, 64]), ALU.mult)
                for s in range(2):
                    ins = dve.tensor_tensor(ps[:, :, s, :], src[:, :, 1 - s, :], sin.to_broadcast([128, H, 64]), ALU.mult)
                link(ins)
                dve.tensor_tensor(out[:, :, 0, :], pc[:, :, 0, :], ps[:, :, 0, :], ALU.subtract)
                ins = dve.tensor_tensor(out[:, :, 1, :], pc[:, :, 1, :], ps[:, :, 1, :], ALU.add)
                ins.then_inc(rotated, 1)
                dve.wait_ge(rotated, n + 1)
            for t in range(NT):
                dve.wait_ge(g_sig, t + 1)
                dve.tensor_tensor(gg[:, t, :], gg[:, t, :], bank[3 + t][:, :], ALU.mult).then_inc(g_out, 1)
            dve.wait_ge(bias_in, 96)
            link(dve.tensor_copy(biasp[:, :], bias32))
            for n in (1, 2):
                for m in range(n, 3):
                    r = slice(E * m, E * (m + 1))
                    ins = dve.tensor_tensor(bias32[r, :], bias32[r, :], biasp[r, :], ALU.subtract)
                    link(ins)
                    ins = dve.tensor_copy(biasp[r, :], bias32[r, :])
                    if n < m:
                        link(ins)
            ins.then_inc(bias_split, 1)

            dve.wait_ge(dm_in, 16)
            dve.wait_ge(pool_ready, 2)
            for h, b in enumerate((0, 1, 2, 7)):
                dve.wait_ge(score_mm, h + 1)
                dve.tensor_tensor(scores[:, h, :], bank[b][:, :], dm[:, h * 512:(h + 1) * 512], ALU.mult)\
                    .then_inc(score_out, 1)

            def q_slabs(h):
                if h:
                    dve.wait_ge(qm_used, h)
                flat = qmask.rearrange("p (b c) -> p b c", b=STREAMS)
                for_b = bass.AP(tensor=flat.tensor, offset=flat.offset,
                                ap=[list(flat.ap[0]), [128 + STEP, STREAMS], [1, STEP]])
                dve.tensor_tensor(for_b, qT[:, h, SEQ:].rearrange("p (b i) -> p b i", b=STREAMS),
                                  mcst[:, M_QD + h * STEP:M_QD + (h + 1) * STEP].unsqueeze(1)
                                  .to_broadcast([128, STREAMS, STEP]), ALU.mult).then_inc(qm_ready, 1)

            q_slabs(0)
            dve.wait_ge(chan_in, 48)
            dve.wait_ge(bias_split, 1)
            sview = u[:, :, SEQ + 2:].rearrange("p c (b i) -> p c b i", b=STREAMS)
            dve.memset(u[:, :, 0:2], 0.0)
            dve.tensor_copy(sview[:, :, :, 0:2], cin[:, :, :, :])
            for c in range(CT):
                chan_done(dve, 5, c)
                b = bank[3 + c]
                dve.tensor_tensor(u[:, c, 2:SEQ + 2], b[:, 0:SEQ], z[:, c, 0:SEQ], ALU.mult)
                dve.tensor_tensor(sview[:, c, :, 2:], b[:, SEQ:T].rearrange("p (b i) -> p b i", b=STREAMS),
                                  z[:, c, SEQ:T].rearrange("p (b i) -> p b i", b=STREAMS), ALU.mult)\
                    .then_inc(u_out, 1)
            for h in range(1, H):
                q_slabs(h)
            dve.wait_ge(u_out, CT)
            dve.tensor_copy(ust[:, :, 0:2], u[:, :, SEQ:SEQ + 2]).then_inc(ust_out, 1)
            dve.tensor_copy(ust[:, :, 2:].rearrange("p c (b r) -> p c b r", r=2), sview[:, :, :, STEP:])\
                .then_inc(ust_out, 1)
            dve.wait_ge(qk_t_out, 6)
            for t in range(NT):
                ins = dve.tensor_tensor(kk[:, t, :].rearrange("p (h d) -> p h d", h=H),
                                        kk[:, t, :].rearrange("p (h d) -> p h d", h=H),
                                        mcst[:, M_KD + t * H:M_KD + (t + 1) * H].unsqueeze(2)
                                        .to_broadcast([128, H, HD]), ALU.mult)
            ins.then_inc(kd_ready, 1)
            dve.wait_ge(qm_used, H)
            for t in range(NT):
                for h in range(H):
                    ins = dve.bn_stats(gst[:, t, h, :], bank[t][:, h * 128:(h + 1) * 128])
                link(ins)
                for h in range(H):
                    ins = dve.bn_aggr(gmv[:, t, h, :], gst[:, t, h, :])
                link(ins)
                dve.tensor_scalar_add(gve[:, t, :], gmv[:, t, :, 1], EPS).then_inc(gn_var, 1)
            for t in range(NT):
                dve.wait_ge(gn_rstd, t + 1)
                for h in range(H):
                    ins = dve.tensor_scalar(qo[:, t, h * 128:(h + 1) * 128], bank[t][:, h * 128:(h + 1) * 128],
                                            gmv[:, t, h, 0:1], grs[:, t, h:h + 1], ALU.subtract, ALU.mult)
                ins.then_inc(o_free, 1)
                dve.wait_ge(o_free, t + 1)
                dve.tensor_tensor(qo[:, t, :], qo[:, t, :], gg[:, t, :], ALU.mult).then_inc(o_ready_m, 1)
            for c in range(CT):
                ins = dve.tensor_scalar(z[:, c, :], u[:, c, 0:ZW], chn[:, c, 0:1], chn[:, c, 3:4], ALU.mult, ALU.add)
            for tap in (1, 2):
                link(ins)
                for c in range(CT):
                    ins = dve.scalar_tensor_tensor(z[:, c, :], u[:, c, tap:tap + ZW], chn[:, c, tap:tap + 1],
                                             z[:, c, :], ALU.mult, ALU.add)
            link(ins)
            for c in range(CT):
                chan_done(dve, 6, c)
                b = bank[3 + c]
                dve.scalar_tensor_tensor(qkt[:, H + c, 0:SEQ], b[:, 0:SEQ], chn[:, c, 4:5], z[:, c, 0:SEQ],
                                         ALU.mult, ALU.mult)
                zs = z[:, c, SEQ + 2:SEQ + 2 + (STREAMS - 1) * (STEP + 2) + STEP]
                zs = bass.AP(tensor=zs.tensor, offset=zs.offset,
                             ap=[list(zs.ap[0]), [STEP + 2, STREAMS], [1, STEP]])
                dve.scalar_tensor_tensor(qkt[:, H + c, SEQ:T].rearrange("p (b i) -> p b i", b=STREAMS),
                                         b[:, SEQ:T].rearrange("p (b i) -> p b i", b=STREAMS), chn[:, c, 4:5],
                                         zs, ALU.mult, ALU.mult).then_inc(conv_ready, 1)
            dve.wait_ge(st_in, 16 * H)

            def new_states(h):
                for n in range(2):
                    i = 2 * h + n
                    dve.wait_ge(sts_mm, i + 1)
                    o = slice(n * 512, (n + 1) * 512)
                    dve.scalar_tensor_tensor(st0[:, h, o], st0[:, h, o], float(carry[h]), bank[5 + i % 2][:, :],
                                             ALU.mult, ALU.add).then_inc(sts_out, 1)

            def row_stats(t, count):
                link(dve.bn_aggr(mv[:, t, :], stat[:, t, :, :].rearrange("p a b -> p (a b)")))
                dve.tensor_scalar_add(veps[:, t:t + 1], mv[:, t, 1:2], EPS).then_inc(ln_var, 1)

            mix_banks = ((0, 1), (2, 7), (3, 4))

            def residual(t, n):
                b, o = bank[mix_banks[t][n]], slice(n * 512, (n + 1) * 512)
                if (t, n) != (NT - 1, 1):
                    dve.wait_ge(mix_mm, 2 * t + n + 1)
                else:
                    dve.wait_ge(piece_used, MIX_PIECES)
                link(dve.scalar_tensor_tensor(b[:, :], xy[:, t, o], ALPHA, b[:, :], ALU.mult, ALU.add))
                ins = dve.bn_stats(stat[:, t, n, :], b[:, :])
                if n == 1:
                    link(ins)

            def first_norm(t):
                dve.wait_ge(ln_rstd, t + 1)
                for n in range(2):
                    b, o = bank[mix_banks[t][n]], slice(n * 512, (n + 1) * 512)
                    ins = dve.scalar_tensor_tensor(b[:, :], b[:, :], mv[:, t, 0:1], lnp[:, 0, o],
                                                   ALU.subtract, ALU.mult)
                    if n == 1:
                        link(ins)
                for n in range(2):
                    b, o = bank[mix_banks[t][n]], slice(n * 512, (n + 1) * 512)
                    ins = dve.scalar_tensor_tensor(hid[:, t, o], b[:, :], rstd[:, t:t + 1], lnp[:, 1, o],
                                                   ALU.mult, ALU.add)
                ins.then_inc(h_ready, 1)

            iota = cst[:, C_IOTA:C_IOTA + E]

            def choose(t):
                dve.wait_ge(logit_mm, t + 1)
                dve.tensor_tensor(lg[:, t, :], bank[5][:, t * E:(t + 1) * E], br[:, :], ALU.add).then_inc(lg_out, 1)
                dve.wait_ge(lg_out, t + 1)
                link(dve.max(m8[:, t, :], lg[:, t, :]))
                dve.tensor_scalar(nm1[:, t:t + 1], m8[:, t, 0:1], -1.0, None, ALU.mult).then_inc(nm_ready, 1)
                link(dve.max_index(ix8[:, t, :], m8[:, t, :], lg[:, t, :]))
                for k in range(TOPK):
                    ins = dve.tensor_scalar(picks[:, k, :], iota, ix8[:, t, k:k + 1], None, ALU.is_equal)
                link(ins)
                dve.reduce_sum(msk[:, t, :], picks.rearrange("p k e -> p e k"), AXX).then_inc(mask_ready, 1)
                dve.wait_ge(mask_ready, t + 1)

            def softmax(t):
                dve.wait_ge(exp_ready, t + 1)
                link(dve.tensor_tensor(ex[:, t, :], ex[:, t, :], msk[:, t, :], ALU.mult))
                link(dve.reduce_sum(gs[:, t, 0:1], ex[:, t, :], AXX))
                link(dve.reciprocal(gs[:, t, 1:2], gs[:, t, 0:1]))
                dve.tensor_scalar(gate_all[:, t, 0:E], ex[:, t, :], gs[:, t, 1:2], None, ALU.mult)\
                    .then_inc(gates_out, 1)

            def first_pair_slots(t0, t1):
                dve.wait_ge(rank_mm, t1)
                n = t1 - t0
                link(dve.scalar_tensor_tensor(rank_all[:, t0:t1, 0:E], bank[2][:, t0 * E:t1 * E]
                                              .rearrange("p (t e) -> p t e", t=n), 1.0, msk[:, t0:t1, :],
                                              ALU.add, ALU.mult))
                dve.tensor_tensor(onehot[:, t0:t1, :].rearrange("p t (a s) -> p t a s", a=2),
                                  cst[:, C_IOTA + 1:C_IOTA + 1 + SLOTS].unsqueeze(1).unsqueeze(1)
                                  .to_broadcast([128, n, 2, SLOTS]),
                                  rank_all[:, t0:t1, 0:2].unsqueeze(3).to_broadcast([128, n, 2, SLOTS]),
                                  ALU.is_equal).then_inc(first_slots, 1)

            def rows_of(n):
                dve.tensor_copy(sel[:, :, :], sel_all[:, bass.ds(2 * n, 2)].unsqueeze(2)
                                .to_broadcast([3 * E, 2, SLOTS])).then_inc(sel_ready, 1)

            dve.wait_ge(x_in, 16)
            dve.wait_ge(ln1_in, 32)
            dve.wait_ge(router_in, 32)
            new_states(0)
            new_states(1)
            residual(0, 0)
            residual(0, 1)
            row_stats(0, 1)
            first_norm(0)
            new_states(2)
            new_states(3)
            link(dve.memset(ones, 1.0))
            residual(1, 0)
            residual(1, 1)
            row_stats(1, 2)
            first_norm(1)
            choose(0)
            residual(2, 0)
            choose(1)
            residual(2, 1)
            row_stats(2, 3)
            dve.wait_ge(conv_ready, CT)
            first_pair_slots(0, 2)
            first_norm(2)
            dve.wait_ge(h_t, NT)
            dve.tensor_copy(xt[:, 4:8, 256:384], bank[1][:, :].rearrange("p (k n) -> p k n", k=4)).then_inc(h_t_out_v, 1)
            link(dve.tensor_copy(sel_all[:, 0:E], cst[0:3 * E, C_SEL:C_SEL + E]))
            rows_of(0)
            choose(2)
            first_pair_slots(2, 3)
            dve.wait_ge(gathered, 1)
            dve.tensor_copy(xg[:, 4:8, :].rearrange("p k n -> p (k n)"), bank[7][:, :]).then_inc(xg_ready_v, 1)
            for t in range(NT):
                softmax(t)
            m3 = msk3.rearrange("p (r e) -> p r e", r=3)
            link(dve.tensor_tensor(msk3[:, 0:E], msk[:, 0, :], msk[:, 1, :], ALU.add))
            link(dve.tensor_tensor(msk3[:, 0:E], msk3[:, 0:E], msk[:, 2, :], ALU.add))
            dve.tensor_copy(m3[:, 1:3, :], m3[:, 0:1, :].to_broadcast([128, 2, E])).then_inc(counts_in, 1)

            more, cnt, cum, end = (ovt[:, n:n + 1] for n in range(4))
            thr_w = ovt[:, 6:6 + MORE]
            oh, off, ws, wq = (ovt[:, 6 + MORE + n * OV:6 + MORE + (n + 1) * OV] for n in range(4))
            rows = slice(0, 3 * E)

            def more_blocks():
                dve.wait_ge(cnt_mm, 1)
                link(dve.tensor_copy(cnt, bank[4][rows, 0:1]))
                link(dve.tensor_scalar(thr_w, cst[rows, C_THR:C_THR + MORE], cnt, None, ALU.is_lt))
                dve.reduce_sum(more, thr_w, AXX).then_inc(more_ready, 1)

            def overflow_blocks():
                dve.wait_ge(cum_mm, 1)
                dve.tensor_copy(half[:, 0:1], bank[4][0:1, 2:3])
                link(dve.tensor_copy(cum, bank[4][rows, 1:2]))
                link(dve.tensor_tensor(end, cum, more, ALU.add))
                orow = cst[rows, C_OV:C_OV + OV]
                dve.tensor_scalar(ws, orow, cum, None, ALU.is_ge)
                link(dve.tensor_scalar(wq, orow, end, None, ALU.is_lt))
                link(dve.tensor_tensor(oh, ws, wq, ALU.mult))
                link(dve.tensor_scalar(ws, orow, cum, -float(SLOTS), ALU.subtract, ALU.mult))
                link(dve.scalar_tensor_tensor(off, ws, -float(SLOTS), oh, ALU.add, ALU.mult))
                dve.tensor_copy(sel_all[:, E:E + OV], oh).then_inc(ov_ready, 1)
                link(dve.tensor_scalar(half[:, 2:], cst[0:1, C_HALF:C_W], half[:, 0:1], None, ALU.is_lt))
                link(dve.reduce_sum(half[:, 1:2], half[:, 2:], AXX))
                dve.tensor_scalar(ntab[:, 0:1], half[:, 1:2], float(E // 2 - 1), None, ALU.add)

            def tables():
                dve.wait_ge(ov_mm, 1)
                dve.tensor_copy(etab[:, :], bank[7][0:1, NT * OV:(NT + 1) * OV])
                dve.tensor_copy(rank_all[:, :, E:E + OV], bank[6][:, 0:NT * OV].rearrange("p (t o) -> p t o", t=NT))
                dve.tensor_copy(gate_all[:, :, E:E + OV], bank[7][:, 0:NT * OV].rearrange("p (t o) -> p t o", t=NT))\
                    .then_inc(tab_ready, 1)
                dve.wait_ge(tab_ready, 1)

            def gated_slots(n):
                og4 = onehot_g[:, :, :].rearrange("p t (a s) -> p t a s", a=2)
                gate = gate_all[:, :, bass.ds(2 * n, 2)].unsqueeze(3).to_broadcast([128, NT, 2, SLOTS])
                dve.tensor_tensor(og4, onehot[:, :, :].rearrange("p t (a s) -> p t a s", a=2), gate, ALU.mult)\
                    .then_inc(onehot_ready, 1)

            def slots_of(n):
                iota4 = cst[:, C_IOTA + 1:C_IOTA + 1 + SLOTS].unsqueeze(1).unsqueeze(1).to_broadcast([128, NT, 2, SLOTS])
                rank = rank_all[:, :, bass.ds(2 * n, 2)].unsqueeze(3).to_broadcast([128, NT, 2, SLOTS])
                dve.tensor_tensor(onehot[:, :, :].rearrange("p t (a s) -> p t a s", a=2), iota4, rank, ALU.is_equal)\
                    .then_inc(onehot_ready, 1)
                dve.wait_ge(onehot_ready, 2 * n)
                gated_slots(n)

            def pair(p, first=False, last=False):
                if first:
                    dve.wait_ge(gates_out, NT)
                    dve.wait_ge(first_slots, 2)
                    gated_slots(0)
                for a in range(2):
                    n = 2 * p + a + 1
                    dve.wait_ge(piece_used, PAIR_PIECES * p + MIX_PIECES + GU_PIECES * (a + 1))
                    dve.tensor_scalar(gate_c[:, :], bank[2 * a][:, :], LIMIT, None, ALU.min).then_inc(gate_ready, 1)
                    dve.tensor_scalar(up_c[:, :], bank[2 * a + 1][:, :], LIMIT, -LIMIT, ALU.min, ALU.max)\
                        .then_inc(up_ready, 1)
                    dve.wait_ge(gate_ready, n)
                    dve.wait_ge(up_ready, n)
                    dve.scalar_tensor_tensor(up_c[:, :], up_c[:, :], 1.0, gate_c[:, :], ALU.add, ALU.mult)\
                        .then_inc(prod_ready, 1)
                    dve.wait_ge(prod_ready, n)
                    dve.wait_ge(sig_ready, n)
                    dve.tensor_tensor(act_h[:, a, :], up_c[:, :], sig[:, :], ALU.mult).then_inc(act_ready, 1)
                    if a == 0:
                        if first:
                            more_blocks()
                            overflow_blocks()
                        if not last:
                            dve.wait_ge(gt_mm, p + 1)
                            slots_of(p + 1)
                if first:
                    tables()
                    dve.wait_ge(y_init, NT)
                for i in range(2 * NT):
                    t, hf = i // 2, i % 2
                    o = slice(hf * 512, (hf + 1) * 512)
                    dve.wait_ge(comb_mm, 6 * p + i + 1)
                    if not last:
                        dve.tensor_tensor(xy[:, t, o], xy[:, t, o], bank[2 + i % 3][:, :], ALU.add)\
                            .then_inc(y_added, 1)
                        continue
                    b = bank[last_banks[i]]
                    link(dve.tensor_tensor(b[:, :], xy[:, t, o], b[:, :], ALU.add))
                    ins = dve.bn_stats(stat[:, t, hf, :], b[:, :])
                    if hf == 1:
                        link(ins)
                        row_stats(t, NT + t + 1)
                if not last:
                    rows_of(p + 1)

            pair(0, first=True)
            last_pair = dve.value_load(ntab[0:1, 0:1], min_val=E // 2 - 1, max_val=NB // 2 - 1)
            with dve.Fori(1, last_pair) as p:
                pair(p)
            pair(last_pair, last=True)
            for t in range(NT):
                dve.wait_ge(ln_rstd, NT + t + 1)
                dve.scalar_tensor_tensor(shift[:, t:t + 1], mv[:, t, 0:1], -1.0, rstd[:, t:t + 1], ALU.mult, ALU.mult)\
                    .then_inc(y_shift, 1)
            dve.wait_ge(ln2_in, 32)
            for t in range(NT):
                for n in range(2):
                    o = slice(n * 512, (n + 1) * 512)
                    dve.wait_ge(y_scaled, 2 * t + n + 1)
                    dve.tensor_tensor(xy[:, t, o], bank[last_banks[2 * t + n]][:, :], lnp[:, 0, o], ALU.mult)\
                        .then_inc(y_gained, 1)


def kernel(x_prompt, x_sample, state_retention, state_conv, w_in, beta_ret, beta_conv, conv_w, conv_b, w_out,
           ln1_g, ln1_b, w_router, b_router, w_gu, b_gu, w_down, b_down, ln2_g, ln2_b):
    import concourse.bacc as bacc
    from concourse.bass_utils import run_bass_kernel_spmd

    a = np.ascontiguousarray
    x = np.concatenate([np.asarray(x_prompt).reshape(SEQ, D), np.asarray(x_sample).reshape(STREAMS * STEP, D)])
    by_channel = [np.asarray(v).reshape(CT, 128).T for v in
                  (*np.asarray(conv_w)[0], np.asarray(conv_b)[0], np.asarray(beta_conv)[0])]
    c, m, dmask, _ = constants()
    arrays = {
        "x_tok": a(x), "x_t": a(x.T), "s_ret": a(np.asarray(state_retention)[0]),
        "conv_in": a(np.asarray(state_conv)[0].reshape(STREAMS, 2, CT, 128).transpose(3, 2, 0, 1)),
        "w_in": a(np.asarray(w_in)[0]), "w_out": a(np.asarray(w_out)[0]),
        "chan": a(np.stack(by_channel, axis=-1)), "beta_ret": a(np.asarray(beta_ret).reshape(H, 128).T),
        "ln1": a(np.concatenate([np.asarray(ln1_g), np.asarray(ln1_b)])),
        "ln2": a(np.concatenate([np.asarray(ln2_g), np.asarray(ln2_b)])),
        "w_router": a(np.asarray(w_router)[0]), "b_router": a(np.asarray(b_router)[0]),
        "w_gu": a(np.asarray(w_gu)[0]), "b_gu": a(np.asarray(b_gu)[0]),
        "w_down": a(np.asarray(w_down)[0]), "b_down": a(np.asarray(b_down)[0]),
        "consts": c, "mconsts": m, "dmask": dmask,
    }
    outs = {"y": (T, D), "retp": (H, HD, HD), "rets": (STREAMS, H, HD, HD), "convs": (128, CT, 2 + 2 * STREAMS)}
    nc = bacc.Bacc("TRN2", target_bir_lowering=False, num_devices=1, dynamic_dma_scratch_size=1024)
    args = [nc.dram_tensor(n, v.shape, F32, kind="ExternalInput").ap() for n, v in arrays.items()]
    args += [nc.dram_tensor(n, s, F32, kind="ExternalOutput").ap() for n, s in outs.items()]
    build(nc, *args)
    r = run_bass_kernel_spmd(nc, [arrays], core_ids=[0]).results[0]
    y, conv = r["y"], r["convs"].transpose(2, 1, 0).reshape(2 + 2 * STREAMS, DC)
    return (y[:SEQ].reshape(1, SEQ, D), y[SEQ:].reshape(STREAMS, STEP, D),
            r["retp"].reshape(1, 1, H, HD, HD), a(conv[:2]).reshape(1, 1, 2, DC),
            r["rets"].reshape(1, STREAMS, H, HD, HD), a(conv[2:]).reshape(1, STREAMS, 2, DC))
```

```python
import math
from contextlib import ExitStack

import numpy as np

import concourse.bass as bass
from concourse import mybir

F32 = mybir.dt.float32
BF16 = mybir.dt.bfloat16
F32R = mybir.dt.float32r
I32 = mybir.dt.int32
U32 = mybir.dt.uint32
ALU = mybir.AluOpType
ACT = mybir.ActivationFunctionType
AXX = mybir.AxisListType.X

D = 1024
KC = D // 128
SEQ, STREAMS, STEP = 256, 8, 16
PAST = 128
T = SEQ + STREAMS * STEP
NT = T // 128
PT = SEQ // 128
DR = 512
H, HD = 4, 128
DC = 512
CT = DC // 128
TAPS = 3
E = 32
TOPK = 4
FF = 1024
LIMIT = 7.0
SIG = 1.702
EPS = 1e-5
ALPHA = 2.0 ** 0.25
SLOTS = 64
MORE = T // SLOTS - 1
OV = (T * TOPK) // (SLOTS + 1) + 1
OV += -OV % 4
NB = E + OV
RING = 12
WIDE = 16
PW = 2048
IN_COLS = [0, DR, 2 * DR, 3 * DR, 4 * DR + DC, 4 * DR + 2 * DC, 4 * DR]
IN_PIECES = 2 * len(IN_COLS)
PARTS = 2
OUT_PIECES = 4
MIX_PIECES = IN_PIECES + OUT_PIECES
GU_PIECES, DN_PIECES = 8, 4
PAIR_PIECES = 2 * (GU_PIECES + DN_PIECES)
SIDE = tuple(range(WIDE, WIDE + 4))
FIRST_FILLS = PAIR_PIECES - len(SIDE)
OLD_ROOMS = WIDE - RING + 1
CW = SEQ + 2 + STREAMS * (STEP + 2)
ZW = CW - 2

C_ID, C_IOTA, C_TRI, C_BM, C_TRIR, C_EC, C_SEL, C_OV, C_THR, C_HALF = np.cumsum(
    [0, 128, 1 + SLOTS, 128, 8, 96, 1, 32, OV, MORE]).tolist()
C_W = C_HALF + OV // 4
M_COS, M_SIN, M_QD, M_KD = np.cumsum([0, NT * 64, NT * 64, H * STEP]).tolist()
M_W = M_KD + NT * H


def constants():
    c = np.zeros((128, C_W), np.float32)
    p = np.arange(128)
    c[:, C_ID:C_ID + 128] = np.eye(128)
    c[:, C_IOTA:C_IOTA + 1 + SLOTS] = np.arange(1 + SLOTS)
    c[:, C_TRI:C_TRI + 128] = p[:, None] < p[None, :]
    c[:, C_BM:C_BM + 8] = (p[:, None] // STEP) == np.arange(8)
    c[:, C_TRIR:C_TRIR + 96] = p[:, None] < (np.arange(96) % E)[None, :]
    c[:, C_EC] = p
    c[:, C_SEL:C_SEL + E] = (p[:, None] % E) == np.arange(E)
    c[:, C_OV:C_OV + OV] = np.arange(OV)
    c[:, C_THR:C_THR + MORE] = SLOTS * np.arange(1, MORE + 1)
    c[:, C_HALF:] = 4 * np.arange(OV // 4)
    gamma = 1.0 - 2.0 ** (-5.0 - np.arange(H))
    lg = np.log(gamma)
    m = np.zeros((128, M_W), np.float32)
    pos = np.stack([p, 128 + p, PAST + p % STEP], 1).astype(np.float32)
    inv = (np.float32(10000.0) ** (-np.arange(0, HD, 2, dtype=np.float32) / np.float32(HD))).astype(np.float32)
    ang = (pos[:, :, None] * inv).astype(np.float32)
    m[:, M_COS:M_SIN] = np.cos(ang).reshape(128, -1)
    m[:, M_SIN:M_QD] = np.sin(ang).reshape(128, -1)
    m[:, M_QD:M_KD] = np.exp(lg[:, None] * (np.arange(STEP) + 1.0)).reshape(1, -1)
    scale = HD ** -0.5
    left = np.stack([255 - p, 127 - p, STEP - 1 - p % STEP], 1)
    m[:, M_KD:] = (np.exp(lg * left[:, :, None]) * scale).reshape(128, -1)
    d = np.zeros((128, H, 4, 128))
    diff = p[None, :] - p[:, None]
    same = (p[None, :] // STEP) == (p[:, None] // STEP)
    for h in range(H):
        near = np.where(diff >= 0, np.exp(lg[h] * np.maximum(diff, 0)), 0.0)
        d[:, h, 0] = near
        d[:, h, 1] = np.exp(lg[h] * (diff + 128))
        d[:, h, 2] = near
        d[:, h, 3] = near * same
    return c, m, (d * scale).reshape(128, H * 512).astype(np.float32), np.exp(lg * STEP)


def build(nc, x_tok, x_t, s_ret, conv_in, w_in, w_out, chan, beta_ret, ln1, ln2, w_router, b_router,
          w_gu, b_gu, w_down, b_down, consts, mconsts, dmask, y_out, retp_out, rets_out, conv_out):
    carry = constants()[3]
    es = ExitStack()
    with es:
        def sb(name, shape, dt=F32, ctx=es):
            return ctx.enter_context(nc.sbuf_tensor(name, shape, dt))

        def sem(name):
            return es.enter_context(nc.semaphore(name))

        with ExitStack() as early:
            w_parts = sb("w_parts", [128, PARTS, 2, PW // 2], F32R, early)
        ring = sb("ring", [128, RING, PW])
        with ExitStack() as early:
            x_lo = sb("x_lo", [128, KC, T], F32R, early)
        xy = sb("xy", [128, NT, D])
        hid = sb("hid", [128, NT, D])
        lnp = sb("lnp", [128, 2, D])
        cst = sb("cst", [128, C_W])
        biasp = sb("biasp", [3 * E, 3 * D], BF16)
        sel_all = sb("sel_all", [3 * E, NB])
        rank_all = sb("rank_all", [128, NT, NB])
        gate_all = sb("gate_all", [128, NT, NB])
        etab = sb("etab", [1, OV], I32)
        ntab = sb("ntab", [1, 2], I32)
        stat = sb("stat", [128, NT, 2, 6])
        mv = sb("mv", [128, NT, 2])
        veps = sb("veps", [128, NT])
        rstd = sb("rstd", [128, NT])
        shift = sb("shift", [128, NT])
        minus_half = sb("minus_half", [128, 16])
        ident = cst[:, C_ID:C_ID + 128]

        bank = [es.enter_context(nc.psum_tensor(f"bank{i}", [128, 512], F32)) for i in range(8)]

        mix = ExitStack()
        with ExitStack() as early:
            x_hi = sb("x_hi", [128, KC, T], F32R, early)
        xt = sb("xt", [128, KC, T], ctx=mix)
        qkt = sb("qkt", [128, 2 * H, T], ctx=mix)
        qo = sb("qo", [128, NT, DR], ctx=mix)
        gg = sb("gg", [128, NT, DR], ctx=mix)
        vv = sb("vv", [128, NT, DR], ctx=mix)
        zu = sb("zu", [128, CT * (ZW + CW)], ctx=mix)
        st0 = sb("st0", [128, H, STREAMS * HD], ctx=mix)
        kk = sb("kk", [128, NT, DR], ctx=mix)
        tmp = sb("tmp", [128, 2, DR], ctx=mix)
        mcst = sb("mcst", [128, M_W], ctx=mix)
        z = zu[:, 0:CT * ZW].rearrange("p (c n) -> p c n", c=CT)
        u = zu[:, CT * ZW:].rearrange("p (c n) -> p c n", c=CT)
        bias32 = zu[0:3 * E, 0:3 * D]
        chn = sb("chn", [128, CT, 5], ctx=mix)
        btr = sb("btr", [128, H], ctx=mix)
        cin = sb("cin", [128, CT, STREAMS, 2], ctx=mix)
        ust = sb("ust", [128, CT, 2 + 2 * STREAMS], ctx=mix)
        gst = sb("gst", [128, NT, H, 6], ctx=mix)
        gmv = sb("gmv", [128, NT, H, 2], ctx=mix)
        gve = sb("gve", [128, NT, H], ctx=mix)
        grs = sb("grs", [128, NT, H], ctx=mix)
        wr = sb("wr", [128, KC, E], ctx=mix)
        br = sb("br", [128, E], ctx=mix)
        nm1 = sb("nm1", [128, NT], ctx=mix)
        ix8 = sb("ix8", [128, NT, 8], U32, ctx=mix)
        gs = sb("gs", [128, NT, 2], ctx=mix)
        m8 = sb("m8", [128, NT, 8], ctx=mix)
        room = vv[:, :, :].rearrange("p a b -> p (a b)")
        cut = [0]

        def carve(words):
            cut[0] += words
            assert cut[0] <= NT * DR
            return room[:, cut[0] - words:cut[0]]

        ones = carve(128)
        lg, ex, msk = (carve(NT * E).rearrange("p (t e) -> p t e", t=NT) for _ in range(3))
        msk3 = carve(3 * E)
        picks = carve(TOPK * E).rearrange("p (k e) -> p k e", k=TOPK)
        tr = carve(2 * T)[0:E, :].rearrange("p (r t) -> p r t", r=2)
        ovt = carve(6 + MORE + 4 * OV)[0:3 * E, :]
        half = carve(2 + OV // 4)[0:1, :]
        hflat = hid[:, :, :].rearrange("p a b -> p (a b)")
        x_landed = hflat.rearrange("p (k t) -> p k t", k=KC)
        scores = hflat[:, 0:H * 512].rearrange("p (h n) -> p h n", h=H)
        qmask = hflat[:, H * 512:H * 512 + 1024]
        dm = lnp[:, :, :].rearrange("p a b -> p (a b)")
        qT, kT = qkt[:, 0:H, :], qkt[:, H:2 * H, :]
        mix.close()

        act_h = sb("act_h", [128, 2, 512])
        act_t = sb("act_t", [128, 2, 4, 128])
        oo = sb("oo", [128, D])
        xg = sb("xg", [128, KC, 128])
        onehot = sb("onehot", [128, NT, 128])
        onehot_g = sb("onehot_g", [128, NT, 128])
        gt = sb("gt", [128, T])
        sel = sb("sel", [3 * E, 2, SLOTS], BF16)
        gate_c = sb("gate_c", [128, 512])
        up_c = sb("up_c", [128, 512])
        sig = sb("sig", [128, 512])
        with ExitStack() as gap:
            over_q = sb("over_q", [128, PW], ctx=gap)
            sb("kept_free", [128, (KC + 2 * H) * T + 2 * NT * DR - (4 * D + 3 * T + SLOTS + 3 * 512) - PW], ctx=gap)
            sb("kept_router", [128, NT * DR], ctx=gap)
            old_rooms = sb("old_rooms", [128, OLD_ROOMS, PW], ctx=gap)
        in_lnp = lnp[:, :, :].rearrange("p a b -> p (a b)")
        in_xy = xy[:, :, :].rearrange("p a b -> p (a b)")[:, 0:PW]
        side = dict(zip(SIDE, (over_q[:, :], old_rooms[:, OLD_ROOMS - 1, :], in_lnp, in_xy)))

        slot_full = [sem(f"slot_full{i}") for i in range(WIDE)]
        side_full = {j: sem(f"side_full{j}") for j in SIDE}
        piece_used = sem("piece_used")
        first_in = [sem(f"first_in{k}") for k in range(4)]
        xt_in, x_in, cst_in, mcst_in, dm_in, st_in = map(sem, ("xt_in", "x_in", "cst_in", "mcst_in", "dm_in", "st_in"))
        chan_in, bias_in, ln1_in, ln2_in, router_in = map(sem, ("chan_in", "bias_in", "ln1_in", "ln2_in", "router_in"))
        y_stored, retp_stored, conv_stored = map(sem, ("y_stored", "retp_stored", "conv_stored"))
        rets_stored = [sem(f"rets_stored{h}") for h in range(H)]
        dve_step = sem("dve_step")
        pool_ready = sem("pool_ready")
        bias_split = sem("bias_split")
        x_hi_ready, x_lo_ready, w_hi_ready, w_lo_ready, half_used = map(
            sem, ("x_hi_ready", "x_lo_ready", "w_hi_ready", "w_lo_ready", "half_used"))
        tok_mm, rotated, v_out, g_sig, g_out = map(sem, ("tok_mm", "rotated", "v_out", "g_sig", "g_out"))
        qk_t, qk_t_out = sem("qk_t"), sem("qk_t_out")
        score_mm, score_out = sem("score_mm"), sem("score_out")
        qm_ready, qm_used = sem("qm_ready"), sem("qm_used")
        chan_mm, c_out, u_out, conv_ready = map(sem, ("chan_mm", "c_out", "u_out", "conv_ready"))
        gn_var, gn_rstd, o_free, o_ready_m = map(sem, ("gn_var", "gn_rstd", "o_free", "o_ready_m"))
        kd_ready, stp_mm, stp_out = sem("kd_ready"), sem("stp_mm"), sem("stp_out")
        vm_ready, sts_mm, sts_out = sem("vm_ready"), sem("sts_mm"), sem("sts_out")
        ust_out = sem("ust_out")
        o_t, o_t_out = sem("o_t"), sem("o_t_out")
        mix_mm, res_out, ln_var, ln_rstd, h_ready = map(sem, ("mix_mm", "res_out", "ln_var", "ln_rstd", "h_ready"))
        h_t, h_t_out, h_t_out_v = sem("h_t"), sem("h_t_out"), sem("h_t_out_v")
        logit_mm, lg_out, nm_ready, exp_ready, mask_ready = map(
            sem, ("logit_mm", "lg_out", "nm_ready", "exp_ready", "mask_ready"))
        rank_mm, rank_out, r_t, r_t_out = map(sem, ("rank_mm", "rank_out", "r_t", "r_t_out"))
        first_slots, xg_ready_v, gates_out = sem("first_slots"), sem("xg_ready_v"), sem("gates_out")
        counts_in, cnt_mm, more_ready, cum_mm, ov_ready, ov_mm, tab_ready = map(
            sem, ("counts_in", "cnt_mm", "more_ready", "cum_mm", "ov_ready", "ov_mm", "tab_ready"))
        onehot_ready, sel_ready = sem("onehot_ready"), sem("sel_ready")
        gathered_low = sem("gathered_low")
        gathered, xg_ready, gt_mm, gt_ready = map(sem, ("gathered", "xg_ready", "gt_mm", "gt_ready"))
        gate_ready, sig_ready, up_ready, prod_ready, act_ready = map(
            sem, ("gate_ready", "sig_ready", "up_ready", "prod_ready", "act_ready"))
        act_tr, act_t_ready, out_ready = map(sem, ("act_tr", "act_t_ready", "out_ready"))
        comb_mm, y_added = sem("comb_mm"), sem("y_added")
        out_ready_v, y_shift, y_scaled, y_gained = map(sem, ("out_ready_v", "y_shift", "y_scaled", "y_gained"))
        y_pool, y_centred, y_done = map(sem, ("y_pool", "y_centred", "y_done"))

        last_banks = (6, 7, 0, 1, 2, 3)

        def mixer_room(i):
            return PARTS + (i - MIX_PIECES) % (RING - PARTS)

        def room(n):
            return ring[:, n, :] if n < RING else old_rooms[:, n - RING, :]

        mixer_fills = [sum(mixer_room(i) == n for i in range(1, MIX_PIECES)) if n < RING else 0 for n in range(WIDE)]

        def first_fill(j):
            return None if j in SIDE else j - sum(n < j for n in SIDE)

        piece_of = {first_fill(j): j for j in range(PAIR_PIECES) if first_fill(j) is not None}

        def pair_fill(j, odd):
            return FIRST_FILLS + (0 if odd else PAIR_PIECES) + j

        def mixer_wait(eng, i):
            n = mixer_room(i)
            eng.wait_ge(slot_full[n], 16 * sum(mixer_room(m) == n for m in range(1, i + 1)))

        def tok_done(eng, group, t):
            if t < NT - 1:
                eng.wait_ge(tok_mm, (NT - 1) * group + t + 1)
            else:
                eng.wait_ge(piece_used, 2 * (group + 1))

        def chan_done(eng, group, c):
            if c < CT - 1:
                eng.wait_ge(chan_mm, (CT - 1) * (group - 4) + c + 1)
            else:
                eng.wait_ge(piece_used, 2 * (group + 1))

        block = es.enter_context(nc.Block())

        @block.sync
        def _(sp):
            def in_piece(i):
                c, k = IN_COLS[i // 2], (i % 2) * 4 * 128
                return room(mixer_room(i)).rearrange("p (k n) -> p k n", n=512), \
                    w_in[k:k + 512, c:c + 512].rearrange("(k p) n -> p k n", p=128)

            def out_piece(i):
                k = (i - IN_PIECES) * 256
                return room(mixer_room(i)).rearrange("p (k n) -> p k n", n=D), \
                    w_out[k:k + 256, :].rearrange("(k p) n -> p k n", p=128)

            for k in range(4):
                dst, src = in_piece(0)
                sp.dma_start(dst[:, k], src[:, k]).then_inc(first_in[k], 16)
            sp.dma_start(x_landed[:, 4:, :], x_t[512:, :].rearrange("(k p) n -> p k n", p=128)).then_inc(xt_in, 16)
            for i in range(1, MIX_PIECES):
                if i >= RING - PARTS:
                    sp.wait_ge(piece_used, i - (RING - PARTS) + 1)
                dst, src = in_piece(i) if i < IN_PIECES else out_piece(i)
                sp.dma_start(dst, src).then_inc(slot_full[mixer_room(i)], 16)

            def expert_piece(j, ea, eb, dst):
                if j < 2 * GU_PIECES:
                    e, k = (ea, eb)[j // GU_PIECES], (j % GU_PIECES) * 128
                    return sp.dma_start(dst.unsqueeze(1), w_gu[bass.ds(e, 1), k:k + 128, :]
                                        .rearrange("e p n -> p e n"))
                i = j - 2 * GU_PIECES
                e, k = (ea, eb)[i // DN_PIECES], (i % DN_PIECES) * 256
                return sp.dma_start(dst.rearrange("p (k n) -> p k n", n=D), w_down[bass.ds(e, 1), k:k + 256, :]
                                    .rearrange("e (k p) n -> p (e k) n", p=128))

            def pair_pieces(first, ea, eb, odd, second=False):
                for j in range(PAIR_PIECES):
                    g = pair_fill(j, odd)
                    if second and j < WIDE:
                        sp.wait_ge(piece_used, MIX_PIECES + piece_of.get(g - WIDE, g - WIDE + len(SIDE)) + 1)
                    else:
                        sp.wait_ge(piece_used, first + (j - WIDE + 1))
                    expert_piece(j, ea, eb, room(g % WIDE)).then_inc(slot_full[g % WIDE], 16)

            free = RING - OUT_PIECES
            order = [*range(PARTS, free), *range(PARTS), SIDE[0], *range(RING, WIDE), SIDE[1], *range(free, RING), *SIDE[2:],
                     *range(SIDE[-1] + 1, PAIR_PIECES)]
            for j in order:
                if j == SIDE[0]:
                    sp.wait_ge(o_t_out, H)
                elif j == RING:
                    sp.wait_ge(conv_ready, CT)
                elif j == RING + 1:
                    sp.wait_ge(rets_stored[0], 16)
                elif j == RING + 2:
                    sp.wait_ge(rets_stored[1], 16)
                    sp.wait_ge(rets_stored[2], 16)
                elif j == RING + 3:
                    sp.wait_ge(rets_stored[3], 16)
                    sp.wait_ge(retp_stored, 16)
                elif j == SIDE[2]:
                    sp.wait_ge(h_ready, 2 * NT)
                g = first_fill(j)
                if g is None:
                    expert_piece(j, 0, 1, side[j]).then_inc(side_full[j], 16)
                    continue
                if g < PARTS:
                    sp.wait_ge(piece_used, IN_PIECES)
                elif g < RING:
                    sp.wait_ge(piece_used, MIX_PIECES - RING + g + 1)
                elif g >= WIDE:
                    sp.wait_ge(piece_used, MIX_PIECES + piece_of[g - WIDE] + 1)
                expert_piece(j, 0, 1, room(g % WIDE)).then_inc(slot_full[g % WIDE], 16)
            pair_pieces(MIX_PIECES + PAIR_PIECES, 2, 3, odd=True, second=True)
            with sp.Fori(1, E // 4) as i:
                for a in range(2):
                    pair_pieces(MIX_PIECES + PAIR_PIECES * (2 * i + a), 4 * i + 2 * a, 4 * i + 2 * a + 1, odd=a == 1)
            sp.wait_ge(tab_ready, 1)
            twos = sp.value_load(ntab[0:1, 0:1], min_val=E // 4 - 1, max_val=NB // 4 - 1)
            with sp.If(twos >= E // 4):
                with sp.Fori(E // 4, twos + 1) as i:
                    for a in range(2):
                        ea, eb = (sp.value_load(etab[0:1, bass.ds(4 * i + (2 * a + b - E), 1)], min_val=0, max_val=E - 1)
                                  for b in range(2))
                        pair_pieces(MIX_PIECES + PAIR_PIECES * (2 * i + a), ea, eb, odd=a == 1)
            for t in (1, 0, 2):
                for n in range(2):
                    if t == 0:
                        sp.wait_ge(y_pool, n + 1)
                    else:
                        sp.wait_ge(y_done, 2 * (t - 1) + n + 1)
                    o = slice(n * 512, (n + 1) * 512)
                    sp.dma_start(y_out[t * 128:(t + 1) * 128, o], xy[:, t, o]).then_inc(y_stored, 16)
            sp.wait_ge(y_stored, 16 * 2 * NT)
            sp.wait_ge(conv_stored, 16)

        @block.tensor
        def _(pe):
            def products(i, h, tiles, operands, bank_free=None):
                parts = w_parts[:, (2 * i + h) % PARTS, :, :].rearrange("p s (k n) -> p s k n", n=512)
                for n, (x, w) in enumerate(((x_hi, 0), (x_lo, 0), (x_hi, 1))):
                    if n == 0:
                        if i == 1:
                            pe.wait_ge(x_hi_ready, KC)
                        pe.wait_ge(w_hi_ready, 2 * i + h - 1)
                    elif n == 1:
                        if i == 1:
                            pe.wait_ge(x_lo_ready, KC)
                    else:
                        pe.wait_ge(w_lo_ready, 2 * i + h - 1)
                    for t in range(tiles):
                        if bank_free and n == h == i % 2 == 0:
                            bank_free(t)
                        for k in range(2):
                            c = 4 * (i % 2) + 2 * h + k
                            out, lhs, rhs = operands(t, x[:, c, :], parts[:, w, k, :])
                            mm = pe.matmul(out, lhs, rhs, start=(n == 0 and c == 0), stop=(n == 2 and c == KC - 1))
                        if n == 2:
                            yield t, mm

            def proj(group, tiles, done, operands, bank_free=None):
                for i in (2 * group, 2 * group + 1):
                    for h in range(2):
                        for t, mm in products(i, h, tiles, operands, bank_free):
                            if t == tiles - 1:
                                mm.then_inc(piece_used if h else half_used, 1)
                            elif h and i % 2:
                                mm.then_inc(done, 1)

            def tok_proj(group, banks):
                proj(group, NT, tok_mm, lambda t, x, w: (bank[banks[t]][:, :], x[:, t * 128:(t + 1) * 128], w))

            def chan_proj(group, bank_free=None):
                proj(group, CT, chan_mm, lambda c, x, w: (bank[3 + c][:, 0:T], w[:, c * 128:(c + 1) * 128], x),
                     bank_free)

            w = room(mixer_room(0)).rearrange("p (k n) -> p k n", n=512)
            for k in range(4):
                pe.wait_ge(first_in[k], 32)
                for t in range(NT):
                    mm = pe.matmul(bank[t][:, :], x_landed[:, k, t * 128:(t + 1) * 128], w[:, k, :],
                                   start=(k == 0), stop=False)
            mm.then_inc(piece_used, 1)
            for h in range(2):
                for t, mm in products(1, h, NT, lambda t, x, w: (bank[t][:, :], x[:, t * 128:(t + 1) * 128], w)):
                    if t == NT - 1:
                        mm.then_inc(piece_used if h else half_used, 1)
                    elif h:
                        mm.then_inc(tok_mm, 1)
            tok_proj(1, (3, 4, 5))
            pe.wait_ge(rotated, 3)
            tok_proj(2, (0, 1, 2))
            pe.wait_ge(rotated, 6)
            tok_proj(3, (3, 4, 5))
            pe.wait_ge(cst_in, 16)
            pe.wait_ge(v_out, 3)
            for n, (src, b) in enumerate(((qo, 0), (qo, 1), (qo, 2), (kk, 7), (kk, 6), (kk, 0))):
                if n == 5:
                    pe.wait_ge(qk_t_out, 1)
                for h in range(H):
                    mm = pe.transpose(bank[b][:, h * 128:(h + 1) * 128],
                                      src[:, n % 3, h * 128:(h + 1) * 128], ident)
                mm.then_inc(qk_t, 1)

            def banks_after_g(c):
                if c < NT:
                    pe.wait_ge(g_out, c + 1)
                else:
                    pe.wait_ge(qk_t_out, 5)

            chan_proj(4, banks_after_g)
            pe.wait_ge(qk_t_out, 6)
            for h, b in enumerate((0, 1, 2, 7)):
                pe.matmul(bank[b][:, 0:256], kT[:, h, 0:128], qT[:, h, 0:256], start=True, stop=True)
                pe.matmul(bank[b][:, 256:384], kT[:, h, 128:256], qT[:, h, 128:256], start=True, stop=True)
                pe.matmul(bank[b][:, 384:512], kT[:, h, 256:384], qT[:, h, 256:384], start=True, stop=True)\
                    .then_inc(score_mm, 1)
            pe.wait_ge(c_out, CT)
            chan_proj(5)
            pe.wait_ge(score_out, H)
            pe.wait_ge(st_in, 16 * H)
            for h in range(H):
                o = slice(h * 128, (h + 1) * 128)
                s = scores[:, h, :]
                mm = pe.matmul(bank[0][:, o], s[:, 0:128], vv[:, 0, o], start=True, stop=True)
                pe.matmul(bank[1][:, o], s[:, 128:256], vv[:, 0, o], start=True, stop=False)
                pe.matmul(bank[1][:, o], s[:, 256:384], vv[:, 1, o], start=False, stop=True)
                pe.matmul(bank[2][:, o], s[:, 384:512], vv[:, 2, o], start=True, stop=False)
                pe.wait_ge(qm_ready, h + 1)
                for b in range(STREAMS):
                    mm = pe.matmul(bank[2][:, o], qmask[:, b * 128:(b + 1) * 128],
                                   st0[:, h, b * HD:(b + 1) * HD], start=False, stop=(b == STREAMS - 1))
                mm.then_inc(qm_used, 1)
            pe.wait_ge(kd_ready, 1)
            for h in range(H):
                o = slice(h * 128, (h + 1) * 128)
                pe.matmul(bank[7][:, o], kk[:, 0, o], vv[:, 0, o], start=True, stop=False)
                mm = pe.matmul(bank[7][:, o], kk[:, 1, o], vv[:, 1, o], start=False, stop=True)
            mm.then_inc(stp_mm, 1)
            pe.wait_ge(u_out, CT)
            chan_proj(6)
            pe.wait_ge(o_ready_m, NT)
            pe.wait_ge(stp_out, 1)
            for h, b in enumerate((0, 1, 2, 7)):
                for t in range(NT):
                    mm = pe.transpose(bank[b][:, t * 128:(t + 1) * 128], qo[:, t, h * 128:(h + 1) * 128], ident)
                mm.then_inc(o_t, 1)

            def streams(h):
                for n in range(2):
                    i = 2 * h + n
                    pe.wait_ge(vm_ready, i + 1)
                    if i >= 2:
                        pe.wait_ge(sts_out, i - 1)
                    mm = pe.matmul(bank[5 + i % 2][:, :], kk[:, 2, h * 128:(h + 1) * 128],
                                   tmp[:, i % 2, :], start=True, stop=True)
                    mm.then_inc(sts_mm, 1)

            for i in range(OUT_PIECES):
                mixer_wait(pe, IN_PIECES + i)
            mix_banks = ((0, 1), (2, 7), (3, 4))
            tr_banks = (0, 1)

            def wout(t, n, between={}):
                for c in range(KC):
                    if (t, n) == (0, 0) and c < H:
                        pe.wait_ge(o_t_out, c + 1)
                    if (t, n, c) == (0, 0, H):
                        pe.wait_ge(conv_ready, CT)
                    if c in between:
                        between[c]()
                    w = room(mixer_room(IN_PIECES + c // 2)).rearrange("p (k n) -> p k n", n=D)
                    mm = pe.matmul(bank[mix_banks[t][n]][:, :], qkt[:, c, t * 128:(t + 1) * 128],
                                   w[:, c % 2, n * 512:(n + 1) * 512], start=(c == 0), stop=(c == KC - 1))
                    if (t, n) == (NT - 1, 1) and c % 2 == 1:
                        mm.then_inc(piece_used, 1)
                if (t, n) != (NT - 1, 1):
                    mm.then_inc(mix_mm, 1)

            def transpose_h(t):
                if t:
                    pe.wait_ge(h_t_out, 2 * t)
                for c in range(KC):
                    if c % 4 == 0:
                        pe.wait_ge(h_ready, 2 * t + c // 4 + 1)
                    mm = pe.transpose(bank[tr_banks[c // 4]][:, (c % 4) * 128:(c % 4 + 1) * 128],
                                      hid[:, t, c * 128:(c + 1) * 128], ident)
                    if c % 4 == 3:
                        mm.then_inc(h_t, 1)

            def logits(t):
                if t < NT - 1:
                    pe.wait_ge(h_t_out, 2 * (t + 1))
                else:
                    pe.wait_ge(h_t_out, 2 * t + 1)
                    pe.wait_ge(h_t_out_v, 1)
                for c in range(KC):
                    mm = pe.matmul(bank[5][:, t * E:(t + 1) * E], xt[:, c, t * 128:(t + 1) * 128], wr[:, c, :],
                                   start=(c == 0), stop=(c == KC - 1))
                mm.then_inc(logit_mm, 1)

            def ranks(t):
                for q in range(t):
                    pe.matmul(bank[2][:, t * E:(t + 1) * E], ones, msk[:, q, :], start=(q == 0), stop=False)
                mm = pe.matmul(bank[2][:, t * E:(t + 1) * E], cst[:, C_TRI:C_TRI + 128], msk[:, t, :],
                               start=(t == 0), stop=True)
                mm.then_inc(rank_mm, 1)

            def early_ranks():
                pe.wait_ge(mask_ready, 2)
                ranks(0)
                ranks(1)

            def gather_first(t, chunks):
                for c in chunks:
                    mm = pe.matmul(bank[6 + c // 4][:, (c % 4) * 128:(c % 4 + 1) * 128],
                                   hid[:, t, c * 128:(c + 1) * 128], onehot[:, t, :],
                                   start=(t == 0 and c % 4 == 0), stop=(t == NT - 1), skip_group_check=True)
                    if t == NT - 1 and c % 4 == 3:
                        mm.then_inc(gathered if c == KC - 1 else gathered_low, 1)

            def gate_up_bias(a):
                for n in range(2):
                    for hf in range(2):
                        pe.matmul(bank[2 * a + n][64 * hf:64 * hf + 64, :], sel[:, a, :],
                                  biasp[:, n * FF + hf * 512:n * FF + (hf + 1) * 512], start=True, stop=False)

            wout(0, 0)
            streams(0)
            wout(0, 1)
            streams(1)
            wout(1, 0)
            streams(2)
            wout(1, 1)
            streams(3)
            pe.wait_ge(router_in, 32)
            transpose_h(0)
            wout(2, 0)
            pe.wait_ge(sts_out, 2 * H)
            logits(0)
            transpose_h(1)
            wout(2, 1, {2: lambda: logits(1), 6: early_ranks})
            pe.wait_ge(first_slots, 1)
            gather_first(0, range(KC))
            gather_first(1, range(5))
            transpose_h(2)
            gather_first(1, range(5, 7))
            logits(2)
            gather_first(1, range(7, KC))
            pe.wait_ge(sel_ready, 1)
            gate_up_bias(0)
            pe.wait_ge(mask_ready, 3)
            ranks(2)
            pe.wait_ge(first_slots, 2)
            gather_first(2, range(KC))

            def count():
                pe.wait_ge(counts_in, 1)
                pe.matmul(bank[4][0:3 * E, 0:1], msk3, ones[:, 0:1], start=True, stop=True).then_inc(cnt_mm, 1)

            def count_before():
                pe.wait_ge(more_ready, 1)
                pe.matmul(bank[4][0:3 * E, 1:2], cst[0:E, C_TRIR:C_TRIR + 96], ovt[0:E, 0:1], start=True, stop=True)
                pe.matmul(bank[4][0:1, 2:3], ovt[0:E, 0:1], ones[0:E, 0:1], start=True, stop=True)\
                    .then_inc(cum_mm, 1)

            def by_expert():
                pe.wait_ge(gates_out, NT)
                pe.wait_ge(xg_ready, 1)
                pe.wait_ge(xg_ready_v, 1)
                for t in range(NT):
                    pe.transpose(bank[6][0:E, t * 128:(t + 1) * 128], rank_all[:, t, 0:E], ident)
                for t in range(NT):
                    mm = pe.transpose(bank[7][0:E, t * 128:(t + 1) * 128], gate_all[:, t, 0:E], ident)
                mm.then_inc(r_t, 1)

            def overflow_tables():
                pe.wait_ge(r_t_out, 2)
                pe.wait_ge(ov_ready, 1)
                oh = ovt[0:E, 6 + MORE:6 + MORE + OV]
                off = ovt[0:E, 6 + MORE + OV:6 + MORE + 2 * OV]
                for t in range(NT):
                    o = slice(t * OV, (t + 1) * OV)
                    pe.matmul(bank[6][:, o], tr[:, 0, t * 128:(t + 1) * 128], oh, start=True, stop=False)
                    pe.matmul(bank[6][:, o], ones[0:E, :], off, start=False, stop=True)
                    pe.matmul(bank[7][:, o], tr[:, 1, t * 128:(t + 1) * 128], oh, start=True, stop=True)
                pe.matmul(bank[7][0:1, NT * OV:(NT + 1) * OV], cst[0:E, C_EC:C_EC + 1], oh, start=True, stop=True)\
                    .then_inc(ov_mm, 1)

            def gather():
                for c in range(KC):
                    for t in range(NT):
                        mm = pe.matmul(bank[6 + c // 4][:, (c % 4) * 128:(c % 4 + 1) * 128],
                                       hid[:, t, c * 128:(c + 1) * 128], onehot[:, t, :],
                                       start=(t == 0), stop=(t == NT - 1))
                mm.then_inc(gathered, 1)

            def gates():
                for t in range(NT):
                    mm = pe.transpose(bank[5][:, t * 128:(t + 1) * 128], onehot_g[:, t, :], ident)
                mm.then_inc(gt_mm, 1)

            def landed(j, turn, odd):
                if turn is None:
                    g = first_fill(j)
                    if g is None:
                        pe.wait_ge(side_full[j], 16)
                        return side[j]
                    pe.wait_ge(slot_full[g % WIDE], 16 * (mixer_fills[g % WIDE] + g // WIDE + 1))
                else:
                    g = pair_fill(j, odd)
                    pe.wait_ge(slot_full[g % WIDE], 16 * (2 * PAIR_PIECES // WIDE) * turn
                               + 16 * (mixer_fills[g % WIDE] + g // WIDE + 1))
                return room(g % WIDE)

            def transpose_act(a, p):
                pe.wait_ge(act_ready, 2 * p + a + 1)
                for j in range(4):
                    mm = pe.transpose(bank[5][:, j * 128:(j + 1) * 128],
                                      act_h[:, a, j * 128:(j + 1) * 128], ident)
                mm.then_inc(act_tr, 1)

            def gate_up(a, turn, odd, between):
                for c in range(KC):
                    if c in between:
                        between[c]()
                    w = landed(GU_PIECES * a + c, turn, odd)
                    for n in range(2):
                        for hf in range(2):
                            col = n * FF + hf * 512
                            mm = pe.matmul(bank[2 * a + n][64 * hf:64 * hf + 64, :],
                                           xg[:, c, 64 * a:64 * a + 64], w[:, col:col + 512],
                                           start=False, stop=(c == KC - 1))
                    mm.then_inc(piece_used, 1)

            def down(a, turn, odd, between):
                for hf in range(2):
                    pe.matmul(bank[4][64 * hf:64 * hf + 64, :], sel[:, a, :],
                              biasp[:, 2 * FF + hf * 512:2 * FF + (hf + 1) * 512], start=True, stop=False)
                for c in range(KC):
                    if c in between:
                        between[c]()
                    if c % 2 == 0:
                        w = landed(2 * GU_PIECES + DN_PIECES * a + c // 2, turn, odd)\
                            .rearrange("p (k n) -> p k n", n=D)
                    for hf in range(2):
                        mm = pe.matmul(bank[4][64 * hf:64 * hf + 64, :],
                                       act_t[:, a, c % 4, 64 * (c // 4):64 * (c // 4) + 64],
                                       w[:, c % 2, hf * 512:(hf + 1) * 512], start=False, stop=(c == KC - 1))
                    if c % 2 == 1:
                        mm.then_inc(piece_used, 1)

            def sums_so_far(*halves):
                for i in halves:
                    pe.matmul(bank[last_banks[i]][:, :], ident, xy[:, i // 2, (i % 2) * 512:(i % 2 + 1) * 512],
                              start=True, stop=False)

            def upper_tokens():
                pe.wait_ge(xg_ready_v, 1)

            def pair(turn, odd=False, last=False):
                first = turn is None
                p = 0 if first else 2 * turn + (1 if odd else 2)
                if not first:
                    pe.wait_ge(sel_ready, p + 1)
                    gate_up_bias(0)
                pe.wait_ge(xg_ready, 2 * p + 1)
                gate_up(0, turn, odd, {4: upper_tokens} if first else {})
                if first:
                    pe.wait_ge(onehot_ready, 1)
                    gates()
                    count()
                if not first:
                    pe.wait_ge(y_added, 6 * p)
                if last:
                    sums_so_far(0, 1)
                gate_up_bias(1)
                gate_up(1, turn, odd, {4: lambda: transpose_act(0, p)} | ({2: count_before, 6: by_expert} if first else {}))
                pe.wait_ge(act_t_ready, 2 * p + 1)
                if first:
                    pe.wait_ge(ov_ready, 1)
                if last:
                    sums_so_far(2, 3)
                down(0, turn, odd, {4: lambda: transpose_act(1, p)})
                if last:
                    sums_so_far(4, 5)
                if first:
                    overflow_tables()
                pe.wait_ge(act_t_ready, 2 * p + 2)
                pe.wait_ge(out_ready, 4 * p + 2)
                down(1, turn, odd, {})
                if not last:
                    if first:
                        pe.wait_ge(tab_ready, 1)
                    pe.wait_ge(onehot_ready, 2 * p + 2)
                    gather()
                pe.wait_ge(gt_ready, p + 1)
                if last:
                    pe.wait_ge(out_ready, 4 * p + 3)
                    for i in (0, 1, 2, 3, 4, 5):
                        if i == 1:
                            pe.wait_ge(out_ready_v, 1)
                        t, hf = i // 2, i % 2
                        pe.matmul(bank[last_banks[i]][:, :], gt[:, t * 128:(t + 1) * 128],
                                  oo[:, hf * 512:(hf + 1) * 512], start=False, stop=True).then_inc(comb_mm, 1)
                    return
                pe.wait_ge(out_ready, 4 * p + 4)
                for i in range(2 * NT):
                    if i >= 3:
                        pe.wait_ge(y_added, 6 * p + i - 2)
                    t, hf = i // 2, i % 2
                    pe.matmul(bank[2 + i % 3][:, :], gt[:, t * 128:(t + 1) * 128],
                              oo[:, hf * 512:(hf + 1) * 512], start=True, stop=True).then_inc(comb_mm, 1)
                pe.wait_ge(onehot_ready, 2 * p + 3)
                gates()

            pair(None)
            twos = pe.value_load(ntab[0:1, 0:1], min_val=E // 4 - 1, max_val=NB // 4 - 1)
            with pe.Fori(0, twos) as turn:
                pair(turn, odd=True)
                pair(turn, odd=False)
            pair(twos, odd=True, last=True)

        @block.scalar
        def _(act):
            for k in range(4):
                act.dma_start(x_landed[:, k, :], x_t[k * 128:(k + 1) * 128, :]).then_inc(first_in[k], 16)
            act.dma_start(cst[:, :], consts).then_inc(cst_in, 16)
            act.dma_start(mcst[:, :], mconsts).then_inc(mcst_in, 16)

            def load_biases(n):
                act.dma_start(bias32[E * n:E * (n + 1), 0:2 * FF], b_gu).then_inc(bias_in, 16)
                act.dma_start(bias32[E * n:E * (n + 1), 2 * FF:], b_down).then_inc(bias_in, 16)

            def load_states(*heads):
                for h in heads:
                    act.dma_start(st0[:, h, :].rearrange("p (b e) -> p b e", b=STREAMS),
                                  s_ret[:, h].rearrange("b d e -> d b e")).then_inc(st_in, 16)

            def high_parts(*halves):
                for n in halves:
                    i, h = n // 2, n % 2
                    mixer_wait(act, i)
                    if i > 1:
                        if h:
                            act.wait_ge(piece_used, i)
                        else:
                            act.wait_ge(half_used, i - 1)
                        act.wait_ge(w_lo_ready, n - 3)
                    w = room(mixer_room(i))[:, h * (PW // 2):(h + 1) * (PW // 2)]
                    act.copy(w_parts[:, n % PARTS, 0, :], w).then_inc(w_hi_ready, 1)

            for k in range(KC):
                if k < 4:
                    act.wait_ge(first_in[k], 32)
                elif k == 4:
                    act.wait_ge(xt_in, 16)
                act.copy(x_hi[:, k, :], x_landed[:, k, :]).then_inc(x_hi_ready, 1)
            high_parts(2, 3)
            load_biases(0)
            high_parts(4)
            load_biases(1)
            high_parts(5)
            load_biases(2)
            high_parts(6)
            act.dma_start(chn[:, :, :], chan).then_inc(chan_in, 16)
            act.dma_start(btr[:, :], beta_ret).then_inc(chan_in, 16)
            high_parts(7)
            act.dma_start(cin[:, :, :, :], conv_in).then_inc(chan_in, 16)
            act.dma_start(dm, dmask).then_inc(dm_in, 16)
            high_parts(8)
            load_states(0, 1)
            high_parts(9)
            load_states(2, 3)
            high_parts(10)
            act.dma_start(wr[:, :, :], w_router.rearrange("(k p) n -> p k n", p=128)).then_inc(router_in, 16)
            act.dma_start(br[:, :], b_router.rearrange("(a n) -> a n", a=1).to_broadcast([128, E]))\
                .then_inc(router_in, 16)
            high_parts(11, 12, 13)
            for t in range(NT):
                tok_done(act, 2, t)
                act.copy(vv[:, t, :], bank[t][:, :]).then_inc(v_out, 1)
            high_parts(14, 15, 16)
            for t in range(NT):
                tok_done(act, 3, t)
                act.activation(gg[:, t, :], bank[3 + t][:, :], ACT.Sigmoid).then_inc(g_sig, 1)
            for n, (dst, b) in enumerate(((qT, 0), (qT, 1), (qT, 2), (kT, 7), (kT, 6), (kT, 0))):
                act.wait_ge(qk_t, n + 1)
                act.copy(dst[:, :, (n % 3) * 128:(n % 3 + 1) * 128],
                         bank[b][:, :].rearrange("p (h n) -> p h n", h=H)).then_inc(qk_t_out, 1)
                if n == 2:
                    high_parts(17)
            high_parts(18, 19, 20)
            act.wait_ge(bias_split, 1)
            for c in range(CT):
                chan_done(act, 4, c)
                act.copy(z[:, c, 0:T], bank[3 + c][:, 0:T]).then_inc(c_out, 1)
            high_parts(*range(21, 26))
            act.wait_ge(score_out, H)
            for n in range(2):
                act.dma_start(lnp[:, n, :], ln1[n:n + 1, :].to_broadcast([128, D])).then_inc(ln1_in, 16)
            act.wait_ge(stp_mm, 1)
            act.wait_ge(qk_t_out, 6)
            act.copy(kk[:, 0, :], bank[7][:, :]).then_inc(stp_out, 1)
            act.wait_ge(stp_out, 1)
            act.dma_start(retp_out.rearrange("h d e -> d h e"), kk[:, 0, :].rearrange("p (h e) -> p h e", h=H))\
                .then_inc(retp_stored, 16)
            act.wait_ge(ust_out, 2)
            act.dma_start(conv_out, ust[:, :, :]).then_inc(conv_stored, 16)
            high_parts(26, 27)
            act.wait_ge(piece_used, IN_PIECES)
            act.dma_start(xy[:, :, :], x_tok.rearrange("(t p) n -> p t n", p=128)).then_inc(x_in, 16)
            act.wait_ge(chan_in, 48)
            for h, b in enumerate((0, 1, 2, 7)):
                act.wait_ge(o_t, h + 1)
                act.activation(qkt[:, h, :], bank[b][:, 0:T], ACT.Copy, scale=btr[:, h:h + 1])\
                    .then_inc(o_t_out, 1)

            def store_states(h):
                act.wait_ge(sts_out, 2 * h + 2)
                act.dma_start(rets_out[:, h].rearrange("b d e -> d b e"),
                              st0[:, h, :].rearrange("p (b e) -> p b e", b=STREAMS)).then_inc(rets_stored[h], 16)

            store_states(0)
            store_states(1)

            for t in range(NT):
                if t == 0:
                    store_states(2)
                    store_states(3)
                for n in range(2 if t < NT - 1 else 1):
                    act.wait_ge(h_t, 2 * t + n + 1)
                    act.copy(xt[:, 4 * n:4 * n + 4, t * 128:(t + 1) * 128],
                             bank[n][:, :].rearrange("p (k n) -> p k n", k=4)).then_inc(h_t_out, 1)
                act.wait_ge(nm_ready, t + 1)
                act.activation(ex[:, t, :], lg[:, t, :], ACT.Exp, bias=nm1[:, t:t + 1]).then_inc(exp_ready, 1)

            act.wait_ge(gathered_low, 1)
            act.copy(xg[:, 0:4, :].rearrange("p k n -> p (k n)"), bank[6][:, :]).then_inc(xg_ready, 1)

            def copy_gates(n):
                act.wait_ge(gt_mm, n)
                act.copy(gt[:, :], bank[5][:, 0:T]).then_inc(gt_ready, 1)

            def pair(p, first=False, last=False):
                if first:
                    copy_gates(1)
                for a in range(2):
                    act.wait_ge(gate_ready, 2 * p + a + 1)
                    act.activation(sig[:, :], gate_c[:, :], ACT.Sigmoid, scale=SIG).then_inc(sig_ready, 1)
                    act.wait_ge(act_tr, 2 * p + a + 1)
                    act.copy(act_t[:, a, :, :].rearrange("p k n -> p (k n)"), bank[5][:, :]).then_inc(act_t_ready, 1)
                    if first and a == 0:
                        act.wait_ge(r_t, 1)
                        act.copy(tr[:, 0, :], bank[6][0:E, 0:T]).then_inc(r_t_out, 1)
                        act.copy(tr[:, 1, :], bank[7][0:E, 0:T]).then_inc(r_t_out, 1)
                for a in range(2):
                    act.wait_ge(piece_used, PAIR_PIECES * p + MIX_PIECES + 2 * GU_PIECES + DN_PIECES * (a + 1))
                    if first and a == 0:
                        for n in range(2):
                            act.dma_start(lnp[:, n, :], ln2[n:n + 1, :].to_broadcast([128, D])).then_inc(ln2_in, 16)
                    for hf in range(1 if last and a else 2):
                        act.copy(oo[64 * a:64 * a + 64, hf * 512:(hf + 1) * 512],
                                 bank[4][64 * hf:64 * hf + 64, :]).then_inc(out_ready, 1)
                if not last:
                    act.wait_ge(gathered, p + 2)
                    for i in range(2):
                        act.copy(xg[:, 4 * i:4 * i + 4, :].rearrange("p k n -> p (k n)"), bank[6 + i][:, :])\
                            .then_inc(xg_ready, 1)
                    copy_gates(p + 2)

            pair(0, first=True)
            act.wait_ge(tab_ready, 1)
            last_pair = 2 * act.value_load(ntab[0:1, 0:1], min_val=E // 4 - 1, max_val=NB // 4 - 1) + 1
            with act.Fori(1, last_pair) as p:
                pair(p)
            pair(last_pair, last=True)
            act.wait_ge(y_shift, 1)
            for n in range(2):
                act.activation(xy[:, 0, n * 512:(n + 1) * 512], bank[last_banks[n]][:, :], ACT.Identity,
                               scale=rstd[:, 0:1], bias=shift[:, 0:1]).then_inc(y_scaled, 1)

        @block.gpsimd
        def _(pool):
            pool.memset(minus_half[:, :], -0.5).then_inc(pool_ready, 1)
            pool.wait_ge(pool_ready, 1)

            def low_parts(*halves):
                for n in halves:
                    i, h = n // 2, n % 2
                    pool.wait_ge(w_hi_ready, n - 1)
                    w = room(mixer_room(i))[:, h * (PW // 2):(h + 1) * (PW // 2)]
                    pool.tensor_tensor(w_parts[:, n % PARTS, 1, :], w, w_parts[:, n % PARTS, 0, :].bitcast(F32),
                                       ALU.subtract).then_inc(w_lo_ready, 1)

            low_parts(*range(2, 8))
            pool.wait_ge(x_lo_ready, KC)
            pool.wait_ge(piece_used, 1)
            pool.memset(qmask, 0.0).then_inc(pool_ready, 1)
            low_parts(*range(8, 26))
            for t in range(NT):
                pool.wait_ge(gn_var, t + 1)
                pool.tensor_tensor(grs[:, t, :], gve[:, t, :], minus_half[:, 0:H], ALU.pow).then_inc(gn_rstd, 1)
            low_parts(26, 27)

            def v_streams(i):
                if i >= 2:
                    pool.wait_ge(sts_mm, i - 1)
                h, b0 = i // 2, (i % 2) * 4
                pool.tensor_tensor(tmp[:, i % 2, :].rearrange("p (b e) -> p b e", b=4),
                                   vv[:, 2, h * 128:(h + 1) * 128].unsqueeze(1).to_broadcast([128, 4, HD]),
                                   cst[:, C_BM + b0:C_BM + b0 + 4].unsqueeze(2).to_broadcast([128, 4, HD]), ALU.mult)\
                    .then_inc(vm_ready, 1)

            def row_rstd(t):
                pool.wait_ge(ln_var, t + 1)
                n = t % NT
                pool.tensor_tensor(rstd[:, n:n + 1], veps[:, n:n + 1], minus_half[:, 0:1], ALU.pow)\
                    .then_inc(ln_rstd, 1)

            pool.wait_ge(cst_in, 16)
            pool.wait_ge(v_out, NT)
            pool.wait_ge(rotated, 2 * NT)
            for i in range(4):
                v_streams(i)
            row_rstd(0)
            for i in range(4, 2 * H):
                v_streams(i)
            for t in range(1, NT):
                row_rstd(t)
            row_rstd(NT)
            pool.wait_ge(ln2_in, 32)
            for n in range(2):
                pool.wait_ge(y_scaled, n + 1)
                o = slice(n * 512, (n + 1) * 512)
                pool.tensor_tensor(xy[:, 0, o], xy[:, 0, o], lnp[:, 0, o], ALU.mult).then_inc(y_gained, 1)
                row_rstd(NT + 1 + n)
                pool.wait_ge(y_gained, n + 1)
                pool.tensor_tensor(xy[:, 0, o], xy[:, 0, o], lnp[:, 1, o], ALU.add).then_inc(y_pool, 1)

        @block.vector
        def _(dve):
            chain = [0]

            def link(ins):
                chain[0] += 1
                ins.then_inc(dve_step, 1)
                dve.wait_ge(dve_step, chain[0])

            for k in range(KC):
                dve.wait_ge(x_hi_ready, k + 1)
                dve.tensor_tensor(x_lo[:, k, :], x_landed[:, k, :], x_hi[:, k, :].bitcast(F32), ALU.subtract)\
                    .then_inc(x_lo_ready, 1)
            dve.wait_ge(mcst_in, 16)
            for n, (dst, b) in enumerate(((qo, 0), (qo, 1), (qo, 2), (kk, 3), (kk, 4), (kk, 5))):
                t = n % NT
                cos = mcst[:, M_COS + 64 * t:M_COS + 64 * t + 64].unsqueeze(1)
                sin = mcst[:, M_SIN + 64 * t:M_SIN + 64 * t + 64].unsqueeze(1)
                src = bank[b][:, :].rearrange("p (h s d) -> p h s d", s=2, d=64)
                out = dst[:, t, :].rearrange("p (h s d) -> p h s d", s=2, d=64)
                pc = tmp[:, 0, :].rearrange("p (h s d) -> p h s d", s=2, d=64)
                ps = tmp[:, 1, :].rearrange("p (h s d) -> p h s d", s=2, d=64)
                tok_done(dve, n // NT, t)
                dve.tensor_tensor(tmp[:, 0, :].rearrange("p (a d) -> p a d", d=64),
                                  bank[b][:, :].rearrange("p (a d) -> p a d", d=64),
                                  cos.to_broadcast([128, 8, 64]), ALU.mult)
                for s in range(2):
                    ins = dve.tensor_tensor(ps[:, :, s, :], src[:, :, 1 - s, :], sin.to_broadcast([128, H, 64]), ALU.mult)
                link(ins)
                dve.tensor_tensor(out[:, :, 0, :], pc[:, :, 0, :], ps[:, :, 0, :], ALU.subtract)
                ins = dve.tensor_tensor(out[:, :, 1, :], pc[:, :, 1, :], ps[:, :, 1, :], ALU.add)
                ins.then_inc(rotated, 1)
                dve.wait_ge(rotated, n + 1)
            for t in range(NT):
                dve.wait_ge(g_sig, t + 1)
                dve.tensor_tensor(gg[:, t, :], gg[:, t, :], bank[3 + t][:, :], ALU.mult).then_inc(g_out, 1)
            dve.wait_ge(bias_in, 96)
            link(dve.tensor_copy(biasp[:, :], bias32))
            for n in (1, 2):
                for m in range(n, 3):
                    r = slice(E * m, E * (m + 1))
                    ins = dve.tensor_tensor(bias32[r, :], bias32[r, :], biasp[r, :], ALU.subtract)
                    link(ins)
                    ins = dve.tensor_copy(biasp[r, :], bias32[r, :])
                    if n < m:
                        link(ins)
            ins.then_inc(bias_split, 1)

            dve.wait_ge(dm_in, 16)
            dve.wait_ge(pool_ready, 2)
            for h, b in enumerate((0, 1, 2, 7)):
                dve.wait_ge(score_mm, h + 1)
                dve.tensor_tensor(scores[:, h, :], bank[b][:, :], dm[:, h * 512:(h + 1) * 512], ALU.mult)\
                    .then_inc(score_out, 1)

            def q_slabs(h):
                if h:
                    dve.wait_ge(qm_used, h)
                flat = qmask.rearrange("p (b c) -> p b c", b=STREAMS)
                for_b = bass.AP(tensor=flat.tensor, offset=flat.offset,
                                ap=[list(flat.ap[0]), [128 + STEP, STREAMS], [1, STEP]])
                dve.tensor_tensor(for_b, qT[:, h, SEQ:].rearrange("p (b i) -> p b i", b=STREAMS),
                                  mcst[:, M_QD + h * STEP:M_QD + (h + 1) * STEP].unsqueeze(1)
                                  .to_broadcast([128, STREAMS, STEP]), ALU.mult).then_inc(qm_ready, 1)

            q_slabs(0)
            dve.wait_ge(chan_in, 48)
            dve.wait_ge(bias_split, 1)
            sview = u[:, :, SEQ + 2:].rearrange("p c (b i) -> p c b i", b=STREAMS)
            dve.memset(u[:, :, 0:2], 0.0)
            dve.tensor_copy(sview[:, :, :, 0:2], cin[:, :, :, :])
            for c in range(CT):
                chan_done(dve, 5, c)
                b = bank[3 + c]
                dve.tensor_tensor(u[:, c, 2:SEQ + 2], b[:, 0:SEQ], z[:, c, 0:SEQ], ALU.mult)
                dve.tensor_tensor(sview[:, c, :, 2:], b[:, SEQ:T].rearrange("p (b i) -> p b i", b=STREAMS),
                                  z[:, c, SEQ:T].rearrange("p (b i) -> p b i", b=STREAMS), ALU.mult)\
                    .then_inc(u_out, 1)
            for h in range(1, H):
                q_slabs(h)
            dve.wait_ge(u_out, CT)
            dve.tensor_copy(ust[:, :, 0:2], u[:, :, SEQ:SEQ + 2]).then_inc(ust_out, 1)
            dve.tensor_copy(ust[:, :, 2:].rearrange("p c (b r) -> p c b r", r=2), sview[:, :, :, STEP:])\
                .then_inc(ust_out, 1)
            dve.wait_ge(qk_t_out, 6)
            for t in range(NT):
                ins = dve.tensor_tensor(kk[:, t, :].rearrange("p (h d) -> p h d", h=H),
                                        kk[:, t, :].rearrange("p (h d) -> p h d", h=H),
                                        mcst[:, M_KD + t * H:M_KD + (t + 1) * H].unsqueeze(2)
                                        .to_broadcast([128, H, HD]), ALU.mult)
            ins.then_inc(kd_ready, 1)
            dve.wait_ge(qm_used, H)
            for t in range(NT):
                for h in range(H):
                    ins = dve.bn_stats(gst[:, t, h, :], bank[t][:, h * 128:(h + 1) * 128])
                link(ins)
                for h in range(H):
                    ins = dve.bn_aggr(gmv[:, t, h, :], gst[:, t, h, :])
                link(ins)
                dve.tensor_scalar_add(gve[:, t, :], gmv[:, t, :, 1], EPS).then_inc(gn_var, 1)
            for t in range(NT):
                dve.wait_ge(gn_rstd, t + 1)
                for h in range(H):
                    ins = dve.tensor_scalar(qo[:, t, h * 128:(h + 1) * 128], bank[t][:, h * 128:(h + 1) * 128],
                                            gmv[:, t, h, 0:1], grs[:, t, h:h + 1], ALU.subtract, ALU.mult)
                ins.then_inc(o_free, 1)
                dve.wait_ge(o_free, t + 1)
                dve.tensor_tensor(qo[:, t, :], qo[:, t, :], gg[:, t, :], ALU.mult).then_inc(o_ready_m, 1)
            for c in range(CT):
                ins = dve.tensor_scalar(z[:, c, :], u[:, c, 0:ZW], chn[:, c, 0:1], chn[:, c, 3:4], ALU.mult, ALU.add)
            for tap in (1, 2):
                link(ins)
                for c in range(CT):
                    ins = dve.scalar_tensor_tensor(z[:, c, :], u[:, c, tap:tap + ZW], chn[:, c, tap:tap + 1],
                                             z[:, c, :], ALU.mult, ALU.add)
            link(ins)
            for c in range(CT):
                chan_done(dve, 6, c)
                b = bank[3 + c]
                dve.scalar_tensor_tensor(qkt[:, H + c, 0:SEQ], b[:, 0:SEQ], chn[:, c, 4:5], z[:, c, 0:SEQ],
                                         ALU.mult, ALU.mult)
                zs = z[:, c, SEQ + 2:SEQ + 2 + (STREAMS - 1) * (STEP + 2) + STEP]
                zs = bass.AP(tensor=zs.tensor, offset=zs.offset,
                             ap=[list(zs.ap[0]), [STEP + 2, STREAMS], [1, STEP]])
                dve.scalar_tensor_tensor(qkt[:, H + c, SEQ:T].rearrange("p (b i) -> p b i", b=STREAMS),
                                         b[:, SEQ:T].rearrange("p (b i) -> p b i", b=STREAMS), chn[:, c, 4:5],
                                         zs, ALU.mult, ALU.mult).then_inc(conv_ready, 1)
            dve.wait_ge(st_in, 16 * H)

            def new_states(h):
                for n in range(2):
                    i = 2 * h + n
                    dve.wait_ge(sts_mm, i + 1)
                    o = slice(n * 512, (n + 1) * 512)
                    dve.scalar_tensor_tensor(st0[:, h, o], st0[:, h, o], float(carry[h]), bank[5 + i % 2][:, :],
                                             ALU.mult, ALU.add).then_inc(sts_out, 1)

            def row_stats(t, count):
                link(dve.bn_aggr(mv[:, t, :], stat[:, t, :, :].rearrange("p a b -> p (a b)")))
                dve.tensor_scalar_add(veps[:, t:t + 1], mv[:, t, 1:2], EPS).then_inc(ln_var, 1)

            mix_banks = ((0, 1), (2, 7), (3, 4))

            def residual(t, n):
                b, o = bank[mix_banks[t][n]], slice(n * 512, (n + 1) * 512)
                if (t, n) != (NT - 1, 1):
                    dve.wait_ge(mix_mm, 2 * t + n + 1)
                else:
                    dve.wait_ge(piece_used, MIX_PIECES)
                link(dve.scalar_tensor_tensor(b[:, :], xy[:, t, o], ALPHA, b[:, :], ALU.mult, ALU.add))
                ins = dve.bn_stats(stat[:, t, n, :], b[:, :])
                if n == 1:
                    link(ins)

            def first_norm(t):
                for n in range(2):
                    b, o = bank[mix_banks[t][n]], slice(n * 512, (n + 1) * 512)
                    ins = dve.scalar_tensor_tensor(b[:, :], b[:, :], mv[:, t, 0:1], lnp[:, 0, o],
                                                   ALU.subtract, ALU.mult)
                    if n == 1:
                        link(ins)
                dve.wait_ge(ln_rstd, t + 1)
                for n in range(2):
                    b, o = bank[mix_banks[t][n]], slice(n * 512, (n + 1) * 512)
                    dve.scalar_tensor_tensor(hid[:, t, o], b[:, :], rstd[:, t:t + 1], lnp[:, 1, o],
                                             ALU.mult, ALU.add).then_inc(h_ready, 1)

            iota = cst[:, C_IOTA:C_IOTA + E]

            def choose(t):
                dve.wait_ge(logit_mm, t + 1)
                dve.tensor_tensor(lg[:, t, :], bank[5][:, t * E:(t + 1) * E], br[:, :], ALU.add).then_inc(lg_out, 1)
                dve.wait_ge(lg_out, t + 1)
                link(dve.max(m8[:, t, :], lg[:, t, :]))
                dve.tensor_scalar(nm1[:, t:t + 1], m8[:, t, 0:1], -1.0, None, ALU.mult).then_inc(nm_ready, 1)
                link(dve.max_index(ix8[:, t, :], m8[:, t, :], lg[:, t, :]))
                for k in range(TOPK):
                    ins = dve.tensor_scalar(picks[:, k, :], iota, ix8[:, t, k:k + 1], None, ALU.is_equal)
                link(ins)
                dve.reduce_sum(msk[:, t, :], picks.rearrange("p k e -> p e k"), AXX).then_inc(mask_ready, 1)
                dve.wait_ge(mask_ready, t + 1)

            def softmax(t):
                dve.wait_ge(exp_ready, t + 1)
                link(dve.tensor_tensor(ex[:, t, :], ex[:, t, :], msk[:, t, :], ALU.mult))
                link(dve.reduce_sum(gs[:, t, 0:1], ex[:, t, :], AXX))
                link(dve.reciprocal(gs[:, t, 1:2], gs[:, t, 0:1]))
                dve.tensor_scalar(gate_all[:, t, 0:E], ex[:, t, :], gs[:, t, 1:2], None, ALU.mult)\
                    .then_inc(gates_out, 1)

            def first_pair_slots(t0, t1):
                dve.wait_ge(rank_mm, t1)
                n = t1 - t0
                link(dve.scalar_tensor_tensor(rank_all[:, t0:t1, 0:E], bank[2][:, t0 * E:t1 * E]
                                              .rearrange("p (t e) -> p t e", t=n), 1.0, msk[:, t0:t1, :],
                                              ALU.add, ALU.mult))
                dve.tensor_tensor(onehot[:, t0:t1, :].rearrange("p t (a s) -> p t a s", a=2),
                                  cst[:, C_IOTA + 1:C_IOTA + 1 + SLOTS].unsqueeze(1).unsqueeze(1)
                                  .to_broadcast([128, n, 2, SLOTS]),
                                  rank_all[:, t0:t1, 0:2].unsqueeze(3).to_broadcast([128, n, 2, SLOTS]),
                                  ALU.is_equal).then_inc(first_slots, 1)

            def rows_of(n):
                dve.tensor_copy(sel[:, :, :], sel_all[:, bass.ds(2 * n, 2)].unsqueeze(2)
                                .to_broadcast([3 * E, 2, SLOTS])).then_inc(sel_ready, 1)

            dve.wait_ge(x_in, 16)
            dve.wait_ge(ln1_in, 32)
            dve.wait_ge(router_in, 32)
            residual(0, 0)
            new_states(0)
            residual(0, 1)
            row_stats(0, 1)
            new_states(1)
            first_norm(0)
            residual(1, 0)
            new_states(2)
            residual(1, 1)
            row_stats(1, 2)
            new_states(3)
            link(dve.memset(ones, 1.0))
            first_norm(1)
            choose(0)
            residual(2, 0)
            choose(1)
            dve.wait_ge(conv_ready, CT)
            first_pair_slots(0, 2)
            residual(2, 1)
            row_stats(2, 3)
            first_norm(2)
            dve.wait_ge(h_t, 2 * NT)
            dve.tensor_copy(xt[:, 4:8, 256:384], bank[1][:, :].rearrange("p (k n) -> p k n", k=4)).then_inc(h_t_out_v, 1)
            link(dve.tensor_copy(sel_all[:, 0:E], cst[0:3 * E, C_SEL:C_SEL + E]))
            rows_of(0)
            choose(2)
            first_pair_slots(2, 3)
            dve.wait_ge(gathered, 1)
            dve.tensor_copy(xg[:, 4:8, :].rearrange("p k n -> p (k n)"), bank[7][:, :]).then_inc(xg_ready_v, 1)
            for t in range(NT):
                softmax(t)
            m3 = msk3.rearrange("p (r e) -> p r e", r=3)
            link(dve.tensor_tensor(msk3[:, 0:E], msk[:, 0, :], msk[:, 1, :], ALU.add))
            link(dve.tensor_tensor(msk3[:, 0:E], msk3[:, 0:E], msk[:, 2, :], ALU.add))
            dve.tensor_copy(m3[:, 1:3, :], m3[:, 0:1, :].to_broadcast([128, 2, E])).then_inc(counts_in, 1)

            more, cnt, cum, end = (ovt[:, n:n + 1] for n in range(4))
            thr_w = ovt[:, 6:6 + MORE]
            oh, off, ws, wq = (ovt[:, 6 + MORE + n * OV:6 + MORE + (n + 1) * OV] for n in range(4))
            rows = slice(0, 3 * E)

            def more_blocks():
                dve.wait_ge(cnt_mm, 1)
                link(dve.tensor_copy(cnt, bank[4][rows, 0:1]))
                link(dve.tensor_scalar(thr_w, cst[rows, C_THR:C_THR + MORE], cnt, None, ALU.is_lt))
                dve.reduce_sum(more, thr_w, AXX).then_inc(more_ready, 1)

            def overflow_blocks():
                dve.wait_ge(cum_mm, 1)
                dve.tensor_copy(half[:, 0:1], bank[4][0:1, 2:3])
                link(dve.tensor_copy(cum, bank[4][rows, 1:2]))
                link(dve.tensor_tensor(end, cum, more, ALU.add))
                orow = cst[rows, C_OV:C_OV + OV]
                dve.tensor_scalar(ws, orow, cum, None, ALU.is_ge)
                link(dve.tensor_scalar(wq, orow, end, None, ALU.is_lt))
                link(dve.tensor_tensor(oh, ws, wq, ALU.mult))
                link(dve.tensor_scalar(ws, orow, cum, -float(SLOTS), ALU.subtract, ALU.mult))
                link(dve.scalar_tensor_tensor(off, ws, -float(SLOTS), oh, ALU.add, ALU.mult))
                dve.tensor_copy(sel_all[:, E:E + OV], oh).then_inc(ov_ready, 1)
                link(dve.tensor_scalar(half[:, 2:], cst[0:1, C_HALF:C_W], half[:, 0:1], None, ALU.is_lt))
                link(dve.reduce_sum(half[:, 1:2], half[:, 2:], AXX))
                dve.tensor_scalar(ntab[:, 0:1], half[:, 1:2], float(E // 4 - 1), None, ALU.add)

            def tables():
                dve.wait_ge(ov_mm, 1)
                dve.tensor_copy(etab[:, :], bank[7][0:1, NT * OV:(NT + 1) * OV])
                dve.tensor_copy(rank_all[:, :, E:E + OV], bank[6][:, 0:NT * OV].rearrange("p (t o) -> p t o", t=NT))
                dve.tensor_copy(gate_all[:, :, E:E + OV], bank[7][:, 0:NT * OV].rearrange("p (t o) -> p t o", t=NT))\
                    .then_inc(tab_ready, 1)
                dve.wait_ge(tab_ready, 1)

            def gated_slots(n):
                og4 = onehot_g[:, :, :].rearrange("p t (a s) -> p t a s", a=2)
                gate = gate_all[:, :, bass.ds(2 * n, 2)].unsqueeze(3).to_broadcast([128, NT, 2, SLOTS])
                dve.tensor_tensor(og4, onehot[:, :, :].rearrange("p t (a s) -> p t a s", a=2), gate, ALU.mult)\
                    .then_inc(onehot_ready, 1)

            def slots_of(n):
                iota4 = cst[:, C_IOTA + 1:C_IOTA + 1 + SLOTS].unsqueeze(1).unsqueeze(1).to_broadcast([128, NT, 2, SLOTS])
                rank = rank_all[:, :, bass.ds(2 * n, 2)].unsqueeze(3).to_broadcast([128, NT, 2, SLOTS])
                dve.tensor_tensor(onehot[:, :, :].rearrange("p t (a s) -> p t a s", a=2), iota4, rank, ALU.is_equal)\
                    .then_inc(onehot_ready, 1)
                dve.wait_ge(onehot_ready, 2 * n)
                gated_slots(n)

            def pair(p, first=False, last=False):
                if first:
                    dve.wait_ge(gates_out, NT)
                    dve.wait_ge(first_slots, 2)
                    gated_slots(0)
                for a in range(2):
                    n = 2 * p + a + 1
                    dve.wait_ge(piece_used, PAIR_PIECES * p + MIX_PIECES + GU_PIECES * (a + 1))
                    dve.tensor_scalar(gate_c[:, :], bank[2 * a][:, :], LIMIT, None, ALU.min).then_inc(gate_ready, 1)
                    dve.tensor_scalar(up_c[:, :], bank[2 * a + 1][:, :], LIMIT, -LIMIT, ALU.min, ALU.max)\
                        .then_inc(up_ready, 1)
                    dve.wait_ge(gate_ready, n)
                    dve.wait_ge(up_ready, n)
                    dve.scalar_tensor_tensor(up_c[:, :], up_c[:, :], 1.0, gate_c[:, :], ALU.add, ALU.mult)\
                        .then_inc(prod_ready, 1)
                    dve.wait_ge(prod_ready, n)
                    dve.wait_ge(sig_ready, n)
                    dve.tensor_tensor(act_h[:, a, :], up_c[:, :], sig[:, :], ALU.mult).then_inc(act_ready, 1)
                    if a == 0:
                        if first:
                            more_blocks()
                            overflow_blocks()
                        if not last:
                            dve.wait_ge(gt_mm, p + 1)
                            slots_of(p + 1)
                if first:
                    tables()
                if last:
                    dve.wait_ge(piece_used, PAIR_PIECES * p + MIX_PIECES + PAIR_PIECES)
                    dve.tensor_copy(oo[64:128, 512:1024], bank[4][64:128, :]).then_inc(out_ready_v, 1)
                    return
                for i in range(2 * NT):
                    t, hf = i // 2, i % 2
                    o = slice(hf * 512, (hf + 1) * 512)
                    dve.wait_ge(comb_mm, 6 * p + i + 1)
                    if i == 0:
                        rows_of(p + 1)
                    if first:
                        dve.scalar_tensor_tensor(xy[:, t, o], hid[:, t, o], ALPHA, bank[2 + i % 3][:, :],
                                                 ALU.mult, ALU.add).then_inc(y_added, 1)
                    else:
                        dve.tensor_tensor(xy[:, t, o], xy[:, t, o], bank[2 + i % 3][:, :], ALU.add)\
                            .then_inc(y_added, 1)

            pair(0, first=True)
            last_pair = 2 * dve.value_load(ntab[0:1, 0:1], min_val=E // 4 - 1, max_val=NB // 4 - 1) + 1
            with dve.Fori(1, last_pair) as p:
                pair(p)
            pair(last_pair, last=True)
            def sums_stats(t, between=None):
                for n in range(2):
                    dve.wait_ge(comb_mm, 6 * last_pair + 2 * t + n + 1)
                    ins = dve.bn_stats(stat[:, t, n, :], bank[last_banks[2 * t + n]][:, :])
                    if n == 0 and between:
                        between()
                link(ins)
                row_stats(t, NT + t + 1)

            def shift_0():
                dve.wait_ge(ln_rstd, NT + 1)
                dve.scalar_tensor_tensor(shift[:, 0:1], mv[:, 0, 0:1], -1.0, rstd[:, 0:1], ALU.mult, ALU.mult)\
                    .then_inc(y_shift, 1)

            def centre(t):
                for n in range(2):
                    b = bank[last_banks[2 * t + n]]
                    dve.scalar_tensor_tensor(b[:, :], b[:, :], mv[:, t, 0:1], lnp[:, 0, n * 512:(n + 1) * 512],
                                             ALU.subtract, ALU.mult).then_inc(y_centred, 1)

            def finish(t):
                dve.wait_ge(ln_rstd, NT + t + 1)
                for n in range(2):
                    o = slice(n * 512, (n + 1) * 512)
                    dve.wait_ge(y_centred, 2 * (t - 1) + n + 1)
                    dve.scalar_tensor_tensor(xy[:, t, o], bank[last_banks[2 * t + n]][:, :], rstd[:, t:t + 1],
                                             lnp[:, 1, o], ALU.mult, ALU.add).then_inc(y_done, 1)

            sums_stats(0)
            sums_stats(1, between=shift_0)
            dve.wait_ge(ln2_in, 32)
            centre(1)
            sums_stats(2)
            finish(1)
            centre(2)
            finish(2)


def kernel(x_prompt, x_sample, state_retention, state_conv, w_in, beta_ret, beta_conv, conv_w, conv_b, w_out,
           ln1_g, ln1_b, w_router, b_router, w_gu, b_gu, w_down, b_down, ln2_g, ln2_b):
    import concourse.bacc as bacc
    from concourse.bass_utils import run_bass_kernel_spmd

    a = np.ascontiguousarray
    x = np.concatenate([np.asarray(x_prompt).reshape(SEQ, D), np.asarray(x_sample).reshape(STREAMS * STEP, D)])
    by_channel = [np.asarray(v).reshape(CT, 128).T for v in
                  (*np.asarray(conv_w)[0], np.asarray(conv_b)[0], np.asarray(beta_conv)[0])]
    c, m, dmask, _ = constants()
    arrays = {
        "x_tok": a(x), "x_t": a(x.T), "s_ret": a(np.asarray(state_retention)[0]),
        "conv_in": a(np.asarray(state_conv)[0].reshape(STREAMS, 2, CT, 128).transpose(3, 2, 0, 1)),
        "w_in": a(np.asarray(w_in)[0]), "w_out": a(np.asarray(w_out)[0]),
        "chan": a(np.stack(by_channel, axis=-1)), "beta_ret": a(np.asarray(beta_ret).reshape(H, 128).T),
        "ln1": a(np.concatenate([np.asarray(ln1_g), np.asarray(ln1_b)])),
        "ln2": a(np.concatenate([np.asarray(ln2_g), np.asarray(ln2_b)])),
        "w_router": a(np.asarray(w_router)[0]), "b_router": a(np.asarray(b_router)[0]),
        "w_gu": a(np.asarray(w_gu)[0]), "b_gu": a(np.asarray(b_gu)[0]),
        "w_down": a(np.asarray(w_down)[0]), "b_down": a(np.asarray(b_down)[0]),
        "consts": c, "mconsts": m, "dmask": dmask,
    }
    outs = {"y": (T, D), "retp": (H, HD, HD), "rets": (STREAMS, H, HD, HD), "convs": (128, CT, 2 + 2 * STREAMS)}
    nc = bacc.Bacc("TRN2", target_bir_lowering=False, num_devices=1, dynamic_dma_scratch_size=1024)
    args = [nc.dram_tensor(n, v.shape, F32, kind="ExternalInput").ap() for n, v in arrays.items()]
    args += [nc.dram_tensor(n, s, F32, kind="ExternalOutput").ap() for n, s in outs.items()]
    build(nc, *args)
    r = run_bass_kernel_spmd(nc, [arrays], core_ids=[0]).results[0]
    y, conv = r["y"], r["convs"].transpose(2, 1, 0).reshape(2 + 2 * STREAMS, DC)
    return (y[:SEQ].reshape(1, SEQ, D), y[SEQ:].reshape(STREAMS, STEP, D),
            r["retp"].reshape(1, 1, H, HD, HD), a(conv[:2]).reshape(1, 1, 2, DC),
            r["rets"].reshape(1, STREAMS, H, HD, HD), a(conv[2:]).reshape(1, STREAMS, 2, DC))
```
